# Optimizing a Trainium2 kernel written in Bass

```python
import math
import jax, jax.numpy as jnp
from jax import lax
import numpy as np

D_MODEL = 1024
BATCH = 1
SEQ = 1024
DEPTH = 2

CHUNK = 64
N_MEM = 256
EXPAND = 2
D_MIX = EXPAND * D_MODEL
GROUP_W = D_MIX // 4

RET_HEADS = 4
RET_DV = GROUP_W // RET_HEADS
RET_DK = RET_DV // 2
ROPE_BASE = 10000.0
S5_CH = 16
S5_GROUPS = GROUP_W // S5_CH
S5_STATE = 64
S5_DT_MIN = 1e-3
S5_DT_MAX = 1e-1
ML_HEADS = 4
ML_DH = GROUP_W // ML_HEADS
ML_CONV = 4
XA_HEADS = 4
XA_DH = GROUP_W // XA_HEADS

LN_EPS = 1e-5
GN_EPS = 1e-6
ALPHA = (2 * DEPTH) ** 0.25
BETA = (8 * DEPTH) ** -0.25

IN_WIDTHS = (RET_HEADS * RET_DK, RET_HEADS * RET_DK, GROUP_W, GROUP_W,
             GROUP_W, GROUP_W,
             GROUP_W, GROUP_W, GROUP_W, GROUP_W, ML_HEADS, ML_HEADS,
             GROUP_W, GROUP_W)
D_IN = 2 * RET_HEADS * RET_DK + 10 * GROUP_W + 2 * ML_HEADS

kernel_name = "hybrid_ret_s5_mlstm_memxattn_deepnorm"

def layer_norm(x, g, b):
    xf = x.astype(jnp.float32)
    mu = jnp.mean(xf, -1, keepdims=True)
    var = jnp.mean(jnp.square(xf - mu), -1, keepdims=True)
    return ((xf - mu) * lax.rsqrt(var + LN_EPS) * g.astype(jnp.float32) + b.astype(jnp.float32)).astype(x.dtype)

def head_norm(h):
    mu = jnp.mean(h, -1, keepdims=True)
    var = jnp.mean(jnp.square(h - mu), -1, keepdims=True)
    return (h - mu) * lax.rsqrt(var + GN_EPS)

def to_chunks(t):
    b, l = t.shape[:2]
    t = t.reshape(b, l // CHUNK, CHUNK, *t.shape[2:])
    return jnp.swapaxes(jnp.moveaxis(t, 1, 0), 2, 3)

def from_chunks(t):
    t = jnp.moveaxis(jnp.swapaxes(t, 2, 3), 0, 1)
    b, nc, c = t.shape[:3]
    return t.reshape(b, nc * c, *t.shape[3:])

def rotary(t, positions):
    half = t.shape[-1] // 2
    inv = ROPE_BASE ** (-jnp.arange(half, dtype=jnp.float32) / half)
    ang = positions.astype(jnp.float32)[..., None] * inv
    cos = jnp.cos(ang)[:, :, None, :]
    sin = jnp.sin(ang)[:, :, None, :]
    t1, t2 = t[..., :half], t[..., half:]
    return jnp.concatenate([t1 * cos - t2 * sin, t1 * sin + t2 * cos], -1)

def causal_conv(x, w):
    k, c = w.shape
    return lax.conv_general_dilated(x, w[:, None, :].astype(x.dtype), window_strides=(1,),
                                    padding=[(k - 1, 0)], dimension_numbers=('NWC', 'WIO', 'NWC'),
                                    feature_group_count=c)

def retention(q, k, v, positions):
    bsz = q.shape[0]
    q = rotary(q, positions)
    k = rotary(k, positions) * RET_DK ** -0.5
    log_g = jnp.log1p(-jnp.exp2(-5.0 - jnp.arange(RET_HEADS, dtype=jnp.float32)))
    r = jnp.arange(CHUNK, dtype=jnp.float32)
    intra = jnp.exp(jnp.abs(r[:, None] - r[None, :]) * log_g[:, None, None])
    q_dec = jnp.exp((r + 1.0) * log_g[:, None])
    k_dec = jnp.exp((CHUNK - 1.0 - r) * log_g[:, None])
    c_dec = jnp.exp(CHUNK * log_g)

    def step(S, xs):
        qc, kc, vc = xs
        att = jnp.einsum('bhrd,bhsd->bhrs', qc, kc) * intra
        o = (jnp.einsum('bhrs,bhse->bhre', att, vc)
             + q_dec[:, :, None] * jnp.einsum('bhrd,bhde->bhre', qc, S))
        S = c_dec[:, None, None] * S + jnp.einsum('bhsd,bhse->bhde', kc * k_dec[:, :, None], vc)
        return S, o

    S0 = jnp.zeros((bsz, RET_HEADS, RET_DK, RET_DV), jnp.float32)
    _, o = lax.scan(step, S0, (to_chunks(q), to_chunks(k), to_chunks(v)))
    return head_norm(from_chunks(o))

def s5(u, a_re, a_im, log_dt, b_re, b_im, c_re, c_im, d, w_glu):
    f32 = jnp.float32
    a_re, a_im, b_re, b_im = (t.astype(f32) for t in (a_re, a_im, b_re, b_im))
    bsz, l, _ = u.shape
    ug = u.reshape(bsz, l, S5_GROUPS, S5_CH)
    dt = jnp.exp(log_dt.astype(f32))[:, None]
    mag = jnp.exp(a_re * dt)
    ab_re = mag * jnp.cos(a_im * dt)
    ab_im = mag * jnp.sin(a_im * dt)
    den = a_re * a_re + a_im * a_im
    p = ab_re - 1.0
    f_re = (p * a_re + ab_im * a_im) / den
    f_im = (ab_im * a_re - p * a_im) / den
    bb_re = f_re[..., None] * b_re - f_im[..., None] * b_im
    bb_im = f_re[..., None] * b_im + f_im[..., None] * b_re
    bu_re = jnp.einsum('blgc,gpc->blgp', ug, bb_re)
    bu_im = jnp.einsum('blgc,gpc->blgp', ug, bb_im)

    def combine(e1, e2):
        a1r, a1i, b1r, b1i = e1
        a2r, a2i, b2r, b2i = e2
        return (a2r * a1r - a2i * a1i, a2r * a1i + a2i * a1r,
                a2r * b1r - a2i * b1i + b2r, a2r * b1i + a2i * b1r + b2i)

    _, _, xr, xi = lax.associative_scan(
        combine, (jnp.broadcast_to(ab_re, bu_re.shape), jnp.broadcast_to(ab_im, bu_re.shape), bu_re, bu_im),
        axis=1)
    y = (jnp.einsum('blgp,gcp->blgc', xr, c_re.astype(f32))
         - jnp.einsum('blgp,gcp->blgc', xi, c_im.astype(f32)))
    y = y.reshape(bsz, l, GROUP_W) + d.astype(f32) * u
    y = jax.nn.gelu(y)
    return y * jax.nn.sigmoid(y @ w_glu.astype(f32))

def mlstm(q, k, v, ig, lf):
    bsz, _, nh, dh = q.shape
    k = k * dh ** -0.5
    causal = jnp.tril(jnp.ones((CHUNK, CHUNK), bool))

    def step(carry, xs):
        C, n, m = carry
        qc, kc, vc, ic, fc = xs
        b = jnp.cumsum(fc, -1)
        dmat = jnp.where(causal, b[..., :, None] - b[..., None, :] + ic[..., None, :], -jnp.inf)
        inter = b + m[..., None]
        m_r = jnp.maximum(jnp.max(dmat, -1), inter)
        w = jnp.exp(dmat - m_r[..., None])
        w_inter = jnp.exp(inter - m_r)
        s = jnp.einsum('bhrd,bhsd->bhrs', qc, kc) * w
        num = (jnp.einsum('bhrs,bhsd->bhrd', s, vc)
               + w_inter[..., None] * jnp.einsum('bhed,bhrd->bhre', C, qc))
        den = jnp.sum(s, -1) + w_inter * jnp.einsum('bhd,bhrd->bhr', n, qc)
        h = num / jnp.maximum(jnp.abs(den), jnp.exp(-m_r))[..., None]
        b_last = b[..., -1]
        g = b_last[..., None] - b + ic
        m_new = jnp.maximum(b_last + m, jnp.max(g, -1))
        wk = jnp.exp(g - m_new[..., None])
        dec = jnp.exp(b_last + m - m_new)
        C = dec[..., None, None] * C + jnp.einsum('bhse,bhsd->bhed', vc * wk[..., None], kc)
        n = dec[..., None] * n + jnp.einsum('bhs,bhsd->bhd', wk, kc)
        return (C, n, m_new), h

    init = (jnp.zeros((bsz, nh, dh, dh), jnp.float32), jnp.zeros((bsz, nh, dh), jnp.float32),
            jnp.zeros((bsz, nh), jnp.float32))
    _, h = lax.scan(step, init, (to_chunks(q), to_chunks(k), to_chunks(v), to_chunks(ig), to_chunks(lf)))
    return from_chunks(h)

def memory_attention(q, mk, mv):
    s = jnp.einsum('blhd,bmhd->bhlm', q, mk).astype(jnp.float32) * XA_DH ** -0.5
    p = jax.nn.softmax(s, -1)
    return jnp.einsum('bhlm,bmhd->blhd', p, mv.astype(jnp.float32))

def hybrid_layer(x, mem, positions, w_in, s5_a_re, s5_a_im, s5_log_dt, s5_b_re, s5_b_im, s5_c_re,
                 s5_c_im, s5_d, s5_w_glu, ml_conv_w, ml_wq, ml_wk, ml_b_ig, ml_b_fg, ml_gn, xa_w_kv,
                 w_out, ln_g, ln_b):
    f32 = jnp.float32
    bsz, l, _ = x.shape
    proj = x @ w_in
    (r_q, r_k, r_v, r_z, s_u, s_z, m_x, m_v, m_o, m_z, m_i, m_f, a_q, a_z) = jnp.split(
        proj, list(np.cumsum(IN_WIDTHS)[:-1]), axis=-1)

    def heads(t, nh):
        return t.reshape(t.shape[0], t.shape[1], nh, -1).astype(f32)

    ret = retention(heads(r_q, RET_HEADS), heads(r_k, RET_HEADS), heads(r_v, RET_HEADS), positions)
    ret = ret.reshape(bsz, l, GROUP_W) * jax.nn.silu(r_z.astype(f32))

    s5o = s5(s_u.astype(f32), s5_a_re, s5_a_im, s5_log_dt, s5_b_re, s5_b_im, s5_c_re, s5_c_im, s5_d, s5_w_glu)
    s5o = s5o * jax.nn.silu(s_z.astype(f32))

    xc = heads(jax.nn.silu(causal_conv(m_x, ml_conv_w)), ML_HEADS)
    q = jnp.einsum('blhd,hde->blhe', xc, ml_wq.astype(f32))
    k = jnp.einsum('blhd,hde->blhe', xc, ml_wk.astype(f32))
    ig = m_i.astype(f32) + ml_b_ig.astype(f32)
    lf = jax.nn.log_sigmoid(m_f.astype(f32) + ml_b_fg.astype(f32))
    h = mlstm(q, k, heads(m_v, ML_HEADS), ig, lf) * jax.nn.sigmoid(heads(m_o, ML_HEADS))
    h = head_norm(h) * ml_gn.astype(f32).reshape(ML_HEADS, ML_DH)
    ml = h.reshape(bsz, l, GROUP_W) * jax.nn.silu(m_z.astype(f32))

    mk, mv = jnp.split(mem @ xa_w_kv, 2, axis=-1)
    xa = memory_attention(heads(a_q, XA_HEADS), heads(mk, XA_HEADS), heads(mv, XA_HEADS))
    xa = xa.reshape(bsz, l, GROUP_W) * jax.nn.silu(a_z.astype(f32))

    y = jnp.concatenate([ret, s5o, ml, xa], -1).astype(x.dtype) @ w_out
    return layer_norm(ALPHA * x + y, ln_g, ln_b)

def setup_inputs(seed: int = 0) -> dict:
    key = jax.random.key(seed)
    ks = jax.random.split(key, 24)
    nrm = jax.random.normal
    f32 = jnp.float32
    x = nrm(ks[0], (BATCH, SEQ, D_MODEL), f32)
    mem = nrm(ks[1], (BATCH, N_MEM, D_MODEL), f32)
    offs = jax.random.randint(ks[2], (BATCH, 1), 0, 4096, dtype=jnp.int32)
    positions = (offs + jnp.arange(SEQ, dtype=jnp.int32)[None, :]).astype(jnp.int32)
    w_in = nrm(ks[3], (DEPTH, D_MODEL, D_IN), f32) * D_MODEL ** -0.5
    s5_a_re = -0.5 + 0.01 * nrm(ks[4], (DEPTH, S5_GROUPS, S5_STATE), f32)
    s5_a_im = (math.pi * jnp.arange(S5_STATE, dtype=f32))[None, None, :] + 0.01 * nrm(ks[5], (DEPTH, S5_GROUPS, S5_STATE), f32)
    s5_log_dt = jax.random.uniform(ks[6], (DEPTH, S5_GROUPS), f32, math.log(S5_DT_MIN), math.log(S5_DT_MAX))
    s5_b_re = nrm(ks[7], (DEPTH, S5_GROUPS, S5_STATE, S5_CH), f32) * (2 * S5_CH) ** -0.5
    s5_b_im = nrm(ks[8], (DEPTH, S5_GROUPS, S5_STATE, S5_CH), f32) * (2 * S5_CH) ** -0.5
    s5_c_re = nrm(ks[9], (DEPTH, S5_GROUPS, S5_CH, S5_STATE), f32) * (2 * S5_STATE) ** -0.5
    s5_c_im = nrm(ks[10], (DEPTH, S5_GROUPS, S5_CH, S5_STATE), f32) * (2 * S5_STATE) ** -0.5
    s5_d = nrm(ks[11], (DEPTH, GROUP_W), f32)
    s5_w_glu = nrm(ks[12], (DEPTH, GROUP_W, GROUP_W), f32) * GROUP_W ** -0.5
    ml_conv_w = nrm(ks[13], (DEPTH, ML_CONV, GROUP_W), f32) * ML_CONV ** -0.5
    ml_wq = nrm(ks[14], (DEPTH, ML_HEADS, ML_DH, ML_DH), f32) * ML_DH ** -0.5
    ml_wk = nrm(ks[15], (DEPTH, ML_HEADS, ML_DH, ML_DH), f32) * ML_DH ** -0.5
    ml_b_ig = 0.1 * nrm(ks[16], (DEPTH, ML_HEADS), f32)
    ml_b_fg = jnp.linspace(3.0, 6.0, ML_HEADS, dtype=f32)[None, :] + 0.1 * nrm(ks[17], (DEPTH, ML_HEADS), f32)
    ml_gn = 1.0 + 0.02 * nrm(ks[18], (DEPTH, GROUP_W), f32)
    xa_w_kv = nrm(ks[19], (DEPTH, D_MODEL, 2 * GROUP_W), f32) * D_MODEL ** -0.5
    w_out = nrm(ks[20], (DEPTH, D_MIX, D_MODEL), f32) * (D_MIX ** -0.5 * BETA)
    ln_g = 1.0 + 0.02 * nrm(ks[21], (DEPTH, D_MODEL), f32)
    ln_b = 0.02 * nrm(ks[22], (DEPTH, D_MODEL), f32)
    return {"x": x, "mem": mem, "positions": positions, "w_in": w_in,
            "s5_a_re": s5_a_re, "s5_a_im": s5_a_im, "s5_log_dt": s5_log_dt,
            "s5_b_re": s5_b_re, "s5_b_im": s5_b_im, "s5_c_re": s5_c_re, "s5_c_im": s5_c_im,
            "s5_d": s5_d, "s5_w_glu": s5_w_glu, "ml_conv_w": ml_conv_w, "ml_wq": ml_wq,
            "ml_wk": ml_wk, "ml_b_ig": ml_b_ig, "ml_b_fg": ml_b_fg, "ml_gn": ml_gn,
            "xa_w_kv": xa_w_kv, "w_out": w_out, "ln_g": ln_g, "ln_b": ln_b}

def reference(x, mem, positions, w_in, s5_a_re, s5_a_im, s5_log_dt, s5_b_re, s5_b_im, s5_c_re,
              s5_c_im, s5_d, s5_w_glu, ml_conv_w, ml_wq, ml_wk, ml_b_ig, ml_b_fg, ml_gn, xa_w_kv,
              w_out, ln_g, ln_b):
    for l in range(DEPTH):
        x = hybrid_layer(x, mem, positions, w_in[l], s5_a_re[l], s5_a_im[l], s5_log_dt[l],
                         s5_b_re[l], s5_b_im[l], s5_c_re[l], s5_c_im[l], s5_d[l], s5_w_glu[l],
                         ml_conv_w[l], ml_wq[l], ml_wk[l], ml_b_ig[l], ml_b_fg[l], ml_gn[l],
                         xa_w_kv[l], w_out[l], ln_g[l], ln_b[l])
    return x


_drawn_inputs = setup_inputs


def setup_inputs(seed=0):
    import zlib

    import numpy as np

    out = dict(_drawn_inputs(seed))
    spreads = {}
    factors = {'mem': 3.781,
     's5_a_re': 64.0,
     's5_a_im': 64.0,
     's5_log_dt': 64.0,
     's5_b_re': 64.0,
     's5_b_im': 64.0,
     's5_c_re': 64.0,
     's5_c_im': 64.0,
     's5_w_glu': 3.693,
     'ml_b_ig': 64.0,
     'ml_gn': 8.0,
     'xa_w_kv': 3.57}
    for name, (base, spread) in spreads.items():
        noise = np.random.default_rng([zlib.crc32(name.encode()), seed]).standard_normal(out[name].shape)
        drawn = base * np.exp(spread * noise) if base else spread * noise
        out[name] = __import__('jax').numpy.asarray(drawn.astype(out[name].dtype))
    for name, factor in factors.items():
        out[name] = (out[name] * factor).astype(out[name].dtype)
    return out
```

```python
import math
import numpy as np
import concourse.bass as bass
from concourse import mybir
from contextlib import ExitStack

F32 = mybir.dt.float32
F32R = mybir.dt.float32r
I32 = mybir.dt.int32
ALU = mybir.AluOpType
ACT = mybir.ActivationFunctionType
AX = mybir.AxisListType

DEPTH, D, T, NMEM, GW = 2, 1024, 1024, 256, 512
HEADS, DK, DV = 4, 64, 128
KT = D // 128
CH = 128
NC = T // CH
REF_CHUNK = 64
ALPHA = (2 * DEPTH) ** 0.25
GN_EPS, LN_EPS = 1e-6, 1e-5
G5, C5, P5 = 32, 16, 64
BS = 8
NB = T // BS
GB = 2
NBATCH = G5 // GB
NBT = NB + 1
TG, TH, TH2, TCOS, TSIN, TRR = 0, GB * 192, GB * 320, GB * 448, GB * 448 + GB * NBT, GB * 448 + 2 * GB * NBT
TTOP = GB * 448 + 3 * GB * NBT
TCOLS = TTOP + GB * 128
(U_MK, U_MV, U_QK, U_RV, U_AQ, U_RZ, U_AZ, U_MX, U_LV, U_LO, U_LZ, U_SU, U_SZ, U_GL) = range(0, 28, 2)
CUNITS = {u + i for u in (U_QK, U_AQ, U_AZ, U_MX, U_SU, U_SZ) for i in range(2)}
NGATE = 10
NUNIT = 28
NOUT = 16
HALVES = 2 * 26 + 2 + 2 * NOUT
NSTORED = NUNIT + NOUT // 2
TWO_PI = 2 * math.pi
C1 = 6.28125
C2 = float(np.float32(round((TWO_PI - C1) * 2 ** 20) / 2 ** 20))
C3 = TWO_PI - C1 - C2
MAGIC = 1.5 * 2 ** 23
PI_LO = 3.1415925
STEPS_V = 296
STEPS_A = 7
K_ID, K_MASK, K_KDEC, K_CAUS, K_ONE, K_MISC = 0, 128, 640, 896, 1024, 1536
(M_SGN, M_NSGN, M_HPI, M_GNE, M_LNE, M_INV, M_ONE, M_QD, M_CD) = (0, 1, 2, 3, 4, 5, 6, 8, 12)
K_COLS = 1536 + 16
J_ROW, J_MASK, J_I16, J_RES = 0, NBT, 2 * NBT, 2 * NBT + 16
J_COLS = J_RES + T


def constants():
    c = np.zeros((128, K_COLS), np.float64)
    c[:, K_ID:K_ID + 128] = np.eye(128)
    g = 1.0 - 2.0 ** (-5.0 - np.arange(HEADS))
    s, t = np.arange(CH)[:, None], np.arange(CH)[None, :]
    same = (s // REF_CHUNK) == (t // REF_CHUNK)
    for h in range(HEADS):
        m = np.where(s <= t, g[h] ** (t - s), np.where(same, g[h] ** (s - t), 0.0))
        m0 = K_MASK + 256 * (h % 2) + 128 * (h // 2)
        c[:, m0:m0 + 128] = m / g[h] ** (t + 1.0) * DK ** -0.5
        c[:, K_KDEC + h * DK:K_KDEC + (h + 1) * DK] = g[h] ** (CH - 1.0 - s) * DK ** -0.5
        c[:, K_MISC + M_QD + h] = (g[h] ** (np.arange(CH) + 1.0))
        c[h, K_ONE + h * 128:K_ONE + (h + 1) * 128] = 1.0
    for p in range(2):
        c[:64, K_MISC + M_CD + p] = g[2 * p] ** CH
        c[64:, K_MISC + M_CD + p] = g[2 * p + 1] ** CH
    c[:, K_CAUS:K_CAUS + 128] = (s <= t)
    c[:64, K_MISC + M_SGN], c[64:, K_MISC + M_SGN] = 1.0, -1.0
    c[:, K_MISC + M_NSGN] = -c[:, K_MISC + M_SGN]
    c[:, K_MISC + M_HPI] = math.pi / 2
    c[:, K_MISC + M_GNE], c[:, K_MISC + M_LNE] = GN_EPS, LN_EPS
    c[:, K_MISC + M_INV] = 10000.0 ** (-(np.arange(128) % 32) / 32.0)
    c[:, K_MISC + M_ONE] = 1.0
    j = np.zeros((128, J_COLS), np.float64)
    j[:, J_ROW:J_ROW + NBT] = np.arange(NBT)
    j[:, J_MASK:J_MASK + NBT] = 1.0
    j[:, J_MASK] = 0.0
    j[:16, J_I16:J_I16 + 16] = np.eye(16)
    j[:, J_RES:] = (np.arange(T) % CH != 0)
    return c.astype(np.float32), j.astype(np.float32)


class Steps:

    def __init__(self, eng, sem, per_layer):
        self.eng, self.sem, self.per, self.n, self.base = eng, sem, per_layer, 0, 0

    def begin(self, layer):
        self.layer, self.n = layer, 0

    def inc(self, ins):
        ins.then_inc(self.sem, 1)
        self.n += 1

    def link(self, ins):
        self.inc(ins)
        self.eng.wait_ge(self.sem, self.layer * self.per + self.n + self.base)

    def join(self):
        self.eng.wait_ge(self.sem, self.layer * self.per + self.n + self.base)


def bcast(ap, n, dim):
    dim = max(dim, 1)
    dims = [list(x) for x in ap.ap]
    return bass.AP(ap.tensor, ap.offset, dims[:dim] + [[0, n]] + dims[dim:])


def tview(x, width, g, u):
    return x.rearrange("p (c n) -> p c n", n=width)[:, 4 * g:4 * g + 4, 256 * u:256 * u + 256]


def build(nc, dram, steps_v=STEPS_V, steps_a=STEPS_A):
    ctx = ExitStack()
    with ctx:
        arena = ctx.enter_context(nc.sbuf_tensor("arena", [128, 53200], F32))
        base = nc.sbuf_base - 53200 * 4 if nc.sbuf_base >= 53200 * 4 else 0

        def at(name, cols, off, dt=F32, rows=128):
            return nc.alloc_sbuf_tensor_at(name, [rows, cols], dt, offset=base + off * 4)[:, :]

        cursor = [0]

        def take(n):
            cursor[0] += (n + 7) // 8 * 8
            assert cursor[0] <= 53200, cursor[0]
            return cursor[0] - (n + 7) // 8 * 8

        o_x = take(2 * KT * T)
        xh, xl = at("xh", KT * T, o_x, F32R), at("xl", KT * T, o_x + KT * T, F32R)
        o_raw = take(2048)
        wraw = [at(f"wraw{i}", 1024, o_raw + 1024 * i) for i in range(2)]
        o_w = take(8192)
        whi = [at(f"whi{i}", 2048, o_w + 4096 * i, F32R) for i in range(2)]
        wlo = [at(f"wlo{i}", 2048, o_w + 4096 * i + 2048, F32R) for i in range(2)]
        R = [take(4096) for _ in range(4)]
        o_v = take(HEADS * NC * 129)
        o_g = take(2048)
        gate = [at(f"gate{i}", 1024, o_g + 1024 * i) for i in range(2)]
        o_ys = take(1024)
        ystage = [at(f"ystage{i}", 512, o_ys + 512 * i) for i in range(2)]
        cst = at("cst", K_COLS, take(K_COLS))
        gn = at("gn", GW, take(GW))
        stats = at("stats", 32 * 6, take(32 * 6))
        mv = at("mv", 64, take(64))
        sd = at("sd", 64, take(64))
        cols = at("cols", NC * 16, take(NC * 16))
        dec = at("dec", 32, take(32))
        small = at("small", 128, take(128))
        qk = at("qk", 4096, R[0])
        rot = at("rot", 4096, R[2])
        hr = at("hr", 4096, R[2])
        rope = at("rope", 2048, o_g)
        rv = at("rv", 4096, o_v)
        qk2 = at("qk2", 4096, R[0])
        mkT, mvT = at("mkT", 1024, R[1]), at("mvT", 1024, R[1] + 1024)
        pm, pt = at("pm", 1024, R[1] + 2048), at("pt", 1024, R[1] + 3072)
        memraw = at("memraw", 2048, R[2])
        memh, meml = at("memh", 2048, R[3], F32R), at("meml", 2048, R[3] + 2048, F32R)
        aq, xo = at("aq", 4096, R[3]), at("xo", 4096, R[0])
        att = [at(f"att{i}", 512, R[1] + 2048 + 512 * i) for i in range(2)]
        kn = [at(f"kn{i}", 256, R[1] + 3072 + 256 * i) for i in range(2)]
        sret = at("sret", 512, R[1] + 3584)
        mx, xc = at("mx", HEADS * (T + 3), o_v), at("xc", 4096, R[3])
        wifr = at("wifr", 1024, R[3])
        wifh, wifl = at("wifh", 1024, R[3] + 1024, F32R), at("wifl", 1024, R[3] + 2048, F32R)
        wqk = at("wqk", 1024, o_g + 1024)
        rowi, rowf, rowb, rowm = (at(f"row{n}", T, R[1] + T * i) for i, n in enumerate("ifbm"))
        rres = at("rres", T, o_g + 1024)
        rk = at("rk", T, o_g)
        va, qT, kTt, wt = at("va", NC * HEADS * 129, o_v), at("qT", 4096, R[0]), at("kTt", 4096, R[1]), at("wt", 4096, R[2])
        hm = at("hm", 4096, R[1])
        kw = [at(f"kw{i}", 512, R[3] + 512 * i) for i in range(2)]
        cst8 = at("cstate", HEADS * 129, R[3] + 1024)
        inter = at("inter", HEADS * 129, R[3] + 1024 + 520)
        us, uu, sz, yb, yc = (at(n, 4096, R[i]) for n, i in (("us", 0), ("uu", 2), ("sz", 3), ("yb", 1), ("yc", 0)))
        tb = [at(f"tb{i}", TCOLS, o_v + 2064 * i) for i in range(2)]
        yh, yl = at("yh", 4096, R[2], F32R), at("yl", 4096, R[1], F32R)
        zin = at("zin", GB * NBT, o_ys)
        zz = at("zz", GB * NBT, o_ys + 264)
        zt1 = at("zt1", GB * NBT, o_g)
        zt2 = at("zt2", GB * NBT, o_g + 264)
        zc = [at(f"zc{i}", GB * NB, o_g + 528 + 256 * i) for i in range(2)]
        zs = [at(f"zs{i}", GB * NB, o_g + 1040 + 256 * i) for i in range(2)]
        s5o = [at(f"s5o{i}", 1024, o_v + 1024 * i) for i in range(2)]
        oyh, oyl = at("oyh", 8192, R[0], F32R), at("oyl", 8192, R[2], F32R)
        yraw = [at(f"yraw{i}", 1024, o_v + 1024 * i) for i in range(2)]
        lng, lnb = at("lng", D, o_x), at("lnb", D, o_x + D)
        xr = [at(f"xr{i}", D, o_x + 2 * D + D * i) for i in range(2)]
        rr = [at(f"rr{i}", D, o_g + D * i) for i in range(2)]
        xn = at("xn", NC * D, R[0])
        xin = at("xin", KT * T, R[0])

        gp = [ctx.enter_context(nc.psum_tensor(f"gp{i}", [128, 1024], F32))[:, :] for i in range(2)]
        mm = [ctx.enter_context(nc.psum_tensor(f"mm{i}", [128, 1024], F32))[:, :] for i in range(2)]
        bank = [mm[i // 2][:, 512 * (i % 2):512 * (i % 2) + 512] for i in range(4)]


        p0 = R[2]
        def ptake(n):
            nonlocal p0
            p0 += n
            return p0 - n
        (p_mag, p_ang, p_sin, p_cos, p_qr, p_qi, p_k, p_t) = (at(f"p_{n}", 576, ptake(576)) for n in
                                                             ("mag", "ang", "sin", "cos", "qr", "qi", "k", "t"))
        p_x, p_y = at("p_x", 512, ptake(512)), at("p_y", 512, ptake(512))
        p_u, p_v = at("p_u", 576, ptake(576)), at("p_v", 576, ptake(576))
        p_t1, p_t2, p_h0, p_w = (at(f"p_{n}", 288, ptake(288)) for n in ("t1", "t2", "h0", "w"))
        assert p0 <= R[3] + 4096, p0 - R[2]
        p_b1, p_b2, p_c1, p_c2 = (at(f"p_{n}", 1024, o_v + 1024 * i) for i, n in enumerate(("b1", "b2", "c1", "c2")))
        p_tab = at("p_tab", TTOP, o_g)
        p_ks, p_jr = at("p_ks", GB * 128, o_w, rows=16), at("p_jr", J_RES, o_w + 256)
        p_di = at("p_di", 1024, o_ys, rows=16)
        p_in = at("p_in", 192, o_w + 1024)
        p_s = at("p_s", 1024, o_w + 1280)
        p_zero = at("p_zero", 112 * 64, R[0], rows=16)

        names = """c_in j_in s5p_in pos_in cp_out zeroed kd_zeroed p_small p_ang p_sin p_h0 p_w p_tr p_ev p_k p_ke tab_out ks_out
            rope_ang rope_sc rope_st xin_in xT_hi xT_lo raw_in0 raw_in1 hi_done lo_done o_used g_done0 g_done1 g_free0
            g_free1 mem_in mem_hi mem_lo rope_in rope_done qk2_in r_sc r_att r_kn r_o r_ho r_u r_state hn_var hn_sd
            gate_used0 gate_used1 tr_done tr_free ys_out0 ys_out1 x_s x_max x_e x_norm x_t x_pt x_pv x_pvev xa_out wif_in
            wif_hi wif_lo bias_in if_done if_act rows_done res_in colt_done cols_done wqk_in conv_done xc_ready
            ones_done a_bc w_arg w_exp w_mask qk_mm qk_ev s_mm s_w k_tr k_w m_num m_read m_c m_st gn_in cw_in ud_out uu_in
            tb_in0 tb_in1 s_g s_gr s_z s_y s_ye yd_out yc_in gy_hi gy_lo s5_out0 s5_out1 y_in0 y_in1 oy_hi oy_lo o_done o_free
            xr_in0 xr_in1 ln_in ln_var ln_sd ln_y xs_out xn_in xt_done v_step a_step""".split()
        S = {n: ctx.enter_context(nc.semaphore(n)) for n in names}
        raw_in, g_done, g_free = [[S[f"{n}{i}"] for i in range(2)] for n in ("raw_in", "g_done", "g_free")]
        gate_used, ys_out = [[S[f"{n}{i}"] for i in range(2)] for n in ("gate_used", "ys_out")]
        s5_out = [S[f"s5_out{i}"] for i in range(2)]
        y_in, xr_in, tb_in = [[S[f"{n}{i}"] for i in range(2)] for n in ("y_in", "xr_in", "tb_in")]

        def half0(u):
            return 2 * u if u < U_GL else 2 * U_GL + (u - U_GL) if u < NUNIT else 2 * U_GL + 2 + 2 * (u - NUNIT)

        def nhalf(u):
            return 1 if U_GL <= u < NUNIT else 2

        def misc(i, n=1, rows=128):
            return cst[0:rows, K_MISC + i:K_MISC + i + n]

        ident = cst[:, K_ID:K_ID + 128]
        block = ctx.enter_context(nc.Block())

        @block.sync
        def _(sp):
            sp.dma_start(cst, dram["cst"]).then_inc(S["c_in"], 16)
            sp.dma_start(p_jr, dram["jcst"][:, 0:J_RES]).then_inc(S["j_in"], 16)
            for i in range(3):
                sp.dma_start(p_in[:, 64 * i:64 * i + 64], dram["s5a"][i]).then_inc(S["s5p_in"], 16)
            for i, t in enumerate((p_b1, p_b2, p_c1, p_c2)):
                sp.dma_start(t, dram["s5bc"][i]).then_inc(S["s5p_in"], 16)
            sp.dma_start(p_di, bass.AP(dram["s5d"].tensor, 0, [[0, 16], [1, DEPTH * GW]])).then_inc(S["s5p_in"], 16)
            sp.dma_start(rot[:, 1024:2048].bitcast(I32), bass.AP(dram["pos"].tensor, 0, [[0, 128], [1, T]])).then_inc(S["pos_in"], 16)
            sp.dma_start(xin.rearrange("p (k t) -> p k t", k=KT), dram["xT"].rearrange("(k p) t -> p k t", p=128)).then_inc(S["xin_in"], 16)
            sp.dma_start(dram["xs"][0], dram["x"]).then_inc(S["cp_out"], 16)

            def raw(l, u):
                for i in range(nhalf(u)):
                    n = half0(u) + i
                    sp.wait_ge(S["hi_done"], l * HALVES + max(n - 1, 0))
                    sp.wait_ge(S["lo_done"], l * HALVES + max(n - 1, 0))
                    row = l * NSTORED + (u if u < NUNIT else NUNIT + (u - NUNIT) % 8)
                    sp.dma_start(wraw[n % 2], dram["w"][row, :, 1024 * i:1024 * i + 1024]).then_inc(raw_in[n % 2], 16)

            with sp.Fori(0, DEPTH) as l:
                sp.wait_ge(S["p_small"], 1)
                sp.wait_ge(S["tab_out"], 16 * DEPTH * NBATCH)
                sp.wait_ge(S["ks_out"], 16 * DEPTH * NBATCH)
                sp.wait_ge(S["kd_zeroed"], 16)
                sp.wait_ge(S["o_used"], l * NOUT)
                sp.dma_start(memraw.rearrange("p (k m) -> p k m", k=KT), dram["memT"].rearrange("(k p) m -> p k m", p=128)).then_inc(S["mem_in"], 16)
                sp.wait_ge(S["xs_out"], l * 16 * NC)
                sp.wait_ge(S["rope_st"], 32)
                sp.dma_start(rope, dram["ropetab"]).then_inc(S["rope_in"], 16)
                sp.dma_start(gn, bass.AP(dram["gn"].tensor, l * GW, [[0, 128], [1, GW]])).then_inc(S["gn_in"], 16)
                sp.dma_start(small[:, 32:48], dram["convw"][l]).then_inc(S["cw_in"], 16)
                sp.dma_start(small[0:4, 48:50], dram["bif"][l]).then_inc(S["bias_in"], 16)
                for u in range(U_QK + 4):
                    raw(l, u)
                sp.wait_ge(S["rope_done"], 2 * l + 2)
                for half in range(2):
                    for h in range(HEADS):
                        src = rot[32 * h:32 * h + 32, 2048 * half:2048 * half + 2048]
                        r0 = 64 * (h % 2) + 32 * half
                        sp.dma_start(qk2[r0:r0 + 32, 2048 * (h // 2):2048 * (h // 2) + 2048], src).then_inc(S["qk2_in"], 16)
                for u in range(U_QK + 4, U_MX + 1):
                    raw(l, u)
                sp.wait_ge(S["x_pvev"], 8 * l + 8)
                sp.dma_start(wifr, dram["wif"][l]).then_inc(S["wif_in"], 16)
                sp.wait_ge(gate_used[1], NGATE * l + 4)
                sp.dma_start(rres[0:4, :], dram["jcst"][0:4, J_RES:J_RES + T]).then_inc(S["res_in"], 16)
                for u in range(U_MX + 1, U_LO + 1):
                    raw(l, u)
                sp.wait_ge(S["rows_done"], l + 1)
                sp.dma_start(wqk, dram["wqk"][l]).then_inc(S["wqk_in"], 16)
                for u in range(U_LO + 1, NUNIT):
                    raw(l, u)
                sp.wait_ge(S["ud_out"], 64 * l + 64)
                for s in range(BS):
                    src = dram["ud"].rearrange("(g c) (s j) -> s c g j", c=C5, s=BS)[BS - 1 - s]
                    sp.dma_start(uu[C5 * s:C5 * s + C5, :].rearrange("c (g j) -> c g j", g=G5), src).then_inc(S["uu_in"], 16)
                for b in range(NBATCH):
                    if b >= 2:
                        sp.wait_ge(S["s_y"], NBATCH * l + b - 1)
                    t = tb[b % 2]
                    sp.dma_start(t[:, 0:TTOP], dram["tabs"][l * NBATCH + b]).then_inc(tb_in[b % 2], 16)
                    for g in range(GB):
                        src = bass.AP(dram["kd"].tensor, ((l * NBATCH + b) * GB + g) * C5 * 240,
                                      [[16, BS], [240, C5], [1, 128]])
                        sp.dma_start(t[:, TTOP + 128 * g:TTOP + 128 * g + 128], src).then_inc(tb_in[b % 2], 16)
                sp.wait_ge(S["s_ye"], NBATCH * l + NBATCH)
                for t in range(BS):
                    dst = dram["yd"].rearrange("(g c) (t j) -> t c g j", c=C5, t=BS)[t]
                    sp.dma_start(dst, yb[C5 * t:C5 * t + C5, :].rearrange("c (g j) -> c g j", g=G5)).then_inc(S["yd_out"], 16)
                sp.wait_ge(S["yd_out"], 128 * l + 128)
                sp.dma_start(yc.rearrange("p (m t) -> p m t", m=4), dram["yd"].rearrange("(m p) t -> p m t", p=128)).then_inc(S["yc_in"], 16)
                raw(l, NUNIT)
                sp.wait_ge(s5_out[0], 32 * l + 32)
                sp.wait_ge(s5_out[1], 32 * l + 32)
                sp.wait_ge(S["xa_out"], 64 * l + 64)
                sp.wait_ge(ys_out[0], 128 * l + 128)
                sp.wait_ge(ys_out[1], 128 * l + 128)
                sp.dma_start(lng, bass.AP(dram["lng"].tensor, l * D, [[0, 128], [1, D]])).then_inc(S["ln_in"], 16)
                sp.dma_start(lnb, bass.AP(dram["lnb"].tensor, l * D, [[0, 128], [1, D]])).then_inc(S["ln_in"], 16)
                for j in range(NOUT):
                    if j % 2 == 0:
                        for i in range(2):
                            n = j + i
                            if n >= 2:
                                sp.wait_ge(S["oy_hi"], 16 * l + n - 1)
                                sp.wait_ge(S["oy_lo"], 16 * l + n - 1)
                            k0, t0 = (2 * n) % 16, 512 * (n // 8)
                            sp.dma_start(yraw[n % 2].rearrange("p (k t) -> p k t", k=2),
                                         dram["yt"][k0:k0 + 2, :, t0:t0 + 512].rearrange("k p t -> p k t")).then_inc(y_in[n % 2], 16)
                    if j:
                        raw(l, NUNIT + j)
                sp.wait_ge(S["xs_out"], 16 * NC * (l + 1))
                for c in range(NC):
                    sp.dma_start(xn[:, D * c:D * c + D], dram["xs"][l + 1, 128 * c:128 * c + 128, :]).then_inc(S["xn_in"], 16)
            sp.wait_ge(S["xn_in"], 16 * NC * DEPTH)

        @block.tensor
        def _(pe):
            def mm3(out, ah, al, bh, bl, start, stop):
                nc.tensor.matmul(out, ah, bh, start=start, stop=False)
                nc.tensor.matmul(out, ah, bl, start=False, stop=False)
                return nc.tensor.matmul(out, al, bh, start=False, stop=stop)

            pe.wait_ge(S["c_in"], 16)
            with pe.Fori(0, DEPTH * NBATCH) as b:
                pe.wait_ge(S["p_w"], b + 1)
                pe.wait_ge(S["p_ev"], b)
                for g in range(GB):
                    last = nc.tensor.transpose(bank[0][:, 128 * g:128 * g + 128], p_w[:, 128 * g:128 * g + 128], ident)
                last.then_inc(S["p_tr"], 1)
                pe.wait_ge(S["p_h0"], b + 1)
                pe.wait_ge(S["p_ke"], b)
                for g in range(GB):
                    last = nc.tensor.matmul(bank[1][0:16, 128 * g:128 * g + 128], p_w[:, 128 * g:128 * g + C5],
                                            p_h0[:, 144 * g:144 * g + 128], start=True, stop=True)
                last.then_inc(S["p_k"], 1)

            def unit(l, u):
                kind = "MC" if u < U_MV else "MT" if u < U_QK else "C" if u in CUNITS else "G" if u >= U_GL else "T"
                wh, wl = whi[u % 2], wlo[u % 2]
                pe.wait_ge(S["lo_done"], l * HALVES + half0(u) + nhalf(u))
                for g in range(2):
                    pe.wait_ge(g_free[g], NUNIT * l + u)
                    if kind in ("C", "G"):
                        kt, rh, rl = (KT, xh, xl) if kind == "C" else (4, yh, yl)
                        for n in range(2):
                            for k in range(kt):
                                w0, x0 = 256 * k + 128 * g, T * k + 512 * n
                                last = mm3(gp[g][:, 512 * n:512 * n + 512], wh[:, w0:w0 + 128], wl[:, w0:w0 + 128],
                                           rh[:, x0:x0 + 512], rl[:, x0:x0 + 512], k == 0, k == kt - 1)
                    elif kind == "MC":
                        for k in range(KT):
                            w0 = 256 * k + 128 * g
                            last = mm3(gp[g][:, 0:256], wh[:, w0:w0 + 128], wl[:, w0:w0 + 128],
                                       memh[:, NMEM * k:NMEM * k + NMEM], meml[:, NMEM * k:NMEM * k + NMEM], k == 0, k == KT - 1)
                    else:
                        for c in range(1 if kind == "MT" else 4):
                            for k in range(KT):
                                if kind == "MT":
                                    ah, al, a0 = memh, meml, NMEM * k + 128 * g
                                else:
                                    ah, al, a0 = xh, xl, T * k + 128 * (4 * g + c)
                                last = mm3(gp[g][:, 256 * c:256 * c + 256], ah[:, a0:a0 + 128], al[:, a0:a0 + 128],
                                           wh[:, 256 * k:256 * k + 256], wl[:, 256 * k:256 * k + 256], k == 0, k == KT - 1)
                    last.then_inc(g_done[g], 1)

            def transposes(l, first, src, used):
                for g in range(2):
                    pe.wait_ge(gate_used[g], NGATE * l + used)
                for i in range(8):
                    j, half, n = i // 2, i % 2, first + i
                    if n >= 2:
                        pe.wait_ge(S["tr_free"], 16 * l + n - 1)
                    for c in range(4):
                        a0 = GW * (4 * half + c) + 128 * j
                        last = nc.tensor.transpose(bank[i % 2][:, 128 * c:128 * c + 128], src[:, a0:a0 + 128], ident)
                    last.then_inc(S["tr_done"], 1)

            with pe.Fori(0, DEPTH) as l:
                pe.wait_ge(S["mem_lo"], l + 1)
                for u in range(U_MK, U_QK):
                    unit(l, u)
                pe.wait_ge(S["xT_hi"], 16 * l + 16)
                pe.wait_ge(S["xT_lo"], 16 * l + 16)
                for u in range(U_QK, U_RZ):
                    unit(l, u)

                pe.wait_ge(S["qk2_in"], 128 * l + 128)
                v = rv

                def r_scores(c):
                    pe.wait_ge(S["r_att"], NC * l + c)
                    pe.wait_ge(S["r_kn"], NC * l + c)
                    for h in range(HEADS):
                        p, r0 = h // 2, 64 * (h % 2)
                        nc.tensor.matmul(bank[h % 2][:, 128 * p:128 * p + 128],
                                         qk2[r0:r0 + 64, 2048 * p + T + 128 * c:2048 * p + T + 128 * c + 128],
                                         qk2[r0:r0 + 64, 2048 * p + 128 * c:2048 * p + 128 * c + 128], start=True, stop=True)
                    for p in range(2):
                        last = nc.tensor.transpose(bank[1][:, 256 + 128 * p:256 + 128 * p + 128],
                                                   qk2[:, 2048 * p + T + 128 * c:2048 * p + T + 128 * c + 128], ident)
                    last.then_inc(S["r_sc"], 1)

                r_scores(0)
                for c in range(NC):
                    if c + 1 < NC:
                        r_scores(c + 1)
                    pe.wait_ge(S["r_att"], NC * l + c + 1)
                    pe.wait_ge(S["r_ho"], NC * l + c)
                    if c:
                        pe.wait_ge(S["r_state"], NC * l + c)
                    for h in range(HEADS):
                        p, r0 = h // 2, 64 * (h % 2)
                        o = bank[2][:, 128 * h:128 * h + 128]
                        last = nc.tensor.matmul(o, att[c % 2][:, 256 * (h % 2) + 128 * p:256 * (h % 2) + 128 * p + 128], v[:, GW * c + 128 * h:GW * c + 128 * h + 128],
                                                start=True, stop=c == 0)
                        if c:
                            last = nc.tensor.matmul(o, qk2[:, 2048 * p + 128 * c:2048 * p + 128 * c + 128],
                                                    sret[:, 128 * h:128 * h + 128], start=False, stop=True)
                    last.then_inc(S["r_o"], 1)
                    pe.wait_ge(S["r_kn"], NC * l + c + 1)
                    pe.wait_ge(S["r_state"], NC * l + c)
                    for h in range(HEADS):
                        p, r0 = h // 2, 64 * (h % 2)
                        last = nc.tensor.matmul(bank[3][r0:r0 + 64, 128 * p:128 * p + 128], kn[c % 2][:, DK * h:DK * h + DK],
                                                v[:, GW * c + 128 * h:GW * c + 128 * h + 128], start=True, stop=True)
                    last.then_inc(S["r_u"], 1)
                unit(l, U_RZ)
                unit(l, U_RZ + 1)

                def x_scores(i):
                    h, half = i // 2, i % 2
                    pe.wait_ge(S["x_e"], 4 * (8 * l + i))
                    for c in range(4):
                        a0 = T * h + 512 * half + 128 * c
                        last = nc.tensor.matmul(mm[0][:, 256 * c:256 * c + 256], aq[:, a0:a0 + 128], mkT[:, NMEM * h:NMEM * h + NMEM],
                                                start=True, stop=True)
                    last.then_inc(S["x_s"], 1)

                pe.wait_ge(S["r_ho"], NC * l + NC)
                pe.wait_ge(S["r_state"], NC * l + NC)
                x_scores(0)
                for i in range(8):
                    h, half = i // 2, i % 2
                    if i < 7:
                        x_scores(i + 1)
                    pe.wait_ge(S["x_norm"], 8 * l + i + 1)
                    pe.wait_ge(S["x_pvev"], 8 * l + i)
                    for m in range(2):
                        for c in range(4):
                            last = nc.tensor.transpose(mm[1][:, 512 * m + 128 * c:512 * m + 128 * c + 128],
                                                       pm[:, 256 * c + 128 * m:256 * c + 128 * m + 128], ident)
                    last.then_inc(S["x_t"], 1)
                    pe.wait_ge(S["x_pt"], 8 * l + i + 1)
                    for m in range(2):
                        last = nc.tensor.matmul(mm[1][:, 0:512], mvT[:, GW * m + 128 * h:GW * m + 128 * h + 128], pt[:, 512 * m:512 * m + 512],
                                                start=m == 0, stop=m == 1)
                    last.then_inc(S["x_pv"], 1)
                unit(l, U_AZ)
                unit(l, U_AZ + 1)
                transposes(l, 0, hr, 2)

                pe.wait_ge(S["wif_hi"], l + 1)
                pe.wait_ge(S["wif_lo"], l + 1)
                pe.wait_ge(S["tr_free"], 16 * l + 8)
                for n in range(2):
                    for k in range(KT):
                        last = mm3(mm[1][:, 512 * n:512 * n + 512], wifh[:, 128 * k:128 * k + 128], wifl[:, 128 * k:128 * k + 128],
                                   xh[:, T * k + 512 * n:T * k + 512 * n + 512], xl[:, T * k + 512 * n:T * k + 512 * n + 512],
                                   k == 0, k == KT - 1)
                last.then_inc(S["if_done"], 1)
                for u in range(U_MX, U_LO):
                    unit(l, u)
                pe.wait_ge(S["rows_done"], l + 1)
                for c in range(NC):
                    last = nc.tensor.transpose(mm[0][:, 128 * c:128 * c + 128], rk[:, 128 * c:128 * c + 128], ident)
                last.then_inc(S["colt_done"], 1)
                for h in range(HEADS):
                    last = nc.tensor.matmul(bank[2][:, NC * h:NC * h + NC], cst[0:4, K_ONE + 128 * h:K_ONE + 128 * h + 128],
                                            small[0:4, 16:24], start=True, stop=True)
                last.then_inc(S["colt_done"], 1)
                pe.wait_ge(S["cols_done"], 5 * l + 5)
                for i in range(8):
                    h, half = i // 2, i % 2
                    if i >= 2:
                        pe.wait_ge(S["w_arg"], 8 * l + i - 1)
                    nc.tensor.matmul(bank[i % 2], cst[0:4, K_ONE + 128 * h:K_ONE + 128 * h + 128],
                                     rowf[0:4, 512 * half:512 * half + 512], start=True, stop=True).then_inc(S["a_bc"], 1)
                pe.wait_ge(S["wqk_in"], 16 * l + 16)
                for i in range(16):
                    w, h, half = i // 8, i // 2 % 4, i % 2
                    pe.wait_ge(S["xc_ready"], 4 * l + h + 1)
                    if i >= 2:
                        pe.wait_ge(S["qk_ev"], 16 * l + i - 1)
                    nc.tensor.matmul(bank[2 + i % 2], wqk[:, 512 * w + 128 * h:512 * w + 128 * h + 128],
                                     xc[:, T * h + 512 * half:T * h + 512 * half + 512], start=True, stop=True).then_inc(S["qk_mm"], 1)
                pe.wait_ge(S["qk_ev"], 16 * l + 16)
                pe.wait_ge(S["w_arg"], 8 * l + 8)
                for c in range(NC):
                    if c >= 2:
                        pe.wait_ge(S["s_w"], NC * l + c - 1)
                    for h in range(HEADS):
                        a0 = 512 * c + 128 * h
                        last = nc.tensor.matmul(bank[c % 2][:, 128 * h:128 * h + 128], kTt[:, a0:a0 + 128], qT[:, a0:a0 + 128],
                                                start=True, stop=True)
                    last.then_inc(S["s_mm"], 1)
                pe.wait_ge(S["ones_done"], l + 1)
                pe.wait_ge(g_free[0], NUNIT * l + U_LO)
                pe.wait_ge(g_free[1], NUNIT * l + U_LO)
                pe.wait_ge(S["s_w"], NC * l + NC)

                def k_natural(c):
                    pe.wait_ge(S["k_w"], NC * l + c)
                    for h in range(HEADS):
                        last = nc.tensor.transpose(bank[3][:, 128 * h:128 * h + 128], kTt[:, 512 * c + 128 * h:512 * c + 128 * h + 128], ident)
                    last.then_inc(S["k_tr"], 1)

                k_natural(0)
                for c in range(NC):
                    if c + 1 < NC:
                        k_natural(c + 1)
                    pe.wait_ge(S["m_read"], NC * l + c)
                    for h in range(HEADS):
                        a0, o0, v0 = 512 * c + 128 * h, 512 * (h // 2) + 129 * (h % 2), 129 * (HEADS * c + h)
                        last = nc.tensor.matmul(gp[0][:, o0:o0 + 129], wt[:, a0:a0 + 128], va[:, v0:v0 + 129], start=True, stop=True)
                    if c:
                        pe.wait_ge(S["m_st"], NC * l + c)
                        for h in range(HEADS):
                            a0, o0 = 512 * c + 128 * h, 512 * (h // 2) + 129 * (h % 2)
                            last = nc.tensor.matmul(gp[1][:, o0:o0 + 129], qT[:, a0:a0 + 128], cst8[:, 129 * h:129 * h + 129],
                                                    start=True, stop=True)
                    last.then_inc(S["m_num"], 1)
                    pe.wait_ge(S["k_w"], NC * l + c + 1)
                    pe.wait_ge(S["m_st"], NC * l + c)
                    for h in range(HEADS):
                        o0, v0 = 512 * (h // 2) + 129 * (h % 2), 129 * (HEADS * c + h)
                        last = nc.tensor.matmul(mm[0][:, o0:o0 + 129], kw[c % 2][:, 128 * h:128 * h + 128], va[:, v0:v0 + 129],
                                                start=True, stop=True)
                    last.then_inc(S["m_c"], 1)
                pe.wait_ge(S["m_read"], NC * l + NC)
                for u in range(U_LO, U_SZ):
                    unit(l, u)
                pe.wait_ge(S["m_st"], NC * l + NC)
                transposes(l, 8, hm, 8)
                unit(l, U_SZ)
                unit(l, U_SZ + 1)

                pe.wait_ge(S["uu_in"], 128 * l + 128)
                pe.wait_ge(S["tr_free"], 16 * l + 16)

                def s_inputs(b):
                    n = (NBATCH // 2) * l + b // 2
                    pe.wait_ge(tb_in[b % 2], 48 * n + 48)
                    pe.wait_ge(S["s_gr"], NBATCH * l + b)
                    for g in range(GB):
                        for w in range(2):
                            a0 = TG + 192 * g + 64 * w
                            last = nc.tensor.matmul(bank[w][:, 128 * g:128 * g + 128], tb[b % 2][:, a0:a0 + 128],
                                                    uu[:, 128 * (GB * b + g):128 * (GB * b + g) + 128], start=True, stop=True)
                    last.then_inc(S["s_g"], 1)

                s_inputs(0)
                for b in range(NBATCH):
                    if b + 1 < NBATCH:
                        s_inputs(b + 1)
                    pe.wait_ge(S["s_z"], NBATCH * l + b + 1)
                    if b >= 2:
                        pe.wait_ge(S["s_ye"], NBATCH * l + b - 1)
                    t = tb[b % 2]
                    for g in range(GB):
                        o = bank[2 + b % 2][:, 128 * g:128 * g + 128]
                        nc.tensor.matmul(o, t[:, TTOP + 128 * g:TTOP + 128 * g + 128],
                                         uu[:, 128 * (GB * b + g):128 * (GB * b + g) + 128], start=True, stop=False)
                        nc.tensor.matmul(o, t[:, TH + 128 * g:TH + 128 * g + 128], zc[b % 2][:, 128 * g:128 * g + 128], start=False, stop=False)
                        last = nc.tensor.matmul(o, t[:, TH2 + 128 * g:TH2 + 128 * g + 128], zs[b % 2][:, 128 * g:128 * g + 128],
                                                start=False, stop=True)
                    last.then_inc(S["s_y"], 1)
                pe.wait_ge(S["gy_hi"], 4 * l + 4)
                pe.wait_ge(S["gy_lo"], 4 * l + 4)
                unit(l, U_GL)
                unit(l, U_GL + 1)

                op = gp + mm
                pe.wait_ge(g_free[0], NUNIT * l + NUNIT)
                pe.wait_ge(g_free[1], NUNIT * l + NUNIT)
                pe.wait_ge(S["s_ye"], NBATCH * l + NBATCH)
                for j in range(NOUT):
                    hf, kq, n = j // 8, j % 8 // 2, j % 2
                    u = NUNIT + j
                    pe.wait_ge(S["lo_done"], l * HALVES + half0(u) + 2)
                    pe.wait_ge(S["oy_hi"], 16 * l + 8 * hf + 2 * kq + 2)
                    pe.wait_ge(S["oy_lo"], 16 * l + 8 * hf + 2 * kq + 2)
                    for cc in range(4):
                        if hf and kq == 0 and n == 0:
                            pe.wait_ge(S["o_free"], NC * l + cc + 1)
                        for k in range(4):
                            y0, w0 = 512 * (4 * kq + k) + 128 * cc, 512 * k
                            last = mm3(op[cc][:, 512 * n:512 * n + 512], oyh[:, y0:y0 + 128], oyl[:, y0:y0 + 128],
                                       whi[u % 2][:, w0:w0 + 512], wlo[u % 2][:, w0:w0 + 512], kq == 0 and k == 0, kq == 3 and k == 3)
                        if kq == 3 and n == 1 and cc < 3:
                            last.then_inc(S["o_done"], 1)
                    last.then_inc(S["o_used"], 1)
                pe.wait_ge(S["xn_in"], 16 * NC * (l + 1))
                for i in range(16):
                    half, k = i // 8, i % 8
                    if i >= 4:
                        pe.wait_ge(S["xT_hi"], 16 * l + 16 + i - 3)
                        pe.wait_ge(S["xT_lo"], 16 * l + 16 + i - 3)
                    for c in range(4):
                        a0 = D * (4 * half + c) + 128 * k
                        last = nc.tensor.transpose(bank[i % 4][:, 128 * c:128 * c + 128], xn[:, a0:a0 + 128], ident)
                    last.then_inc(S["xt_done"], 1)
                pe.wait_ge(S["xT_hi"], 16 * l + 32)
                pe.wait_ge(S["xT_lo"], 16 * l + 32)

        @block.gpsimd
        def _(pool):
            def lo(l, u):
                for i in range(nhalf(u)):
                    n = half0(u) + i
                    pool.wait_ge(S["hi_done"], l * HALVES + n + 1)
                    nc.gpsimd.tensor_tensor(wlo[u % 2][:, 1024 * i:1024 * i + 1024], wraw[n % 2],
                                            whi[u % 2][:, 1024 * i:1024 * i + 1024].bitcast(F32), ALU.subtract).then_inc(S["lo_done"], 1)

            pool.wait_ge(S["xT_lo"], 16)
            nc.gpsimd.memset(p_zero[:, 0:7168], 0.0).then_inc(S["zeroed"], 1)
            pool.wait_ge(S["zeroed"], 1)
            pool.dma_start(bass.AP(dram["kd"].tensor, 0, [[240, C5], [C5 * 240, DEPTH * G5], [1, 112]]),
                           p_zero[:, 0:7168].rearrange("c (g z) -> c g z", z=112)).then_inc(S["kd_zeroed"], 16)
            pool.wait_ge(S["kd_zeroed"], 16)
            pool.wait_ge(S["ks_out"], 16 * DEPTH * NBATCH)
            with pool.Fori(0, DEPTH) as l:
                for u in range(U_LO + 1):
                    lo(l, u)
                for c in range(NC):
                    pool.wait_ge(S["w_exp"], NC * l + c + 1)
                    w = wt[:, 512 * c:512 * c + 512].rearrange("p (h t) -> p h t", h=HEADS)
                    nc.gpsimd.tensor_tensor(w, w, bcast(cst[:, K_CAUS:K_CAUS + 128], HEADS, 0), ALU.mult).then_inc(S["w_mask"], 1)
                for u in range(U_LO + 1, NUNIT + NOUT):
                    lo(l, u)

        @block.scalar
        def _(act):
            A = Steps(act, S["a_step"], steps_a)
            A.layer, A.base = 0, 0
            F = nc.scalar.activation

            def sines(out_sin, out_cos, ang, tmp, sem_in, n_in, sem_out):
                act.wait_ge(sem_in, n_in)
                A.link(F(tmp, ang, ACT.Abs))
                A.link(F(out_cos, tmp, ACT.Sin, scale=-1.0, bias=misc(M_HPI)))
                F(out_sin, ang, ACT.Sin).then_inc(sem_out, 1)

            act.wait_ge(S["c_in"], 16)
            act.wait_ge(S["xin_in"], 16)
            for i in range(16):
                F(xh[:, 512 * i:512 * i + 512], xin[:, 512 * i:512 * i + 512], ACT.Copy).then_inc(S["xT_hi"], 1)
            act.wait_ge(S["rope_ang"], 1)
            A.link(F(rot[:, 2048:3072], rot[:, 0:1024], ACT.Abs))
            A.link(F(rot[:, 3072:4096], rot[:, 2048:3072], ACT.Sin, scale=-1.0, bias=misc(M_HPI)))
            F(rot[:, 1024:2048], rot[:, 0:1024], ACT.Sin).then_inc(S["rope_sc"], 1)
            act.wait_ge(S["rope_sc"], 1)
            act.dma_start(dram["ropetab"][:, 0:1024], rot[:, 3072:4096]).then_inc(S["rope_st"], 16)
            act.dma_start(dram["ropetab"][:, 1024:2048], rot[:, 1024:2048]).then_inc(S["rope_st"], 16)
            sines(p_sin, p_cos, p_ang, p_t, S["p_ang"], 1, S["p_sin"])
            npre = A.n
            with act.Fori(0, DEPTH * NBATCH) as b:
                act.wait_ge(S["p_ang"], b + 2)
                tc_, ts_ = p_tab[:, TCOS:TCOS + GB * NBT], p_tab[:, TSIN:TSIN + GB * NBT]
                F(p_t1[:, 0:GB * NBT], ts_, ACT.Abs).then_inc(S["a_step"], 1)
                act.wait_ge(S["a_step"], npre + b * 2 + 1)
                F(tc_, p_t1[:, 0:GB * NBT], ACT.Sin, scale=-1.0, bias=misc(M_HPI))
                F(ts_, ts_, ACT.Sin, scale=misc(M_SGN)).then_inc(S["a_step"], 1)
                act.wait_ge(S["a_step"], npre + b * 2 + 2)
                act.wait_ge(S["p_tr"], b + 1)
                tg = p_tab[:, TG:TG + GB * 192].rearrange("p (g n) -> p g n", g=GB)
                bk = bank[0][:, 0:GB * 128].rearrange("p (g n) -> p g n", g=GB)
                F(tg[:, :, 0:128], bk, ACT.Copy)
                F(tg[:, :, 128:192], bk[:, :, 0:64], ACT.Copy).then_inc(S["p_ev"], 1)
                act.wait_ge(S["p_ev"], b + 1)
                act.wait_ge(S["p_h0"], b + 1)
                act.dma_start(dram["tabs"][b], p_tab).then_inc(S["tab_out"], 16)
                act.wait_ge(S["p_ke"], b + 1)
                act.dma_start(dram["kd"].rearrange("g c n -> c g n")[:, bass.ds(b * GB, GB), 112:240], p_ks.rearrange("c (g n) -> c g n", g=GB)).then_inc(S["ks_out"], 16)
                act.wait_ge(S["tab_out"], 16 * b + 16)
                act.wait_ge(S["ks_out"], 16 * b + 16)
            A.base = npre + 2 * DEPTH * NBATCH

            def split(l, u):
                if u < 2:
                    act.wait_ge(S["o_used"], NOUT * l)
                elif u - 2 < NUNIT:
                    act.wait_ge(g_done[1], NUNIT * l + u - 1)
                else:
                    act.wait_ge(S["o_used"], NOUT * l + u - 2 - NUNIT + 1)
                for i in range(nhalf(u)):
                    n = half0(u) + i
                    act.wait_ge(raw_in[n % 2], 16 * ((HALVES // 2) * l + n // 2 + 1))
                    F(whi[u % 2][:, 1024 * i:1024 * i + 1024], wraw[n % 2], ACT.Copy).then_inc(S["hi_done"], 1)

            def take_out(l, u, fn):
                split(l, u + 1)
                for g in range(2):
                    act.wait_ge(g_done[g], NUNIT * l + u + 1)
                    fn(u, g).then_inc(g_free[g], 1)

            def gates(l, u, n, func, scale=1.0):
                split(l, u + 1)
                for g in range(2):
                    act.wait_ge(g_done[g], NUNIT * l + u + 1)
                    act.wait_ge(gate_used[g], NGATE * l + n)
                    F(gate[g], gp[g], func, scale=scale).then_inc(g_free[g], 1)

            def store_tiles(l, first, tile0):
                for i in range(8):
                    j, half, n = i // 2, i % 2, first + i
                    act.wait_ge(S["tr_done"], 16 * l + n + 1)
                    act.wait_ge(ys_out[i % 2], 16 * (8 * l + n // 2))
                    F(ystage[i % 2], bank[i % 2], ACT.Copy).then_inc(S["tr_free"], 1)
                    act.wait_ge(S["tr_free"], 16 * l + n + 1)
                    act.dma_start(dram["yt"][tile0 + j, :, 512 * half:512 * half + 512], ystage[i % 2]).then_inc(ys_out[i % 2], 16)

            with act.Fori(0, DEPTH) as l:
                A.begin(l)
                act.wait_ge(S["mem_in"], 16 * l + 16)
                F(memh, memraw, ACT.Copy).then_inc(S["mem_hi"], 1)
                split(l, 0)
                for u in (U_MK, U_MK + 1):
                    take_out(l, u, lambda u, g: F(mkT[:, NMEM * (2 * (u - U_MK) + g):NMEM * (2 * (u - U_MK) + g) + NMEM],
                                                  gp[g][:, 0:NMEM], ACT.Copy))
                for u in (U_MV, U_MV + 1):
                    take_out(l, u, lambda u, g: F(mvT[:, GW * g + 256 * (u - U_MV):GW * g + 256 * (u - U_MV) + 256],
                                                  gp[g][:, 0:256], ACT.Copy))
                for u in (U_QK, U_QK + 1):
                    take_out(l, u, lambda u, g: F(qk[:, T * (2 * (u - U_QK) + g):T * (2 * (u - U_QK) + g) + T], gp[g], ACT.Copy))
                for u in (U_RV, U_RV + 1):
                    take_out(l, u, lambda u, g: F(tview(rv, GW, g, u - U_RV), gp[g].rearrange("p (c n) -> p c n", c=4), ACT.Copy))
                for u in (U_AQ, U_AQ + 1):
                    take_out(l, u, lambda u, g: F(aq[:, T * (2 * (u - U_AQ) + g):T * (2 * (u - U_AQ) + g) + T], gp[g], ACT.Copy))
                act.wait_ge(S["hn_var"], 2 * l + 1)
                F(sd[:, 0:32], mv.rearrange("p (n k) -> p n k", k=2)[:, :, 1], ACT.Sqrt, bias=misc(M_GNE)).then_inc(S["hn_sd"], 1)
                gates(l, U_RZ, 0, ACT.Silu)
                gates(l, U_RZ + 1, 1, ACT.Silu)
                for i in range(8):
                    h, half = i // 2, i % 2
                    act.wait_ge(S["x_max"], 8 * l + i + 1)
                    act.wait_ge(S["x_t"], 8 * l + i)
                    for c in range(4):
                        F(pm[:, 256 * c:256 * c + 256], mm[0][:, 256 * c:256 * c + 256], ACT.Exp, scale=128 ** -0.5,
                          bias=small[:, 4 + c:5 + c], accum_out=small[:, 8 + c:9 + c]).then_inc(S["x_e"], 1)
                    act.wait_ge(S["x_t"], 8 * l + i + 1)
                    act.wait_ge(S["x_pv"], 8 * l + i)
                    F(pt, mm[1], ACT.Copy).then_inc(S["x_pt"], 1)
                    act.wait_ge(S["x_pv"], 8 * l + i + 1)
                    F(xo[:, T * h + 512 * half:T * h + 512 * half + 512], mm[1][:, 0:512], ACT.Copy).then_inc(S["x_pvev"], 1)
                gates(l, U_AZ, 2, ACT.Silu)
                gates(l, U_AZ + 1, 3, ACT.Silu)
                for j in range(4):
                    act.wait_ge(gate_used[j % 2], NGATE * l + 3 + j // 2)
                    act.dma_start(dram["yt"][12 + j], xo[:, T * j:T * j + T]).then_inc(S["xa_out"], 16)
                store_tiles(l, 0, 0)
                act.wait_ge(S["wif_in"], 16 * l + 16)
                F(wifh, wifr, ACT.Copy).then_inc(S["wif_hi"], 1)
                act.wait_ge(S["if_done"], l + 1)
                act.wait_ge(S["bias_in"], 16 * l + 16)
                F(rowi[0:4, :], mm[1][0:4, :], ACT.Identity, bias=small[0:4, 48:49]).then_inc(S["if_act"], 1)
                A.link(F(rowb[0:4, :], mm[1][32:36, :], ACT.Identity, bias=small[0:4, 49:50]))
                A.link(F(rowm[0:4, :], rowb[0:4, :], ACT.Abs))
                A.link(F(rowm[0:4, :], rowm[0:4, :], ACT.Exp, scale=-1.0))
                F(rowm[0:4, :], rowm[0:4, :], ACT.Ln, bias=misc(M_ONE, 1, 4)).then_inc(S["if_act"], 1)
                for u in (U_MX, U_MX + 1):
                    take_out(l, u, lambda u, g: F(mx[:, (T + 3) * (2 * (u - U_MX) + g) + 3:(T + 3) * (2 * (u - U_MX) + g) + 3 + T], gp[g], ACT.Copy))
                for h in range(HEADS):
                    act.wait_ge(S["conv_done"], 4 * l + h + 1)
                    F(xc[:, T * h:T * h + T], xc[:, T * h:T * h + T], ACT.Silu).then_inc(S["xc_ready"], 1)
                vview = va.rearrange("p (c h e) -> p c h e", c=NC, h=HEADS)
                for u in (U_LV, U_LV + 1):
                    h0 = 2 * (u - U_LV)
                    take_out(l, u, lambda u, g: F(vview[:, 4 * g:4 * g + 4, h0:h0 + 2, 0:128],
                                                  gp[g].rearrange("p (c h e) -> p c h e", c=4, h=2), ACT.Copy))
                act.wait_ge(S["colt_done"], 2 * l + 2)
                src = mm[0].rearrange("p (c x) -> p c x", c=NC)
                for k in range(4):
                    F(cols[:, 32 * k:32 * k + 32].rearrange("p (c h) -> p c h", c=NC), src[:, :, 32 * k:32 * k + 4],
                      ACT.Exp if k else ACT.Copy).then_inc(S["cols_done"], 1)
                F(dec, bank[2][:, 0:32], ACT.Exp).then_inc(S["cols_done"], 1)
                for c in range(NC):
                    act.wait_ge(S["w_arg"], 8 * l + 8)
                    F(wt[:, 512 * c:512 * c + 512], wt[:, 512 * c:512 * c + 512], ACT.Exp).then_inc(S["w_exp"], 1)
                for i in range(16):
                    w, h, half = i // 8, i // 2 % 4, i % 2
                    act.wait_ge(S["qk_mm"], 16 * l + i + 1)
                    dst = (kTt if w else qT).rearrange("p (c h t) -> p c h t", c=NC, h=HEADS)[:, 4 * half:4 * half + 4, h, :]
                    F(dst, bank[2 + i % 2].rearrange("p (c t) -> p c t", c=4), ACT.Copy, scale=128 ** -0.5 if w else 1.0).then_inc(S["qk_ev"], 1)
                gates(l, U_LO, 4, ACT.Tanh, 0.5)
                gates(l, U_LO + 1, 5, ACT.Tanh, 0.5)
                act.wait_ge(S["hn_var"], 2 * l + 2)
                F(sd[:, 0:32], mv.rearrange("p (n k) -> p n k", k=2)[:, :, 1], ACT.Sqrt, bias=misc(M_GNE)).then_inc(S["hn_sd"], 1)
                gates(l, U_LZ, 6, ACT.Silu)
                gates(l, U_LZ + 1, 7, ACT.Silu)
                for u in (U_SU, U_SU + 1):
                    take_out(l, u, lambda u, g: F(us[:, T * (2 * (u - U_SU) + g):T * (2 * (u - U_SU) + g) + T].rearrange("p (s j) -> p j s", s=BS),
                                                  gp[g].rearrange("p (j s) -> p j s", s=BS), ACT.Copy))
                for m in range(4):
                    act.wait_ge(g_free[m % 2], NUNIT * l + U_SU + m // 2 + 1)
                    act.dma_start(dram["ud"][128 * m:128 * m + 128, :], us[:, T * m:T * m + T]).then_inc(S["ud_out"], 16)
                store_tiles(l, 8, 8)
                for u in (U_SZ, U_SZ + 1):
                    take_out(l, u, lambda u, g: F(sz[:, T * (2 * (u - U_SZ) + g):T * (2 * (u - U_SZ) + g) + T].rearrange("p (s j) -> p j s", s=BS),
                                                  gp[g].rearrange("p (j s) -> p j s", s=BS), ACT.Silu))
                for b in range(NBATCH):
                    act.wait_ge(S["s_y"], NBATCH * l + b + 1)
                    F(yb[:, 256 * b:256 * b + 256], bank[2 + b % 2][:, 0:256], ACT.Copy).then_inc(S["s_ye"], 1)
                act.wait_ge(S["yc_in"], 16 * l + 16)
                for m in range(4):
                    A.link(F(yc[:, T * m:T * m + T], yc[:, T * m:T * m + T], ACT.Gelu_apprx_tanh))
                    F(yh[:, T * m:T * m + T], yc[:, T * m:T * m + T], ACT.Copy).then_inc(S["gy_hi"], 1)
                gates(l, U_GL, 8, ACT.Tanh, 0.5)
                gates(l, U_GL + 1, 9, ACT.Tanh, 0.5)
                for m in range(4):
                    act.wait_ge(gate_used[m % 2], NGATE * l + 9 + m // 2)
                    act.dma_start(dram["yt"][4 + m], s5o[m % 2]).then_inc(s5_out[m % 2], 16)

                def yhi(n):
                    kq = n % 8 // 2
                    act.wait_ge(y_in[n % 2], 16 * (8 * l + n // 2 + 1))
                    if n >= 8:
                        act.wait_ge(S["o_used"], NOUT * l + 2 * kq + 2)
                    F(oyh[:, 1024 * (n % 8):1024 * (n % 8) + 1024], yraw[n % 2], ACT.Copy).then_inc(S["oy_hi"], 1)

                def norm(c):
                    act.wait_ge(S["ln_var"], NC * l + c + 1)
                    F(sd[:, 32:33], mv[:, 33:34], ACT.Sqrt, bias=misc(M_LNE)).then_inc(S["ln_sd"], 1)
                    act.wait_ge(S["ln_y"], NC * l + c + 1)
                    act.dma_start(dram["xs"][l + 1, 128 * c:128 * c + 128, :], rr[c % 2]).then_inc(S["xs_out"], 16)
                    if c + 2 < NC:
                        xload(c + 2)

                def xload(c):
                    act.dma_start(xr[c % 2], dram["xs"][l, 128 * c:128 * c + 128, :]).then_inc(xr_in[c % 2], 16)

                act.wait_ge(S["cp_out"], 16)
                act.wait_ge(S["xs_out"], 16 * NC * l)
                xload(0)
                xload(1)
                for j in range(NOUT):
                    if j % 2 == 0:
                        yhi(j)
                        yhi(j + 1)
                    if j + 1 < NOUT:
                        split(l, NUNIT + j + 1)
                    if j == 8:
                        for c in range(4):
                            norm(c)
                for c in range(4, NC):
                    norm(c)
                for i in range(16):
                    half, k = i // 8, i % 8
                    act.wait_ge(S["xt_done"], 16 * l + i + 1)
                    F(xh[:, T * k + 512 * half:T * k + 512 * half + 512], bank[i % 4], ACT.Copy).then_inc(S["xT_hi"], 1)
            assert A.n == steps_a, A.n

        @block.vector
        def _(dve):
            V = Steps(dve, S["v_step"], steps_v)
            V.layer = 0
            TT, TS, STT = nc.vector.tensor_tensor, nc.vector.tensor_scalar, nc.vector.scalar_tensor_tensor

            def reduce_angle(link, x, k):
                link(TS(k, x, 1.0 / TWO_PI, MAGIC, ALU.mult, ALU.add))
                link(TS(k, k, MAGIC, None, ALU.subtract))
                for part in (C1, C2, C3):
                    link(STT(x, k, -part, x, ALU.mult, ALU.add))
                return TS(x, x, PI_LO, -PI_LO, ALU.min, ALU.max)

            def exp_(x, out, t):
                V.link(TS(x, x, -200.0, 200.0, ALU.max, ALU.min))
                V.link(TS(t, x, 1.0 / math.log(2.0), MAGIC, ALU.mult, ALU.add))
                V.link(TS(t, t, MAGIC, None, ALU.subtract))
                V.link(STT(x, t, -0.693359375, x, ALU.mult, ALU.add))
                V.link(STT(x, t, 2.12194440054690583e-4, x, ALU.mult, ALU.add))
                coef = [1 / math.factorial(n) for n in range(9)]
                V.link(TS(out, x, coef[8], coef[7], ALU.mult, ALU.add))
                for n in range(6, -1, -1):
                    V.link(TT(out, out, x, ALU.mult))
                    V.link(TS(out, out, coef[n], None, ALU.add))
                V.link(TS(t, t, -127.0, 128.0, ALU.max, ALU.min))
                V.link(TS(t, t, 127.0, 2.0 ** 23, ALU.add, ALU.mult))
                V.link(nc.vector.tensor_copy(x.bitcast(I32), t))
                V.link(TT(out, out, x, ALU.mult))

            dve.wait_ge(S["xin_in"], 16)
            for i in range(16):
                dve.wait_ge(S["xT_hi"], i + 1)
                TT(xl[:, 512 * i:512 * i + 512], xin[:, 512 * i:512 * i + 512], xh[:, 512 * i:512 * i + 512].bitcast(F32),
                   ALU.subtract).then_inc(S["xT_lo"], 1)
            dve.wait_ge(S["c_in"], 16)
            dve.wait_ge(S["pos_in"], 16)
            V.link(nc.vector.tensor_copy(rot[:, 0:1024], rot[:, 1024:2048].bitcast(I32)))
            V.link(TS(rot[:, 0:1024], rot[:, 0:1024], misc(M_INV), None, ALU.mult))
            reduce_angle(V.link, rot[:, 0:1024], rot[:, 1024:2048]).then_inc(S["rope_ang"], 1)
            dve.wait_ge(S["rope_st"], 32)

            dve.wait_ge(S["s5p_in"], 128)
            dve.wait_ge(S["j_in"], 16)
            are, aim, ldt = (p_in[:, 64 * i:64 * i + 64] for i in range(3))
            sc = [p_s[:, 64 * i:64 * i + 64] for i in range(16)]
            dt, la, th, kk, pp, dn, fr, fi, s8, s9, a8 = sc[:11]
            exp_(ldt, dt, kk)
            V.link(TT(la, are, dt, ALU.mult))
            V.link(TT(th, aim, dt, ALU.mult))
            V.link(reduce_angle(V.link, th, kk))
            for t in range(BS + 1):
                V.link(TS(p_mag[:, 64 * t:64 * t + 64], la, float(t), None, ALU.mult))
                V.link(TS(p_ang[:, 64 * t:64 * t + 64], th, float(t), None, ALU.mult))
            exp_(p_mag, p_qr, p_k)
            V.link(reduce_angle(V.link, p_ang, p_k))
            V.link(nc.vector.tensor_copy(p_mag, p_qr))
            nc.vector.tensor_copy(a8, p_ang[:, 512:576]).then_inc(S["p_ang"], 1)
            dve.wait_ge(S["p_sin"], 1)
            V.link(TT(p_qr, p_mag, p_cos, ALU.mult))
            V.link(TT(p_qi, p_mag, p_sin, ALU.mult))
            V.link(TS(pp, p_qr[:, 64:128], -1.0, None, ALU.add))
            ai = p_qi[:, 64:128]
            V.link(TT(dn, are, are, ALU.mult))
            V.link(TT(s8, aim, aim, ALU.mult))
            V.link(TT(dn, dn, s8, ALU.add))
            V.link(nc.vector.reciprocal(dn, dn))
            V.link(TT(fr, pp, are, ALU.mult))
            V.link(TT(s8, ai, aim, ALU.mult))
            V.link(TT(fr, fr, s8, ALU.add))
            V.link(TT(fr, fr, dn, ALU.mult))
            V.link(TT(fi, ai, are, ALU.mult))
            V.link(TT(s8, pp, aim, ALU.mult))
            V.link(TT(fi, fi, s8, ALU.subtract))
            V.link(TT(fi, fi, dn, ALU.mult))

            def v3(x, n=8):
                return x.rearrange("p (t g) -> p t g", g=64)[:, 0:n, :]

            frb, fib = bcast(fr, 8, 0), bcast(fi, 8, 0)
            kv, tv = v3(p_k), v3(p_t)
            V.link(TT(v3(p_x), v3(p_qr), frb, ALU.mult))
            V.link(TT(kv, v3(p_qi), fib, ALU.mult))
            V.link(TT(v3(p_x), v3(p_x), kv, ALU.subtract))
            V.link(TT(v3(p_y), v3(p_qr), fib, ALU.mult))
            V.link(TT(kv, v3(p_qi), frb, ALU.mult))
            V.link(TT(v3(p_y), v3(p_y), kv, ALU.add))
            V.link(TS(p_y, p_y, misc(M_NSGN), None, ALU.mult))
            V.link(TS(p_u, p_qr, misc(M_SGN), None, ALU.mult))
            V.link(TS(p_v, p_qi, -1.0, None, ALU.mult))
            di = p_di.rearrange("c (g o) -> c g o", o=C5)
            V.link(TT(di, di, bcast(p_jr[0:16, J_I16:J_I16 + 16], 64, 0), ALU.mult))
            nc.vector.tensor_copy(s9, p_mag[:, 512:576]).then_inc(S["p_small"], 1)
            dve.wait_ge(S["p_small"], 1)
            npre, PER_B = V.n, 18
            with dve.Fori(0, DEPTH * NBATCH) as b:
                q = [0]

                def link(ins):
                    q[0] += 1
                    ins.then_inc(S["v_step"], 1)
                    dve.wait_ge(S["v_step"], npre + b * PER_B + q[0])

                def pair(x, y, n, t0=0):
                    out = []
                    for z in (x, y):
                        z = z.rearrange("p (t g) -> p g t", g=64)[:, bass.ds(b * GB, GB), t0:t0 + n]
                        out.append(bcast(z, C5, 3))
                    return out

                def chan(x, n):
                    x = x.rearrange("p (g c) -> p g c", c=C5)[:, bass.ds(b * GB, GB), :]
                    return bcast(x, n, 2)

                def view(x, n):
                    return x[:, 0:GB * n * C5].rearrange("p (g t c) -> p g t c", g=GB, t=n)

                dve.wait_ge(S["tab_out"], b * 16)
                dve.wait_ge(S["ks_out"], b * 16)
                X, Y = pair(p_x, p_y, BS)
                U, Vv = pair(p_u, p_v, BS + 1)
                for g in range(GB):
                    ph = p_tab[:, TSIN + NBT * g:TSIN + NBT * g + NBT]
                    link(TS(ph, p_jr[:, J_ROW:J_ROW + NBT], a8[:, bass.ds(b * GB + g, 1)], None, ALU.mult))
                ph = p_tab[:, TSIN:TSIN + GB * NBT]
                reduce_angle(link, ph, p_t[:, 0:GB * NBT]).then_inc(S["p_ang"], 1)
                link(TT(view(p_w, BS), X, chan(p_b1, BS), ALU.mult))
                link(TT(view(p_t2, BS), Y, chan(p_b2, BS), ALU.mult))
                TT(view(p_w, BS), view(p_w, BS), view(p_t2, BS), ALU.add).then_inc(S["p_w"], 1)
                dve.wait_ge(S["p_w"], b + 1)
                link(TT(view(p_h0, 9), U, chan(p_c1, 9), ALU.mult))
                link(TT(view(p_t2, 9), Vv, chan(p_c2, 9), ALU.mult))
                link(TT(view(p_h0, 9), view(p_h0, 9), view(p_t2, 9), ALU.add))
                for g in range(GB):
                    link(nc.vector.tensor_copy(p_tab[:, TH + 128 * g:TH + 128 * g + 128], p_h0[:, 144 * g + 16:144 * g + 144]))
                U1, V1 = pair(p_u, p_v, BS, 1)
                h2 = p_tab[:, TH2:TH2 + GB * 128].rearrange("p (g t c) -> p g t c", g=GB, t=BS)
                link(TT(h2, V1, chan(p_c1, BS), ALU.mult))
                link(TT(view(p_t2, BS), U1, chan(p_c2, BS), ALU.mult))
                link(TT(h2, h2, view(p_t2, BS), ALU.subtract))
                for g in range(GB):
                    last = TS(p_tab[:, TRR + NBT * g:TRR + NBT * g + NBT], p_jr[:, J_MASK:J_MASK + NBT], s9[:, bass.ds(b * GB + g, 1)],
                              None, ALU.mult)
                last.then_inc(S["p_h0"], 1)
                dve.wait_ge(S["p_k"], b + 1)
                link(nc.vector.tensor_copy(p_ks, bank[1][0:16, 0:GB * 128]))
                ks = p_ks.rearrange("c (g n) -> c g n", g=GB)[:, :, 0:C5]
                TT(ks, ks, di[:, bass.ds(b * GB, GB), :], ALU.add).then_inc(S["p_ke"], 1)
                assert q[0] == PER_B, q
            V.base = npre + DEPTH * NBATCH * PER_B

            def head_norm(l, h_, n):
                for i in range(32):
                    nc.vector.bn_stats(stats[:, 6 * i:6 * i + 6], h_[:, 128 * i:128 * i + 128]).then_inc(S["v_step"], 1)
                    V.n += 1
                V.join()
                nc.vector.memset(sd[0:1, 40:41], 0.0)
                for i in range(32):
                    last = nc.vector.bn_aggr(mv[:, 2 * i:2 * i + 2], stats[:, 6 * i:6 * i + 6])
                last.then_inc(S["hn_var"], 1)
                dve.wait_ge(S["hn_sd"], 2 * l + n + 1)
                V.link(nc.vector.reciprocal(sd[:, 0:32], sd[:, 0:32]))
                for i in range(32):
                    V.inc(TS(h_[:, 128 * i:128 * i + 128], h_[:, 128 * i:128 * i + 128], mv[:, 2 * i:2 * i + 1], sd[:, i:i + 1],
                             ALU.subtract, ALU.mult))
                V.join()

            with dve.Fori(0, DEPTH) as l:
                V.begin(l)
                dve.wait_ge(S["mem_hi"], l + 1)
                TT(meml, memraw, memh.bitcast(F32), ALU.subtract).then_inc(S["mem_lo"], 1)
                dve.wait_ge(g_free[0], NUNIT * l + U_QK + 2)
                dve.wait_ge(g_free[1], NUNIT * l + U_QK + 2)
                dve.wait_ge(S["rope_in"], 16 * l + 16)
                a, b_ = (qk[:, 2048 * i:2048 * i + 2048].rearrange("p (k t) -> p k t", k=2) for i in range(2))
                ra, rb = (rot[:, 2048 * i:2048 * i + 2048].rearrange("p (k t) -> p k t", k=2) for i in range(2))
                co, si = bcast(rope[:, 0:T], 2, 0), bcast(rope[:, T:2 * T], 2, 0)
                V.inc(TT(ra, a, co, ALU.mult))
                V.link(TT(rb, b_, si, ALU.mult))
                TT(ra, ra, rb, ALU.subtract).then_inc(S["rope_done"], 1)
                V.inc(TT(a, a, si, ALU.mult))
                V.link(TT(b_, b_, co, ALU.mult))
                dve.wait_ge(S["rope_done"], 2 * l + 1)
                TT(rb, a, b_, ALU.add).then_inc(S["rope_done"], 1)

                dve.wait_ge(g_done[1], NUNIT * l + U_QK + 1)
                V.link(nc.vector.memset(sret, 0.0))
                dve.wait_ge(S["qk2_in"], 128 * l + 128)
                for c in range(NC):
                    dve.wait_ge(S["r_sc"], NC * l + c + 1)
                    if c >= 2:
                        dve.wait_ge(S["r_o"], NC * l + c - 1)
                        dve.wait_ge(S["r_u"], NC * l + c - 1)
                    TT(att[c % 2].rearrange("p (b n) -> p b n", b=2), mm[0].rearrange("p (b n) -> p b n", b=2)[:, :, 0:256],
                       cst[:, K_MASK:K_MASK + 512].rearrange("p (b n) -> p b n", b=2), ALU.mult).then_inc(S["r_att"], 1)
                    TT(kn[c % 2], bank[1][:, 256:512], cst[:, K_KDEC:K_KDEC + 256], ALU.mult).then_inc(S["r_kn"], 1)
                    dve.wait_ge(S["r_o"], NC * l + c + 1)
                    hv = hr[:, GW * c:GW * c + GW].rearrange("p (h e) -> p h e", h=HEADS)
                    TT(hv, bank[2].rearrange("p (h e) -> p h e", h=HEADS), bcast(misc(M_QD, 4), 128, 2), ALU.mult).then_inc(S["r_ho"], 1)
                    dve.wait_ge(S["r_u"], NC * l + c + 1)
                    if c:
                        dve.wait_ge(S["r_state"], NC * l + c)
                    for h in range(HEADS):
                        p, r0 = h // 2, 64 * (h % 2)
                        new, up = sret[r0:r0 + 64, 128 * h:128 * h + 128], bank[3][r0:r0 + 64, 128 * p:128 * p + 128]
                        if c:
                            last = STT(new, new, cst[r0:r0 + 64, K_MISC + M_CD + p:K_MISC + M_CD + p + 1], up, ALU.mult, ALU.add)
                        else:
                            last = nc.vector.tensor_copy(new, up)
                    last.then_inc(S["r_state"], 1)
                dve.wait_ge(S["r_ho"], NC * l + NC)
                head_norm(l, hr, 0)
                for i in range(4):
                    u, g = i // 2, i % 2
                    dve.wait_ge(g_free[g], NUNIT * l + U_RZ + u + 1)
                    hv = tview(hr, GW, g, u)
                    TT(hv, hv, gate[g].rearrange("p (c n) -> p c n", c=4), ALU.mult).then_inc(gate_used[g], 1)

                for i in range(8):
                    dve.wait_ge(S["x_s"], 8 * l + i + 1)
                    V.link(nc.vector.tensor_reduce(small[:, 0:4], mm[0].rearrange("p (c m) -> p c m", c=4), AX.X, ALU.max))
                    TS(small[:, 4:8], small[:, 0:4], -(128 ** -0.5), None, ALU.mult).then_inc(S["x_max"], 1)
                    dve.wait_ge(S["x_e"], 4 * (8 * l + i + 1))
                    V.link(nc.vector.reciprocal(small[:, 12:16], small[:, 8:12]))
                    pv = pm.rearrange("p (c m) -> p c m", c=4)
                    TT(pv, pv, bcast(small[:, 12:16], NMEM, 2), ALU.mult).then_inc(S["x_norm"], 1)
                for i in range(4):
                    u, g = i // 2, i % 2
                    dve.wait_ge(g_free[g], NUNIT * l + U_AZ + u + 1)
                    dve.wait_ge(S["x_pvev"], 8 * l + 8)
                    TT(xo[:, T * i:T * i + T], xo[:, T * i:T * i + T], gate[g], ALU.mult).then_inc(gate_used[g], 1)

                dve.wait_ge(S["wif_hi"], l + 1)
                TT(wifl, wifr, wifh.bitcast(F32), ALU.subtract).then_inc(S["wif_lo"], 1)
                dve.wait_ge(S["if_act"], 2 * l + 2)
                dve.wait_ge(S["res_in"], 16 * l + 16)
                V.link(STT(rowf[0:4, :], rowb[0:4, :], 0.0, rowm[0:4, :], ALU.min, ALU.subtract))
                V.inc(nc.vector.tensor_tensor_scan(rowb[0:4, :], rres[0:4, :], rowf[0:4, :], 0.0, ALU.mult, ALU.add))
                V.link(nc.vector.tensor_tensor_scan(rowm[0:4, :], rowf[0:4, :], rowi[0:4, :], 0.0, ALU.add, ALU.max))
                V.link(nc.vector.memset(rk, 0.0))
                V.inc(TT(rk[0:4, :], rowi[0:4, :], rowb[0:4, :], ALU.subtract))
                V.inc(TS(rk[96:100, :], rowm[0:4, :], -1.0, None, ALU.mult))
                V.inc(nc.vector.memset(small[0:4, 0:1], 0.0))
                V.inc(nc.vector.tensor_copy(small[0:4, 1:8], rowm[0:4, :].rearrange("p (c t) -> p c t", t=CH)[:, 0:7, CH - 1]))
                V.link(TT(rowf[0:4, :], rowb[0:4, :], rowm[0:4, :], ALU.subtract))
                V.link(nc.vector.tensor_copy(small[0:4, 8:16], rowf[0:4, :].rearrange("p (c t) -> p c t", t=CH)[:, :, CH - 1]))
                V.inc(TT(small[0:4, 16:24], small[0:4, 8:16], small[0:4, 0:8], ALU.add))

                def rows(x):
                    return x.rearrange("p (c t) -> p c t", t=CH)

                V.inc(TT(rows(rk[32:36, :]), rows(rowf[0:4, :]), bcast(small[0:4, 0:8], CH, 2), ALU.add))
                TT(rows(rk[64:68, :]), rows(rk[0:4, :]), bcast(small[0:4, 8:16], CH, 2), ALU.add).then_inc(S["rows_done"], 1)
                mxv = mx.rearrange("p (h t) -> p h t", h=HEADS)
                V.link(nc.vector.memset(mxv[:, :, 0:3], 0.0))
                dve.wait_ge(S["cw_in"], 16 * l + 16)
                for h in range(HEADS):
                    dve.wait_ge(g_free[h % 2], NUNIT * l + U_MX + h // 2 + 1)
                    y = xc[:, T * h:T * h + T]
                    for k in (3, 2, 1):
                        w = small[:, 32 + 4 * h + k:33 + 4 * h + k]
                        x_ = mxv[:, h, k:k + T]
                        V.link(TS(y, x_, w, None, ALU.mult) if k == 3 else STT(y, x_, w, y, ALU.mult, ALU.add))
                    STT(y, mxv[:, h, 0:T], small[:, 32 + 4 * h:33 + 4 * h], y, ALU.mult, ALU.add).then_inc(S["conv_done"], 1)
                dve.wait_ge(S["conv_done"], 4 * l + 4)
                nc.vector.memset(va.rearrange("p (g e) -> p g e", e=129)[:, :, 128:129], 1.0).then_inc(S["ones_done"], 1)
                dve.wait_ge(S["cols_done"], 5 * l + 5)
                for i in range(8):
                    h, half = i // 2, i % 2
                    dve.wait_ge(S["a_bc"], 8 * l + i + 1)
                    for c in range(4 * half, 4 * half + 4):
                        last = TS(wt[:, 512 * c + 128 * h:512 * c + 128 * h + 128], bank[i % 2][:, 128 * (c % 4):128 * (c % 4) + 128],
                                  cols[:, 4 * c + h:4 * c + h + 1], 0.0, ALU.add, ALU.min)
                    last.then_inc(S["w_arg"], 1)
                for c in range(NC):
                    dve.wait_ge(S["s_mm"], NC * l + c + 1)
                    dve.wait_ge(S["w_mask"], NC * l + c + 1)
                    w = wt[:, 512 * c:512 * c + 512]
                    TT(w, w, bank[c % 2], ALU.mult).then_inc(S["s_w"], 1)
                wi, wk, em = (cols[:, 32 * k:32 * k + 32] for k in (1, 2, 3))

                def k_weights(c):
                    dve.wait_ge(S["k_tr"], NC * l + c + 1)
                    if c >= 2:
                        dve.wait_ge(S["m_c"], NC * l + c - 1)
                    TT(kw[c % 2].rearrange("p (h d) -> p h d", h=HEADS), bank[3].rearrange("p (h d) -> p h d", h=HEADS),
                       bcast(wk[:, 4 * c:4 * c + 4], 128, 2), ALU.mult).then_inc(S["k_w"], 1)

                def heads2(x):
                    return x.rearrange("p (a x) -> p a x", a=2)[:, :, 0:258].rearrange("p a (b e) -> p a b e", b=2)

                num = inter.rearrange("p (a b e) -> p a b e", a=2, b=2)
                k_weights(0)
                for c in range(NC):
                    dve.wait_ge(S["m_num"], NC * l + c + 1)
                    if c == 0:
                        nc.vector.tensor_copy(num, heads2(gp[0])).then_inc(S["m_read"], 1)
                    else:
                        V.link(TT(num, heads2(gp[1]), bcast(wi[:, 4 * c:4 * c + 4].rearrange("p (a b) -> p a b", a=2), 129, 3), ALU.mult))
                        TT(num, num, heads2(gp[0]), ALU.add).then_inc(S["m_read"], 1)
                    dve.wait_ge(S["m_read"], NC * l + c + 1)
                    dn4 = small[:, 52:56]
                    den = inter.rearrange("p (h e) -> p h e", h=HEADS)[:, :, 128]
                    V.link(STT(dn4, den, -1.0, den, ALU.mult, ALU.max))
                    V.link(TT(dn4, dn4, em[:, 4 * c:4 * c + 4], ALU.max))
                    V.link(nc.vector.reciprocal(dn4, dn4))
                    V.link(TS(dn4, dn4, 0.5, None, ALU.mult))
                    V.inc(TT(hm[:, GW * c:GW * c + GW].rearrange("p (h e) -> p h e", h=HEADS),
                             inter.rearrange("p (h e) -> p h e", h=HEADS)[:, :, 0:128], bcast(dn4, 128, 2), ALU.mult))
                    if c + 1 < NC:
                        k_weights(c + 1)
                    dve.wait_ge(S["m_c"], NC * l + c + 1)
                    if c == 0:
                        nc.vector.tensor_copy(cst8.rearrange("p (a b e) -> p a b e", a=2, b=2), heads2(mm[0])).then_inc(S["m_st"], 1)
                    else:
                        dve.wait_ge(S["m_st"], NC * l + c)
                        for h in range(HEADS):
                            o0 = 512 * (h // 2) + 129 * (h % 2)
                            last = STT(cst8[:, 129 * h:129 * h + 129], cst8[:, 129 * h:129 * h + 129], dec[:, NC * h + c:NC * h + c + 1],
                                       mm[0][:, o0:o0 + 129], ALU.mult, ALU.add)
                        last.then_inc(S["m_st"], 1)
                V.join()
                for i in range(4):
                    u, g = i // 2, i % 2
                    dve.wait_ge(g_free[g], NUNIT * l + U_LO + u + 1)
                    hv = tview(hm, GW, g, u)
                    STT(hv, gate[g].rearrange("p (c n) -> p c n", c=4), 1.0, hv, ALU.add, ALU.mult).then_inc(gate_used[g], 1)
                for g in range(2):
                    dve.wait_ge(gate_used[g], NGATE * l + 6)
                head_norm(l, hm, 1)
                dve.wait_ge(S["gn_in"], 16 * l + 16)
                for i in range(4):
                    u, g = i // 2, i % 2
                    dve.wait_ge(g_free[g], NUNIT * l + U_LZ + u + 1)
                    hv = tview(hm, GW, g, u)
                    V.link(TT(hv, hv, gate[g].rearrange("p (c n) -> p c n", c=4), ALU.mult))
                    TT(hv, hv, bcast(gn[:, 256 * u:256 * u + 256], 4, 0), ALU.mult).then_inc(gate_used[g], 1)

                dve.wait_ge(ys_out[0], 16 * 8 * (l + 1))
                dve.wait_ge(ys_out[1], 16 * 8 * (l + 1))
                zv = zin.rearrange("p (g j) -> p g j", g=GB)
                V.link(nc.vector.memset(zv[:, :, 0:1], 0.0))
                for b in range(NBATCH):
                    t = tb[b % 2]
                    ct, st = (t[:, o:o + GB * NBT].rearrange("p (g j) -> p g j", g=GB) for o in (TCOS, TSIN))
                    dve.wait_ge(tb_in[b % 2], 48 * ((NBATCH // 2) * l + b // 2) + 48)
                    dve.wait_ge(S["s_g"], NBATCH * l + b + 1)
                    z1, z2 = (z.rearrange("p (g j) -> p g j", g=GB)[:, :, 1:NBT] for z in (zt1, zt2))
                    (TT(z1, ct[:, :, 1:NBT], bank[0][:, 0:256].rearrange("p (g j) -> p g j", g=GB), ALU.mult))
                    TT(z2, st[:, :, 1:NBT], bank[1][:, 0:256].rearrange("p (g j) -> p g j", g=GB), ALU.mult).then_inc(S["s_gr"], 1)
                    dve.wait_ge(S["s_gr"], NBATCH * l + b + 1)
                    V.link(TT(zv[:, :, 1:NBT], z1, z2, ALU.add))
                    V.link(nc.vector.tensor_tensor_scan(zz, t[:, TRR:TRR + GB * NBT], zin, 0.0, ALU.mult, ALU.add))
                    if b >= 2:
                        dve.wait_ge(S["s_y"], NBATCH * l + b - 1)
                    zf = zz.rearrange("p (g j) -> p g j", g=GB)[:, :, 0:NB]
                    TT(zc[b % 2].rearrange("p (g j) -> p g j", g=GB), zf, ct[:, :, 0:NB], ALU.mult)
                    TT(zs[b % 2].rearrange("p (g j) -> p g j", g=GB), zf, st[:, :, 0:NB], ALU.mult).then_inc(S["s_z"], 1)
                dve.wait_ge(S["yd_out"], 128 * l + 128)
                for m in range(4):
                    dve.wait_ge(S["gy_hi"], 4 * l + m + 1)
                    TT(yl[:, T * m:T * m + T], yc[:, T * m:T * m + T], yh[:, T * m:T * m + T].bitcast(F32), ALU.subtract).then_inc(S["gy_lo"], 1)
                for m in range(4):
                    u, g = m // 2, m % 2
                    dve.wait_ge(g_free[g], NUNIT * l + U_GL + u + 1)
                    V.link(STT(gate[g], gate[g], 1.0, yc[:, T * m:T * m + T], ALU.add, ALU.mult))
                    if m >= 2:
                        dve.wait_ge(s5_out[g], 32 * l + 16)
                    (STT(s5o[g].rearrange("p (j s) -> p s j", s=BS), gate[g].rearrange("p (s j) -> p s j", s=BS), 0.5,
                               sz[:, T * m:T * m + T].rearrange("p (s j) -> p s j", s=BS), ALU.mult, ALU.mult)).then_inc(gate_used[g], 1)

                def ylo(n):
                    dve.wait_ge(S["oy_hi"], 16 * l + n + 1)
                    TT(oyl[:, 1024 * (n % 8):1024 * (n % 8) + 1024], yraw[n % 2],
                       oyh[:, 1024 * (n % 8):1024 * (n % 8) + 1024].bitcast(F32), ALU.subtract).then_inc(S["oy_lo"], 1)

                def norm(c):
                    dve.wait_ge(S["o_done"], 6 * l + 3 * (c // 4) + min(c % 4 + 1, 3))
                    if c % 4 == 3:
                        dve.wait_ge(S["o_used"], NOUT * l + 8 * (c // 4) + 8)
                    dve.wait_ge(xr_in[c % 2], 16 * (4 * l + c // 2 + 1))
                    if c >= 2:
                        dve.wait_ge(S["xs_out"], 16 * (NC * l + c - 1))
                    x_, r_ = xr[c % 2], rr[c % 2]
                    STT(r_, x_, ALPHA, (gp + mm)[c % 4], ALU.mult, ALU.add).then_inc(S["o_free"], 1)
                    dve.wait_ge(S["o_free"], NC * l + c + 1)
                    for i in range(2):
                        V.inc(nc.vector.bn_stats(stats[:, 6 * i:6 * i + 6], r_[:, 512 * i:512 * i + 512]))
                    V.join()
                    nc.vector.memset(sd[0:1, 40:41], 0.0)
                    nc.vector.bn_aggr(mv[:, 32:34], stats[:, 0:12]).then_inc(S["ln_var"], 1)
                    dve.wait_ge(S["ln_sd"], NC * l + c + 1)
                    V.link(nc.vector.reciprocal(sd[:, 33:34], sd[:, 32:33]))
                    V.link(STT(r_, r_, mv[:, 32:33], lng, ALU.subtract, ALU.mult))
                    STT(r_, r_, sd[:, 33:34], lnb, ALU.mult, ALU.add).then_inc(S["ln_y"], 1)

                dve.wait_ge(S["ln_in"], 32 * l + 32)
                for n in range(10):
                    ylo(n)
                for c in range(4):
                    norm(c)
                for n in range(10, 16):
                    ylo(n)
                for c in range(4, NC):
                    norm(c)
                for i in range(16):
                    half, k = i // 8, i % 8
                    x0 = T * k + 512 * half
                    dve.wait_ge(S["xT_hi"], 16 * l + 16 + i + 1)
                    TT(xl[:, x0:x0 + 512], bank[i % 4], xh[:, x0:x0 + 512].bitcast(F32), ALU.subtract).then_inc(S["xT_lo"], 1)
            assert V.n == steps_v, V.n


_OUT = (DEPTH + 1, T, D)


def kernel(x, mem, positions, w_in, s5_a_re, s5_a_im, s5_log_dt, s5_b_re, s5_b_im, s5_c_re, s5_c_im, s5_d, s5_w_glu,
           ml_conv_w, ml_wq, ml_wk, ml_b_ig, ml_b_fg, ml_gn, xa_w_kv, w_out, ln_g, ln_b):
    import concourse.bacc as bacc
    from concourse.bass_utils import run_bass_kernel_spmd

    A = np.ascontiguousarray
    x, mem, w_in = np.asarray(x), np.asarray(mem), np.asarray(w_in)
    widths = [256, 256] + [GW] * 8 + [HEADS, HEADS, GW, GW]
    edge = np.cumsum([0] + widths)
    rq, rk_, rv, rz, su, sz, mx, lv, lo, lz, mi, mf, aq, az = (w_in[:, :, a:b] for a, b in zip(edge[:-1], edge[1:]))

    def rope_halves(w):
        w = w.reshape(DEPTH, D, HEADS, 2, 32)
        return [w[:, :, :, i, :].reshape(DEPTH, D, 128) for i in range(2)]

    q0, q1 = rope_halves(rq)
    k0, k1 = rope_halves(rk_)
    kv = np.asarray(xa_w_kv)
    order = [kv[:, :, :GW], kv[:, :, GW:], np.concatenate([q0, k0, q1, k1], -1), rv, aq, rz, az, mx, lv, lo, lz, su, sz]

    def units(w, k, n):
        N = w.shape[-1]
        return w.reshape(DEPTH, k, 128, N // n, n).transpose(0, 3, 2, 1, 4).reshape(DEPTH, N // n, 128, k * n)

    parts = [units(w, KT, 256) for w in order]
    glu = units(np.asarray(s5_w_glu), 4, 256)
    parts.append(np.concatenate([glu, np.zeros_like(glu)], -1))
    wo = np.asarray(w_out).reshape(DEPTH, 4, GW, D)
    wo = [units(wo[:, q], 4, 512) for q in range(4)]
    parts += wo
    w = np.concatenate(parts, 1).reshape(DEPTH * NSTORED, 128, 2048)
    wif = np.zeros((DEPTH, D, 128), np.float32)
    wif[:, :, 0:HEADS], wif[:, :, 32:32 + HEADS] = mi, mf
    wif = wif.reshape(DEPTH, KT, 128, 128).transpose(0, 2, 1, 3).reshape(DEPTH, 128, KT * 128)
    wqk = np.stack([np.asarray(ml_wq), np.asarray(ml_wk)], 1).transpose(0, 3, 1, 2, 4).reshape(DEPTH, 128, 1024)

    def states(a):
        a = np.moveaxis(np.asarray(a), 2, 0)
        return a.reshape((P5, DEPTH * G5) + a.shape[3:])

    ldt = np.broadcast_to(np.asarray(s5_log_dt).reshape(1, DEPTH * G5), (128, DEPTH * G5))
    s5a = np.stack([np.concatenate([states(s5_a_re)] * 2), np.concatenate([states(s5_a_im)] * 2), ldt])
    br, bi = (states(b).reshape(P5, -1) for b in (s5_b_re, s5_b_im))
    cr, ci = (states(np.swapaxes(np.asarray(c), 2, 3)).reshape(P5, -1) for c in (s5_c_re, s5_c_im))
    s5bc = np.stack([np.concatenate(p) for p in ((br, bi), (bi, br), (cr, ci), (ci, cr))])
    conv = np.asarray(ml_conv_w).reshape(DEPTH, 4, HEADS, 128).transpose(0, 3, 2, 1).reshape(DEPTH, 128, 16)
    bif = np.stack([np.asarray(ml_b_ig), np.asarray(ml_b_fg)], -1)
    cst, jc = constants()
    arrays = dict(x=x[0], xT=x[0].T, memT=mem[0].T, pos=np.asarray(positions)[0].astype(np.int32), w=w, wif=wif, wqk=wqk,
                  s5a=s5a, s5bc=s5bc, s5d=np.asarray(s5_d).reshape(-1), convw=conv, bif=bif, gn=np.asarray(ml_gn).reshape(-1),
                  lng=np.asarray(ln_g).reshape(-1), lnb=np.asarray(ln_b).reshape(-1), cst=cst, jcst=jc)
    arrays = {k: A(v) for k, v in arrays.items()}
    nc = bacc.Bacc("TRN2", target_bir_lowering=False, num_devices=1)
    dram = {k: nc.dram_tensor("in_" + k, v.shape, mybir.dt.from_np(v.dtype), kind="ExternalInput").ap() for k, v in arrays.items()}
    for name, shape in (("yt", (16, 128, T)), ("ud", (GW, T)), ("yd", (GW, T)), ("ropetab", (128, 2 * T)),
                        ("tabs", (DEPTH * NBATCH, 128, TTOP)), ("kd", (DEPTH * G5, C5, 240))):
        dram[name] = nc.dram_tensor(name, shape, F32, kind="Internal").ap()
    dram["xs"] = nc.dram_tensor("xs", _OUT, F32, kind="ExternalOutput").ap()
    build(nc, dram)
    r = run_bass_kernel_spmd(nc, [{"in_" + k: v for k, v in arrays.items()}], core_ids=[0])
    return np.asarray(r.results[0]["xs"])[DEPTH:DEPTH + 1]
```

```python
import math
import numpy as np
import concourse.bass as bass
from concourse import mybir
from contextlib import ExitStack

F32 = mybir.dt.float32
F32R = mybir.dt.float32r
I32 = mybir.dt.int32
ALU = mybir.AluOpType
ACT = mybir.ActivationFunctionType
AX = mybir.AxisListType

DEPTH, D, T, NMEM, GW = 2, 1024, 1024, 256, 512
HEADS, DK, DV = 4, 64, 128
KT = D // 128
CH = 128
NC = T // CH
REF_CHUNK = 64
ALPHA = (2 * DEPTH) ** 0.25
GN_EPS, LN_EPS = 1e-6, 1e-5
G5, C5, P5 = 32, 16, 64
BS = 8
NB = T // BS
GB = 2
NBATCH = G5 // GB
NBT = NB + 1
TG, TH, TH2, TCOS, TSIN, TR, TTOP = 0, 192, 320, 448, 448 + NBT, 448 + 2 * NBT, 708
GCOLS = TTOP + 128
SLOTS = 4
GP = 4
NPB = G5 // GP
SX, SY, SU_, SV, SA, SR = 0, 8 * G5, 16 * G5, 25 * G5, 34 * G5, 35 * G5
SCOLS = 36 * G5
(U_MK, U_MV, U_QK, U_RV, U_AQ, U_RZ, U_AZ, U_MX, U_LV, U_LO, U_LZ, U_SU, U_SZ, U_GL) = range(0, 28, 2)
TABLES_AT = {U_LO: (0,), U_LO + 1: (), U_LZ: (1,), U_LZ + 1: (2, 3), U_SU: (4, 5), U_SU + 1: (6, 7)}
CUNITS = {u + i for u in (U_QK, U_AQ, U_AZ, U_MX, U_SU, U_SZ) for i in range(2)}
NGATE = 10
NUNIT = 28
NOUT = 16
HALVES = 2 * 26 + 2 + 2 * NOUT
NSTORED = NUNIT + NOUT // 2
TWO_PI = 2 * math.pi
C1 = 6.28125
C2 = float(np.float32(round((TWO_PI - C1) * 2 ** 20) / 2 ** 20))
C3 = TWO_PI - C1 - C2
MAGIC = 1.5 * 2 ** 23
TURN = 6.283185
PI_LO = 3.1415925
STEPS_V = 506
STEPS_A = 41
K_ID, K_MASK, K_KDEC, K_CAUS, K_ONE, K_MISC = 0, 128, 640, 896, 1024, 1536
(M_SGN, M_NSGN, M_HPI, M_GNE, M_LNE, M_INV, M_ONE, M_TURN, M_QD, M_CD) = (0, 1, 2, 3, 4, 5, 6, 7, 8, 12)
K_COLS = 1536 + 16
J_ROW, J_RES = 0, 136
J_COLS = J_RES + T


def constants():
    c = np.zeros((128, K_COLS), np.float64)
    c[:, K_ID:K_ID + 128] = np.eye(128)
    g = 1.0 - 2.0 ** (-5.0 - np.arange(HEADS))
    s, t = np.arange(CH)[:, None], np.arange(CH)[None, :]
    same = (s // REF_CHUNK) == (t // REF_CHUNK)
    for h in range(HEADS):
        m = np.where(s <= t, g[h] ** (t - s), np.where(same, g[h] ** (s - t), 0.0))
        m0 = K_MASK + 256 * (h % 2) + 128 * (h // 2)
        c[:, m0:m0 + 128] = m / g[h] ** (t + 1.0) * DK ** -0.5
        c[:, K_KDEC + h * DK:K_KDEC + (h + 1) * DK] = g[h] ** (CH - 1.0 - s) * DK ** -0.5
        c[:, K_MISC + M_QD + h] = (g[h] ** (np.arange(CH) + 1.0))
        c[h, K_ONE + h * 128:K_ONE + (h + 1) * 128] = 1.0
    for p in range(2):
        c[:64, K_MISC + M_CD + p] = g[2 * p] ** CH
        c[64:, K_MISC + M_CD + p] = g[2 * p + 1] ** CH
    c[:, K_CAUS:K_CAUS + 128] = (s <= t)
    c[:64, K_MISC + M_SGN], c[64:, K_MISC + M_SGN] = 1.0, -1.0
    c[:, K_MISC + M_NSGN] = -c[:, K_MISC + M_SGN]
    c[:, K_MISC + M_HPI] = math.pi / 2
    c[:, K_MISC + M_TURN] = TURN * c[:, K_MISC + M_NSGN]
    c[:, K_MISC + M_GNE], c[:, K_MISC + M_LNE] = GN_EPS, LN_EPS
    c[:, K_MISC + M_INV] = 10000.0 ** (-(np.arange(128) % 32) / 32.0)
    c[:, K_MISC + M_ONE] = 1.0
    j = np.zeros((128, J_COLS), np.float64)
    j[:, J_ROW:J_ROW + NBT] = np.arange(NBT)
    j[:, J_RES:] = (np.arange(T) % CH != 0)
    return c.astype(np.float32), j.astype(np.float32)


class Steps:

    def __init__(self, eng, sem, per_layer):
        self.eng, self.sem, self.per, self.n, self.base = eng, sem, per_layer, 0, 0

    def begin(self, layer):
        self.layer, self.n = layer, 0

    def inc(self, ins):
        ins.then_inc(self.sem, 1)
        self.n += 1

    def link(self, ins):
        self.inc(ins)
        self.eng.wait_ge(self.sem, self.layer * self.per + self.n + self.base)

    def join(self):
        self.eng.wait_ge(self.sem, self.layer * self.per + self.n + self.base)


def bcast(ap, n, dim):
    dim = max(dim, 1)
    dims = [list(x) for x in ap.ap]
    return bass.AP(ap.tensor, ap.offset, dims[:dim] + [[0, n]] + dims[dim:])


def tview(x, width, g, u):
    return x.rearrange("p (c n) -> p c n", n=width)[:, 4 * g:4 * g + 4, 256 * u:256 * u + 256]


def build(nc, dram, steps_v=STEPS_V, steps_a=STEPS_A):
    ctx = ExitStack()
    with ctx:
        arena = ctx.enter_context(nc.sbuf_tensor("arena", [128, 53200], F32))
        base = nc.sbuf_base - 53200 * 4 if nc.sbuf_base >= 53200 * 4 else 0

        def at(name, cols, off, dt=F32, rows=128):
            return nc.alloc_sbuf_tensor_at(name, [rows, cols], dt, offset=base + off * 4)[:, :]

        cursor = [0]

        def take(n):
            cursor[0] += (n + 7) // 8 * 8
            assert cursor[0] <= 53200, cursor[0]
            return cursor[0] - (n + 7) // 8 * 8

        o_x = take(2 * KT * T)
        xh, xl = at("xh", KT * T, o_x, F32R), at("xl", KT * T, o_x + KT * T, F32R)
        o_raw = take(2048)
        wraw = [at(f"wraw{i}", 1024, o_raw + 1024 * i) for i in range(2)]
        o_w = take(8192)
        whi = [at(f"whi{i}", 2048, o_w + 4096 * i, F32R) for i in range(2)]
        wlo = [at(f"wlo{i}", 2048, o_w + 4096 * i + 2048, F32R) for i in range(2)]
        R = [take(4096) for _ in range(4)]
        o_v = take(HEADS * NC * 129)
        o_g = take(2048)
        gate = [at(f"gate{i}", 1024, o_g + 1024 * i) for i in range(2)]
        o_ys = take(1024)
        ystage = [at(f"ystage{i}", 512, o_ys + 512 * i) for i in range(2)]
        cst = at("cst", K_COLS, take(K_COLS))
        gn = at("gn", GW, take(GW))
        stats = at("stats", 32 * 6, take(32 * 6))
        mv = at("mv", 64, take(64))
        sd = at("sd", 64, take(64))
        cols = at("cols", NC * 16, take(NC * 16))
        dec = at("dec", 32, take(32))
        small = at("small", 128, take(128))
        qk = at("qk", 4096, R[0])
        rot = at("rot", 4096, R[2])
        hr = at("hr", 4096, R[2])
        rope = at("rope", 2048, o_g)
        rv = at("rv", 4096, o_v)
        qk2 = at("qk2", 4096, R[0])
        mkT, mvT = at("mkT", 1024, R[1]), at("mvT", 1024, R[1] + 1024)
        pm, pt = at("pm", 1024, R[1] + 2048), at("pt", 1024, R[1] + 3072)
        memraw = at("memraw", 2048, R[2])
        memh, meml = at("memh", 2048, R[3], F32R), at("meml", 2048, R[3] + 2048, F32R)
        aq, xo = at("aq", 4096, R[3]), at("xo", 4096, R[0])
        att = [at(f"att{i}", 512, R[1] + 2048 + 512 * i) for i in range(2)]
        kn = [at(f"kn{i}", 256, R[1] + 3072 + 256 * i) for i in range(2)]
        sret = at("sret", 512, R[1] + 3584)
        mx, xc = at("mx", HEADS * (T + 3), o_v), at("xc", 4096, R[3])
        wifr = at("wifr", 1024, R[3])
        wifh, wifl = at("wifh", 1024, R[3] + 1024, F32R), at("wifl", 1024, R[3] + 2048, F32R)
        wqk = at("wqk", 1024, o_g + 1024)
        rowi, rowf, rowb, rowm = (at(f"row{n}", T, R[1] + T * i) for i, n in enumerate("ifbm"))
        rres = at("rres", T, o_g + 1024)
        rk = at("rk", T, o_g)
        va, qT, kTt, wt = at("va", NC * HEADS * 129, o_v), at("qT", 4096, R[0]), at("kTt", 4096, R[1]), at("wt", 4096, R[2])
        hm = at("hm", 4096, R[1])
        kw = [at(f"kw{i}", 512, R[3] + 512 * i) for i in range(2)]
        cst8 = at("cstate", HEADS * 129, R[3] + 1024)
        inter = at("inter", HEADS * 129, R[3] + 1024 + 520)
        us, uu, sz, yb, yc = (at(n, 4096, R[i]) for n, i in (("us", 0), ("uu", 2), ("sz", 1), ("yb", 3), ("yc", 0)))
        tb = [at(f"tb{i}", GB * GCOLS, (o_v, R[0])[i // 2] + GB * GCOLS * (i % 2)) for i in range(SLOTS)]
        yh, yl = at("yh", 4096, R[2], F32R), at("yl", 4096, R[3], F32R)
        zin = at("zin", GB * NBT, o_ys)
        zz = at("zz", GB * NBT, o_ys + 264)
        zt1 = at("zt1", GB * NBT, o_g)
        zt2 = at("zt2", GB * NBT, o_g + 264)
        zc = [at(f"zc{i}", GB * NB, o_g + 528 + 256 * i) for i in range(2)]
        zs = [at(f"zs{i}", GB * NB, o_g + 1040 + 256 * i) for i in range(2)]
        s5o = [at(f"s5o{i}", 1024, o_v + 1024 * i) for i in range(2)]
        oyh, oyl = at("oyh", 8192, R[0], F32R), at("oyl", 8192, R[2], F32R)
        yraw = [at(f"yraw{i}", 1024, o_v + 1024 * i) for i in range(2)]
        lng, lnb = at("lng", D, o_x), at("lnb", D, o_x + D)
        xr = [at(f"xr{i}", D, o_x + 2 * D + D * i) for i in range(2)]
        rr = [at(f"rr{i}", D, o_g + D * i) for i in range(2)]
        xn = [at(f"xn{i}", 4 * D, (R[0], o_v)[i]) for i in range(2)]

        gp = [ctx.enter_context(nc.psum_tensor(f"gp{i}", [128, 1024], F32))[:, :] for i in range(2)]
        mm = [ctx.enter_context(nc.psum_tensor(f"mm{i}", [128, 1024], F32))[:, :] for i in range(2)]
        bank = [mm[i // 2][:, 512 * (i % 2):512 * (i % 2) + 512] for i in range(4)]


        s_co = at("s_co", SCOLS, R[1] + 2048)
        s_mag, s_ang = at("s_mag", 288, R[1] + 3200), at("s_ang", 288, R[1] + 3488)
        s_in = at("s_in", 96, R[1] + 3776)
        s_sin, s_cos = at("s_sin", 288, o_ys), at("s_cos", 288, o_ys + 288)
        s_s = at("s_s", 352, o_ys + 576)
        p_co = at("p_co", SCOLS, R[2])
        p_w = [at(f"p_w{i}", GP * 128, R[2] + (1152, 2952)[i]) for i in range(2)]
        p_bc = [at(f"p_bc{i}", 320, R[2] + 1664 + 320 * i) for i in range(2)]
        p_ks, p_jr = at("p_ks", GP * 128, R[2] + 2304, rows=16), at("p_jr", 136, R[2] + 2816)
        p_tab = [at(f"p_tab{i}", GP * TTOP, (o_v, R[3])[i]) for i in range(2)]
        p_h0 = [at(f"p_h0{i}", GP * 144, (o_v + 2832, R[2] + 3464)[i]) for i in range(2)]
        p_t2, p_k = at("p_t2", GP * 144, R[3] + 2832), at("p_k", GP * NBT, R[3] + 3408)
        assert SCOLS <= 1152 and 3408 + GP * NBT <= 4096
        p_zero = at("p_zero", 112 * G5, R[0], rows=16)

        names = """c_in pos_in s_par s_pow s_sc s_made co_out co_in bc_in0 bc_in1 cp_out zeroed kd_zeroed p_ang p_h0 p_w p_tr p_ev p_k p_ke p_hc tab_out0 tab_out1 ks_out
            rope_ang rope_sc rope_st xT_hi xT_lo raw_in0 raw_in1 hi_done lo_done o_used g_done0 g_done1 g_free0
            g_free1 mem_in mem_hi mem_lo rope_in rope_done qk2_in r_sc r_att r_kn r_o r_ho r_u r_state hn_var hn_sd
            gate_used0 gate_used1 tr_done tr_free ys_out0 ys_out1 x_s x_max x_e x_norm x_t x_pt x_pv x_pvev xa_out wif_in
            wif_hi wif_lo bias_in if_done if_act rows_done res_in colt_done cols_done wqk_in conv_done xc_ready
            ones_done a_bc w_arg w_exp w_mask qk_mm qk_ev s_mm s_w k_tr k_w m_num m_read m_c m_st gn_in cw_in ud_out uu_in
            tb_in0 tb_in1 tb_in2 tb_in3 s_g s_gr s_z s_y s_ye yd_out yc_in gy_hi gy_lo s5_out0 s5_out1 y_in0 y_in1 oy_hi oy_lo o_done o_free
            xr_in0 xr_in1 ln_in ln_var ln_sd ln_y xs_out0 xs_out1 xn_in xt_done v_step a_step""".split()
        S = {n: ctx.enter_context(nc.semaphore(n)) for n in names}
        raw_in, g_done, g_free = [[S[f"{n}{i}"] for i in range(2)] for n in ("raw_in", "g_done", "g_free")]
        gate_used, ys_out = [[S[f"{n}{i}"] for i in range(2)] for n in ("gate_used", "ys_out")]
        s5_out, bc_in, tab_out, xs_out = [[S[f"{n}{i}"] for i in range(2)] for n in ("s5_out", "bc_in", "tab_out", "xs_out")]
        y_in, xr_in = [[S[f"{n}{i}"] for i in range(2)] for n in ("y_in", "xr_in")]
        tb_in = [S[f"tb_in{i}"] for i in range(SLOTS)]

        def half0(u):
            return 2 * u if u < U_GL else 2 * U_GL + (u - U_GL) if u < NUNIT else 2 * U_GL + 2 + 2 * (u - NUNIT)

        def nhalf(u):
            return 1 if U_GL <= u < NUNIT else 2

        def misc(i, n=1, rows=128):
            return cst[0:rows, K_MISC + i:K_MISC + i + n]

        ident = cst[:, K_ID:K_ID + 128]
        block = ctx.enter_context(nc.Block())

        @block.sync
        def _(sp):
            sp.dma_start(cst, dram["cst"]).then_inc(S["c_in"], 16)
            sp.dma_start(rot[:, 1024:2048].bitcast(I32), bass.AP(dram["pos"].tensor, 0, [[0, 128], [1, T]])).then_inc(S["pos_in"], 16)
            sp.dma_start(s_in, dram["s5a"][0]).then_inc(S["s_par"], 16)
            sp.dma_start(dram["xs"][0], dram["x"]).then_inc(S["cp_out"], 16)

            def raw(l, u):
                for i in range(nhalf(u)):
                    n = half0(u) + i
                    if n >= 2:
                        sp.wait_ge(S["hi_done"], l * HALVES + n - 1)
                        sp.wait_ge(S["lo_done"], l * HALVES + n - 1)
                    row = l * NSTORED + (u if u < NUNIT else NUNIT + (u - NUNIT) % 8)
                    sp.dma_start(wraw[n % 2], dram["w"][row, :, 1024 * i:1024 * i + 1024]).then_inc(raw_in[n % 2], 16)

            with sp.Fori(0, DEPTH) as l:
                sp.wait_ge(S["rope_st"], 32)
                sp.dma_start(memraw.rearrange("p (k m) -> p k m", k=KT), dram["memT"].rearrange("(k p) m -> p k m", p=128)).then_inc(S["mem_in"], 16)
                sp.wait_ge(S["cp_out"], 16)
                sp.wait_ge(S["zeroed"], 1)
                sp.wait_ge(S["kd_zeroed"], 16)
                for c in range(NC):
                    sp.dma_start(xn[c // 4][:, D * (c % 4):D * (c % 4) + D],
                                 dram["xs"][l, 128 * c:128 * c + 128, :]).then_inc(S["xn_in"], 16)
                sp.dma_start(rope, dram["ropetab"]).then_inc(S["rope_in"], 16)
                sp.dma_start(gn, bass.AP(dram["gn"].tensor, l * GW, [[0, 128], [1, GW]])).then_inc(S["gn_in"], 16)
                sp.dma_start(small[:, 32:48], dram["convw"][l]).then_inc(S["cw_in"], 16)
                sp.dma_start(small[0:4, 48:50], dram["bif"][l]).then_inc(S["bias_in"], 16)
                for u in range(U_QK + 4):
                    raw(l, u)
                sp.wait_ge(S["rope_done"], 2 * l + 2)
                for half in range(2):
                    for h in range(HEADS):
                        src = rot[32 * h:32 * h + 32, 2048 * half:2048 * half + 2048]
                        r0 = 64 * (h % 2) + 32 * half
                        sp.dma_start(qk2[r0:r0 + 32, 2048 * (h // 2):2048 * (h // 2) + 2048], src).then_inc(S["qk2_in"], 16)
                for u in range(U_QK + 4, U_MX + 1):
                    raw(l, u)
                sp.wait_ge(S["x_pvev"], 8 * l + 8)
                sp.dma_start(wifr, dram["wif"][l]).then_inc(S["wif_in"], 16)
                sp.wait_ge(gate_used[1], NGATE * l + 4)
                sp.dma_start(rres[0:4, :], dram["jcst"][0:4, J_RES:J_RES + T]).then_inc(S["res_in"], 16)
                for u in range(U_MX + 1, U_LO + 1):
                    raw(l, u)
                sp.wait_ge(S["rows_done"], l + 1)
                sp.dma_start(wqk, dram["wqk"][l]).then_inc(S["wqk_in"], 16)
                raw(l, U_LO + 1)
                sp.wait_ge(S["m_st"], NC * l + NC)
                sp.wait_ge(S["co_out"], 16 * l + 16)
                sp.dma_start(p_co, dram["s5co"]).then_inc(S["co_in"], 16)
                sp.dma_start(p_jr, dram["jcst"][:, 0:136]).then_inc(S["co_in"], 16)
                for u in range(U_LO + 1, NUNIT):
                    if u > U_LO + 1:
                        raw(l, u)
                    for q in ((0, 1) if u == U_LO + 1 else (u - U_LO - 1,)):
                        if u == U_LO + 1 or 2 <= q < NPB:
                            if q >= 2:
                                sp.wait_ge(S["p_ke"], NPB * l + q - 1)
                            sp.dma_start(p_bc[q % 2], dram["s5bc"][l * NPB + q]).then_inc(bc_in[q % 2], 16)
                sp.wait_ge(S["ud_out"], 64 * l + 64)
                for i in range(2):
                    sp.wait_ge(tab_out[i], 64 * l + 64)
                sp.wait_ge(S["ks_out"], 128 * l + 128)
                for s in range(BS):
                    src = dram["ud"].rearrange("(g c) (s j) -> s c g j", c=C5, s=BS)[BS - 1 - s]
                    sp.dma_start(uu[C5 * s:C5 * s + C5, :].rearrange("c (g j) -> c g j", g=G5), src).then_inc(S["uu_in"], 16)
                for b in range(NBATCH):
                    if b >= SLOTS:
                        sp.wait_ge(S["s_y"], NBATCH * l + b - SLOTS + 1)
                    t = tb[b % SLOTS].rearrange("p (g n) -> p g n", g=GB)
                    sp.dma_start(t[:, :, 0:TTOP], dram["tabs"][GB * b:GB * b + GB].rearrange("g p n -> p g n")).then_inc(tb_in[b % SLOTS], 16)
                    for g in range(GB):
                        src = bass.AP(dram["kd"].tensor, (b * GB + g) * C5 * 240, [[16, BS], [240, C5], [1, 128]])
                        sp.dma_start(t[:, g, TTOP:GCOLS], src).then_inc(tb_in[b % SLOTS], 16)
                sp.wait_ge(S["s_ye"], NBATCH * l + NBATCH)
                for t in range(BS):
                    dst = dram["yd"].rearrange("(g c) (t j) -> t c g j", c=C5, t=BS)[t]
                    sp.dma_start(dst, yb[C5 * t:C5 * t + C5, :].rearrange("c (g j) -> c g j", g=G5)).then_inc(S["yd_out"], 16)
                sp.wait_ge(S["yd_out"], 128 * l + 128)
                sp.dma_start(yc.rearrange("p (m t) -> p m t", m=4), dram["yd"].rearrange("(m p) t -> p m t", p=128)).then_inc(S["yc_in"], 16)
                raw(l, NUNIT)
                sp.wait_ge(s5_out[0], 32 * l + 32)
                sp.wait_ge(s5_out[1], 32 * l + 32)
                sp.wait_ge(S["xa_out"], 64 * l + 64)
                sp.wait_ge(ys_out[0], 128 * l + 128)
                sp.wait_ge(ys_out[1], 128 * l + 128)
                sp.dma_start(lng, bass.AP(dram["lng"].tensor, l * D, [[0, 128], [1, D]])).then_inc(S["ln_in"], 16)
                sp.dma_start(lnb, bass.AP(dram["lnb"].tensor, l * D, [[0, 128], [1, D]])).then_inc(S["ln_in"], 16)
                for j in range(NOUT):
                    if j % 2 == 0:
                        for i in range(2):
                            n = j + i
                            if n >= 2:
                                sp.wait_ge(S["oy_hi"], 16 * l + n - 1)
                                sp.wait_ge(S["oy_lo"], 16 * l + n - 1)
                            k0, t0 = (2 * n) % 16, 512 * (n // 8)
                            sp.dma_start(yraw[n % 2].rearrange("p (k t) -> p k t", k=2),
                                         dram["yt"][k0:k0 + 2, :, t0:t0 + 512].rearrange("k p t -> p k t")).then_inc(y_in[n % 2], 16)
                    if j:
                        raw(l, NUNIT + j)
                for i in range(2):
                    sp.wait_ge(xs_out[i], 64 * l + 64)
                sp.dma_start(s_in, dram["s5a"][l + 1]).then_inc(S["s_par"], 16)
            sp.wait_ge(S["s_par"], 16 * DEPTH + 16)

        @block.tensor
        def _(pe):
            def mm3(out, ah, al, bh, bl, start, stop):
                nc.tensor.matmul(out, ah, bh, start=start, stop=False)
                nc.tensor.matmul(out, ah, bl, start=False, stop=False)
                return nc.tensor.matmul(out, al, bh, start=False, stop=stop)

            pe.wait_ge(S["c_in"], 16)

            def tables(l, q):
                n = NPB * l + q
                pe.wait_ge(S["p_w"], n + 1)
                if q:
                    pe.wait_ge(S["p_ev"], n)
                for g in range(GP):
                    last = nc.tensor.transpose(bank[2][:, 128 * g:128 * g + 128], p_w[q % 2][:, 128 * g:128 * g + 128], ident)
                last.then_inc(S["p_tr"], 1)
                pe.wait_ge(S["p_h0"], n + 1)
                if q:
                    pe.wait_ge(S["p_ke"], n)
                for g in range(GP):
                    last = nc.tensor.matmul(bank[3][0:16, 128 * g:128 * g + 128], p_w[q % 2][:, 128 * g:128 * g + C5],
                                            p_h0[q % 2][:, 144 * g:144 * g + 128], start=True, stop=True)
                last.then_inc(S["p_k"], 1)

            def unit(l, u):
                kind = "MC" if u < U_MV else "MT" if u < U_QK else "C" if u in CUNITS else "G" if u >= U_GL else "T"
                wh, wl = whi[u % 2], wlo[u % 2]
                pe.wait_ge(S["lo_done"], l * HALVES + half0(u) + nhalf(u))
                for g in range(2):
                    if u:
                        pe.wait_ge(g_free[g], NUNIT * l + u)
                    if kind in ("C", "G"):
                        kt, rh, rl = (KT, xh, xl) if kind == "C" else (4, yh, yl)
                        for n in range(2):
                            for k in range(kt):
                                w0, x0 = 256 * k + 128 * g, T * k + 512 * n
                                last = mm3(gp[g][:, 512 * n:512 * n + 512], wh[:, w0:w0 + 128], wl[:, w0:w0 + 128],
                                           rh[:, x0:x0 + 512], rl[:, x0:x0 + 512], k == 0, k == kt - 1)
                    elif kind == "MC":
                        for k in range(KT):
                            w0 = 256 * k + 128 * g
                            last = mm3(gp[g][:, 0:256], wh[:, w0:w0 + 128], wl[:, w0:w0 + 128],
                                       memh[:, NMEM * k:NMEM * k + NMEM], meml[:, NMEM * k:NMEM * k + NMEM], k == 0, k == KT - 1)
                    else:
                        for c in range(1 if kind == "MT" else 4):
                            for k in range(KT):
                                if kind == "MT":
                                    ah, al, a0 = memh, meml, NMEM * k + 128 * g
                                else:
                                    ah, al, a0 = xh, xl, T * k + 128 * (4 * g + c)
                                last = mm3(gp[g][:, 256 * c:256 * c + 256], ah[:, a0:a0 + 128], al[:, a0:a0 + 128],
                                           wh[:, 256 * k:256 * k + 256], wl[:, 256 * k:256 * k + 256], k == 0, k == KT - 1)
                    last.then_inc(g_done[g], 1)

            def transposes(l, first, src, used):
                for g in range(2):
                    pe.wait_ge(gate_used[g], NGATE * l + used)
                for i in range(8):
                    j, half, n = i // 2, i % 2, first + i
                    if n >= 2:
                        pe.wait_ge(S["tr_free"], 16 * l + n - 1)
                    for c in range(4):
                        a0 = GW * (4 * half + c) + 128 * j
                        last = nc.tensor.transpose(bank[i % 2][:, 128 * c:128 * c + 128], src[:, a0:a0 + 128], ident)
                    last.then_inc(S["tr_done"], 1)

            with pe.Fori(0, DEPTH) as l:
                pe.wait_ge(S["mem_lo"], l + 1)
                for u in range(U_MK, U_QK):
                    unit(l, u)
                pe.wait_ge(S["xn_in"], 16 * NC * (l + 1))
                for i in range(16):
                    half, k = i // 8, i % 8
                    if i >= 4:
                        pe.wait_ge(S["xT_hi"], 16 * l + i - 3)
                        pe.wait_ge(S["xT_lo"], 16 * l + i - 3)
                    for c in range(4):
                        last = nc.tensor.transpose(bank[i % 4][:, 128 * c:128 * c + 128], xn[half][:, D * c + 128 * k:D * c + 128 * k + 128],
                                                   ident)
                    last.then_inc(S["xt_done"], 1)
                pe.wait_ge(S["xT_hi"], 16 * l + 16)
                pe.wait_ge(S["xT_lo"], 16 * l + 16)
                for u in range(U_QK, U_RZ):
                    unit(l, u)

                pe.wait_ge(S["qk2_in"], 128 * l + 128)
                v = rv

                def r_scores(c):
                    if c:
                        pe.wait_ge(S["r_att"], NC * l + c)
                        pe.wait_ge(S["r_kn"], NC * l + c)
                    for h in range(HEADS):
                        p, r0 = h // 2, 64 * (h % 2)
                        nc.tensor.matmul(bank[h % 2][:, 128 * p:128 * p + 128],
                                         qk2[r0:r0 + 64, 2048 * p + T + 128 * c:2048 * p + T + 128 * c + 128],
                                         qk2[r0:r0 + 64, 2048 * p + 128 * c:2048 * p + 128 * c + 128], start=True, stop=True)
                    for p in range(2):
                        last = nc.tensor.transpose(bank[1][:, 256 + 128 * p:256 + 128 * p + 128],
                                                   qk2[:, 2048 * p + T + 128 * c:2048 * p + T + 128 * c + 128], ident)
                    last.then_inc(S["r_sc"], 1)

                r_scores(0)
                for c in range(NC):
                    if c + 1 < NC:
                        r_scores(c + 1)
                    pe.wait_ge(S["r_att"], NC * l + c + 1)
                    if c:
                        pe.wait_ge(S["r_ho"], NC * l + c)
                        pe.wait_ge(S["r_state"], NC * l + c)
                    for h in range(HEADS):
                        p, r0 = h // 2, 64 * (h % 2)
                        o = bank[2][:, 128 * h:128 * h + 128]
                        last = nc.tensor.matmul(o, att[c % 2][:, 256 * (h % 2) + 128 * p:256 * (h % 2) + 128 * p + 128], v[:, GW * c + 128 * h:GW * c + 128 * h + 128],
                                                start=True, stop=c == 0)
                        if c:
                            last = nc.tensor.matmul(o, qk2[:, 2048 * p + 128 * c:2048 * p + 128 * c + 128],
                                                    sret[:, 128 * h:128 * h + 128], start=False, stop=True)
                    last.then_inc(S["r_o"], 1)
                    pe.wait_ge(S["r_kn"], NC * l + c + 1)
                    if c:
                        pe.wait_ge(S["r_state"], NC * l + c)
                    for h in range(HEADS):
                        p, r0 = h // 2, 64 * (h % 2)
                        last = nc.tensor.matmul(bank[3][r0:r0 + 64, 128 * p:128 * p + 128], kn[c % 2][:, DK * h:DK * h + DK],
                                                v[:, GW * c + 128 * h:GW * c + 128 * h + 128], start=True, stop=True)
                    last.then_inc(S["r_u"], 1)
                unit(l, U_RZ)
                unit(l, U_RZ + 1)

                def x_scores(i):
                    h, half = i // 2, i % 2
                    if i:
                        pe.wait_ge(S["x_e"], 4 * (8 * l + i))
                    for c in range(4):
                        a0 = T * h + 512 * half + 128 * c
                        last = nc.tensor.matmul(mm[0][:, 256 * c:256 * c + 256], aq[:, a0:a0 + 128], mkT[:, NMEM * h:NMEM * h + NMEM],
                                                start=True, stop=True)
                    last.then_inc(S["x_s"], 1)

                pe.wait_ge(S["r_ho"], NC * l + NC)
                pe.wait_ge(S["r_state"], NC * l + NC)
                x_scores(0)
                for i in range(8):
                    h, half = i // 2, i % 2
                    if i < 7:
                        x_scores(i + 1)
                    pe.wait_ge(S["x_norm"], 8 * l + i + 1)
                    if i:
                        pe.wait_ge(S["x_pvev"], 8 * l + i)
                    for m in range(2):
                        for c in range(4):
                            last = nc.tensor.transpose(mm[1][:, 512 * m + 128 * c:512 * m + 128 * c + 128],
                                                       pm[:, 256 * c + 128 * m:256 * c + 128 * m + 128], ident)
                    last.then_inc(S["x_t"], 1)
                    pe.wait_ge(S["x_pt"], 8 * l + i + 1)
                    for m in range(2):
                        last = nc.tensor.matmul(mm[1][:, 0:512], mvT[:, GW * m + 128 * h:GW * m + 128 * h + 128], pt[:, 512 * m:512 * m + 512],
                                                start=m == 0, stop=m == 1)
                    last.then_inc(S["x_pv"], 1)
                unit(l, U_AZ)
                unit(l, U_AZ + 1)
                transposes(l, 0, hr, 2)

                pe.wait_ge(S["wif_hi"], l + 1)
                pe.wait_ge(S["wif_lo"], l + 1)
                pe.wait_ge(S["tr_free"], 16 * l + 8)
                for n in range(2):
                    for k in range(KT):
                        last = mm3(mm[1][:, 512 * n:512 * n + 512], wifh[:, 128 * k:128 * k + 128], wifl[:, 128 * k:128 * k + 128],
                                   xh[:, T * k + 512 * n:T * k + 512 * n + 512], xl[:, T * k + 512 * n:T * k + 512 * n + 512],
                                   k == 0, k == KT - 1)
                last.then_inc(S["if_done"], 1)
                for u in range(U_MX, U_LO):
                    unit(l, u)
                pe.wait_ge(S["rows_done"], l + 1)
                for c in range(NC):
                    last = nc.tensor.transpose(mm[0][:, 128 * c:128 * c + 128], rk[:, 128 * c:128 * c + 128], ident)
                last.then_inc(S["colt_done"], 1)
                for h in range(HEADS):
                    last = nc.tensor.matmul(bank[2][:, NC * h:NC * h + NC], cst[0:4, K_ONE + 128 * h:K_ONE + 128 * h + 128],
                                            small[0:4, 16:24], start=True, stop=True)
                last.then_inc(S["colt_done"], 1)
                pe.wait_ge(S["cols_done"], 5 * l + 5)
                for i in range(8):
                    h, half = i // 2, i % 2
                    if i >= 2:
                        pe.wait_ge(S["w_arg"], 8 * l + i - 1)
                    nc.tensor.matmul(bank[i % 2], cst[0:4, K_ONE + 128 * h:K_ONE + 128 * h + 128],
                                     rowf[0:4, 512 * half:512 * half + 512], start=True, stop=True).then_inc(S["a_bc"], 1)
                pe.wait_ge(S["wqk_in"], 16 * l + 16)
                for i in range(16):
                    w, h, half = i // 8, i // 2 % 4, i % 2
                    pe.wait_ge(S["xc_ready"], 4 * l + h + 1)
                    if i >= 2:
                        pe.wait_ge(S["qk_ev"], 16 * l + i - 1)
                    nc.tensor.matmul(bank[2 + i % 2], wqk[:, 512 * w + 128 * h:512 * w + 128 * h + 128],
                                     xc[:, T * h + 512 * half:T * h + 512 * half + 512], start=True, stop=True).then_inc(S["qk_mm"], 1)
                pe.wait_ge(S["qk_ev"], 16 * l + 16)
                pe.wait_ge(S["w_arg"], 8 * l + 8)
                for c in range(NC):
                    if c >= 2:
                        pe.wait_ge(S["s_w"], NC * l + c - 1)
                    for h in range(HEADS):
                        a0 = 512 * c + 128 * h
                        last = nc.tensor.matmul(bank[c % 2][:, 128 * h:128 * h + 128], kTt[:, a0:a0 + 128], qT[:, a0:a0 + 128],
                                                start=True, stop=True)
                    last.then_inc(S["s_mm"], 1)
                pe.wait_ge(S["ones_done"], l + 1)
                pe.wait_ge(g_free[0], NUNIT * l + U_LO)
                pe.wait_ge(g_free[1], NUNIT * l + U_LO)
                pe.wait_ge(S["s_w"], NC * l + NC)

                def k_natural(c):
                    if c:
                        pe.wait_ge(S["k_w"], NC * l + c)
                    for h in range(HEADS):
                        last = nc.tensor.transpose(bank[3][:, 128 * h:128 * h + 128], kTt[:, 512 * c + 128 * h:512 * c + 128 * h + 128], ident)
                    last.then_inc(S["k_tr"], 1)

                k_natural(0)
                for c in range(NC):
                    if c + 1 < NC:
                        k_natural(c + 1)
                    if c:
                        pe.wait_ge(S["m_read"], NC * l + c)
                    for h in range(HEADS):
                        a0, o0, v0 = 512 * c + 128 * h, 512 * (h // 2) + 129 * (h % 2), 129 * (HEADS * c + h)
                        last = nc.tensor.matmul(gp[0][:, o0:o0 + 129], wt[:, a0:a0 + 128], va[:, v0:v0 + 129], start=True, stop=True)
                    if c:
                        pe.wait_ge(S["m_st"], NC * l + c)
                        for h in range(HEADS):
                            a0, o0 = 512 * c + 128 * h, 512 * (h // 2) + 129 * (h % 2)
                            last = nc.tensor.matmul(gp[1][:, o0:o0 + 129], qT[:, a0:a0 + 128], cst8[:, 129 * h:129 * h + 129],
                                                    start=True, stop=True)
                    last.then_inc(S["m_num"], 1)
                    pe.wait_ge(S["k_w"], NC * l + c + 1)
                    if c:
                        pe.wait_ge(S["m_st"], NC * l + c)
                    for h in range(HEADS):
                        o0, v0 = 512 * (h // 2) + 129 * (h % 2), 129 * (HEADS * c + h)
                        last = nc.tensor.matmul(mm[0][:, o0:o0 + 129], kw[c % 2][:, 128 * h:128 * h + 128], va[:, v0:v0 + 129],
                                                start=True, stop=True)
                    last.then_inc(S["m_c"], 1)
                pe.wait_ge(S["m_read"], NC * l + NC)
                pe.wait_ge(S["m_st"], NC * l + NC)
                for u in range(U_LO, U_SZ + 2):
                    unit(l, u)
                    for q in TABLES_AT.get(u - 1, ()):
                        tables(l, q)
                    if u == U_SU + 1:
                        transposes(l, 8, hm, 8)

                pe.wait_ge(S["uu_in"], 128 * l + 128)
                pe.wait_ge(S["tr_free"], 16 * l + 16)

                def s_inputs(b):
                    pe.wait_ge(tb_in[b % SLOTS], 48 * ((NBATCH // SLOTS) * l + b // SLOTS) + 48)
                    if b:
                        pe.wait_ge(S["s_gr"], NBATCH * l + b)
                    for g in range(GB):
                        for w in range(2):
                            a0 = GCOLS * g + TG + 64 * w
                            last = nc.tensor.matmul(bank[w][:, 128 * g:128 * g + 128], tb[b % SLOTS][:, a0:a0 + 128],
                                                    uu[:, 128 * (GB * b + g):128 * (GB * b + g) + 128], start=True, stop=True)
                    last.then_inc(S["s_g"], 1)

                s_inputs(0)
                for b in range(NBATCH):
                    if b + 1 < NBATCH:
                        s_inputs(b + 1)
                    pe.wait_ge(S["s_z"], NBATCH * l + b + 1)
                    if b >= 2:
                        pe.wait_ge(S["s_ye"], NBATCH * l + b - 1)
                    for g in range(GB):
                        t = tb[b % SLOTS][:, GCOLS * g:GCOLS * g + GCOLS]
                        o = bank[2 + b % 2][:, 128 * g:128 * g + 128]
                        nc.tensor.matmul(o, t[:, TTOP:TTOP + 128],
                                         uu[:, 128 * (GB * b + g):128 * (GB * b + g) + 128], start=True, stop=False)
                        nc.tensor.matmul(o, t[:, TH:TH + 128], zc[b % 2][:, 128 * g:128 * g + 128], start=False, stop=False)
                        last = nc.tensor.matmul(o, t[:, TH2:TH2 + 128], zs[b % 2][:, 128 * g:128 * g + 128],
                                                start=False, stop=True)
                    last.then_inc(S["s_y"], 1)
                pe.wait_ge(S["gy_hi"], 4 * l + 4)
                pe.wait_ge(S["gy_lo"], 4 * l + 4)
                unit(l, U_GL)
                unit(l, U_GL + 1)

                op = gp + mm
                pe.wait_ge(g_free[0], NUNIT * l + NUNIT)
                pe.wait_ge(g_free[1], NUNIT * l + NUNIT)
                pe.wait_ge(S["s_ye"], NBATCH * l + NBATCH)
                for j in range(NOUT):
                    hf, kq, n = j // 8, j % 8 // 2, j % 2
                    u = NUNIT + j
                    pe.wait_ge(S["lo_done"], l * HALVES + half0(u) + 2)
                    pe.wait_ge(S["oy_hi"], 16 * l + 8 * hf + 2 * kq + 2)
                    pe.wait_ge(S["oy_lo"], 16 * l + 8 * hf + 2 * kq + 2)
                    for cc in range(4):
                        if hf and kq == 0 and n == 0:
                            pe.wait_ge(S["o_free"], NC * l + cc + 1)
                        for k in range(4):
                            y0, w0 = 512 * (4 * kq + k) + 128 * cc, 512 * k
                            last = mm3(op[cc][:, 512 * n:512 * n + 512], oyh[:, y0:y0 + 128], oyl[:, y0:y0 + 128],
                                       whi[u % 2][:, w0:w0 + 512], wlo[u % 2][:, w0:w0 + 512], kq == 0 and k == 0, kq == 3 and k == 3)
                        if kq == 3 and n == 1 and cc < 3:
                            last.then_inc(S["o_done"], 1)
                    last.then_inc(S["o_used"], 1)
                pe.wait_ge(S["o_free"], NC * (l + 1))

        @block.gpsimd
        def _(pool):
            def lo(l, u):
                for i in range(nhalf(u)):
                    n = half0(u) + i
                    pool.wait_ge(S["hi_done"], l * HALVES + n + 1)
                    nc.gpsimd.tensor_tensor(wlo[u % 2][:, 1024 * i:1024 * i + 1024], wraw[n % 2],
                                            whi[u % 2][:, 1024 * i:1024 * i + 1024].bitcast(F32), ALU.subtract).then_inc(S["lo_done"], 1)

            nc.gpsimd.memset(p_zero[:, 0:112 * G5], 0.0).then_inc(S["zeroed"], 1)
            pool.wait_ge(S["zeroed"], 1)
            pool.dma_start(bass.AP(dram["kd"].tensor, 0, [[240, C5], [C5 * 240, G5], [1, 112]]),
                           p_zero[:, 0:112 * G5].rearrange("c (g z) -> c g z", z=112)).then_inc(S["kd_zeroed"], 16)
            pool.wait_ge(S["kd_zeroed"], 16)
            with pool.Fori(0, DEPTH) as l:
                for u in range(U_LO + 1):
                    lo(l, u)
                for c in range(NC):
                    pool.wait_ge(S["w_exp"], NC * l + c + 1)
                    w = wt[:, 512 * c:512 * c + 512].rearrange("p (h t) -> p h t", h=HEADS)
                    nc.gpsimd.tensor_tensor(w, w, bcast(cst[:, K_CAUS:K_CAUS + 128], HEADS, 0), ALU.mult).then_inc(S["w_mask"], 1)
                for u in range(U_LO + 1, NUNIT + NOUT):
                    lo(l, u)

        @block.scalar
        def _(act):
            A = Steps(act, S["a_step"], steps_a)
            A.layer, A.base = 0, 0
            F = nc.scalar.activation

            act.wait_ge(S["c_in"], 16)
            act.wait_ge(S["rope_ang"], 1)
            A.link(F(rot[:, 2048:3072], rot[:, 0:1024], ACT.Abs))
            A.link(F(rot[:, 3072:4096], rot[:, 2048:3072], ACT.Sin, scale=-1.0, bias=misc(M_HPI)))
            F(rot[:, 1024:2048], rot[:, 0:1024], ACT.Sin).then_inc(S["rope_sc"], 1)
            act.wait_ge(S["rope_sc"], 1)
            act.dma_start(dram["ropetab"][:, 0:1024], rot[:, 3072:4096]).then_inc(S["rope_st"], 16)
            act.dma_start(dram["ropetab"][:, 1024:2048], rot[:, 1024:2048]).then_inc(S["rope_st"], 16)
            A.base = A.n

            def tables(l, q):
                n = NPB * l + q
                tab = p_tab[q % 2].rearrange("p (g n) -> p g n", g=GP)
                co, si = tab[:, :, TCOS:TCOS + NBT], tab[:, :, TSIN:TSIN + NBT]
                act.wait_ge(S["p_ang"], n + 1)
                A.link(F(co, si, ACT.Abs))
                A.inc(F(co, co, ACT.Sin, scale=-TURN, bias=misc(M_HPI)))
                A.inc(F(si, si, ACT.Sin, scale=misc(M_TURN)))
                act.wait_ge(S["p_h0"], n + 1)
                F(tab[:, :, TH:TH + 128], p_h0[q % 2].rearrange("p (g n) -> p g n", g=GP)[:, :, C5:144], ACT.Copy).then_inc(S["p_hc"], 1)
                act.wait_ge(S["p_tr"], n + 1)
                bk = bank[2].rearrange("p (g n) -> p g n", g=GP)
                A.inc(F(tab[:, :, TG:TG + 128], bk, ACT.Copy))
                F(tab[:, :, TG + 128:TG + 192], bk[:, :, 0:64], ACT.Copy).then_inc(S["p_ev"], 1)
                A.join()
                act.wait_ge(S["p_ev"], n + 1)
                act.wait_ge(S["p_hc"], n + 1)
                act.wait_ge(S["p_ke"], n + 1)
                act.dma_start(dram["tabs"][GP * q:GP * q + GP].rearrange("g p n -> p g n"), tab).then_inc(tab_out[q % 2], 16)
                act.dma_start(dram["kd"].rearrange("g c n -> c g n")[:, GP * q:GP * q + GP, 112:240],
                              p_ks.rearrange("c (g n) -> c g n", g=GP)).then_inc(S["ks_out"], 16)

            def split(l, u):
                if 2 <= u < NUNIT + 2:
                    act.wait_ge(g_done[1], NUNIT * l + u - 1)
                elif u >= 2:
                    act.wait_ge(S["o_used"], NOUT * l + u - 2 - NUNIT + 1)
                for i in range(nhalf(u)):
                    n = half0(u) + i
                    act.wait_ge(raw_in[n % 2], 16 * ((HALVES // 2) * l + n // 2 + 1))
                    F(whi[u % 2][:, 1024 * i:1024 * i + 1024], wraw[n % 2], ACT.Copy).then_inc(S["hi_done"], 1)

            def take_out(l, u, fn):
                split(l, u + 1)
                for g in range(2):
                    act.wait_ge(g_done[g], NUNIT * l + u + 1)
                    fn(u, g).then_inc(g_free[g], 1)

            def gates(l, u, n, func, scale=1.0):
                split(l, u + 1)
                for g in range(2):
                    act.wait_ge(g_done[g], NUNIT * l + u + 1)
                    if n:
                        act.wait_ge(gate_used[g], NGATE * l + n)
                    F(gate[g], gp[g], func, scale=scale).then_inc(g_free[g], 1)

            def store_tiles(l, first, tile0):
                for i in range(8):
                    j, half, n = i // 2, i % 2, first + i
                    act.wait_ge(S["tr_done"], 16 * l + n + 1)
                    if n >= 2:
                        act.wait_ge(ys_out[i % 2], 16 * (8 * l + n // 2))
                    F(ystage[i % 2], bank[i % 2], ACT.Copy).then_inc(S["tr_free"], 1)
                    act.wait_ge(S["tr_free"], 16 * l + n + 1)
                    act.dma_start(dram["yt"][tile0 + j, :, 512 * half:512 * half + 512], ystage[i % 2]).then_inc(ys_out[i % 2], 16)

            with act.Fori(0, DEPTH) as l:
                A.begin(l)
                act.wait_ge(S["mem_in"], 16 * l + 16)
                F(memh, memraw, ACT.Copy).then_inc(S["mem_hi"], 1)
                split(l, 0)
                for u in (U_MK, U_MK + 1):
                    take_out(l, u, lambda u, g: F(mkT[:, NMEM * (2 * (u - U_MK) + g):NMEM * (2 * (u - U_MK) + g) + NMEM],
                                                  gp[g][:, 0:NMEM], ACT.Copy))
                for u in (U_MV, U_MV + 1):
                    take_out(l, u, lambda u, g: F(mvT[:, GW * g + 256 * (u - U_MV):GW * g + 256 * (u - U_MV) + 256],
                                                  gp[g][:, 0:256], ACT.Copy))
                for i in range(16):
                    half, k = i // 8, i % 8
                    act.wait_ge(S["xt_done"], 16 * l + i + 1)
                    F(xh[:, T * k + 512 * half:T * k + 512 * half + 512], bank[i % 4], ACT.Copy).then_inc(S["xT_hi"], 1)
                for u in (U_QK, U_QK + 1):
                    take_out(l, u, lambda u, g: F(qk[:, T * (2 * (u - U_QK) + g):T * (2 * (u - U_QK) + g) + T], gp[g], ACT.Copy))
                act.wait_ge(S["s_pow"], l + 1)
                A.link(F(s_cos, s_ang, ACT.Abs))
                A.link(F(s_cos, s_cos, ACT.Sin, scale=-1.0, bias=misc(M_HPI)))
                F(s_sin, s_ang, ACT.Sin).then_inc(S["s_sc"], 1)
                for u in (U_RV, U_RV + 1):
                    take_out(l, u, lambda u, g: F(tview(rv, GW, g, u - U_RV), gp[g].rearrange("p (c n) -> p c n", c=4), ACT.Copy))
                for u in (U_AQ, U_AQ + 1):
                    take_out(l, u, lambda u, g: F(aq[:, T * (2 * (u - U_AQ) + g):T * (2 * (u - U_AQ) + g) + T], gp[g], ACT.Copy))
                act.wait_ge(S["s_made"], l + 1)
                act.dma_start(dram["s5co"], s_co).then_inc(S["co_out"], 16)
                act.wait_ge(S["hn_var"], 2 * l + 1)
                F(sd[:, 0:32], mv.rearrange("p (n k) -> p n k", k=2)[:, :, 1], ACT.Sqrt, bias=misc(M_GNE)).then_inc(S["hn_sd"], 1)
                gates(l, U_RZ, 0, ACT.Silu)
                gates(l, U_RZ + 1, 1, ACT.Silu)
                for i in range(8):
                    h, half = i // 2, i % 2
                    act.wait_ge(S["x_max"], 8 * l + i + 1)
                    if i:
                        act.wait_ge(S["x_t"], 8 * l + i)
                    for c in range(4):
                        F(pm[:, 256 * c:256 * c + 256], mm[0][:, 256 * c:256 * c + 256], ACT.Exp, scale=128 ** -0.5,
                          bias=small[:, 4 + c:5 + c], accum_out=small[:, 8 + c:9 + c]).then_inc(S["x_e"], 1)
                    act.wait_ge(S["x_t"], 8 * l + i + 1)
                    if i:
                        act.wait_ge(S["x_pv"], 8 * l + i)
                    F(pt, mm[1], ACT.Copy).then_inc(S["x_pt"], 1)
                    act.wait_ge(S["x_pv"], 8 * l + i + 1)
                    F(xo[:, T * h + 512 * half:T * h + 512 * half + 512], mm[1][:, 0:512], ACT.Copy).then_inc(S["x_pvev"], 1)
                gates(l, U_AZ, 2, ACT.Silu)
                gates(l, U_AZ + 1, 3, ACT.Silu)
                for j in range(4):
                    act.wait_ge(gate_used[j % 2], NGATE * l + 3 + j // 2)
                    act.dma_start(dram["yt"][12 + j], xo[:, T * j:T * j + T]).then_inc(S["xa_out"], 16)
                store_tiles(l, 0, 0)
                act.wait_ge(S["wif_in"], 16 * l + 16)
                F(wifh, wifr, ACT.Copy).then_inc(S["wif_hi"], 1)
                act.wait_ge(S["if_done"], l + 1)
                act.wait_ge(S["bias_in"], 16 * l + 16)
                F(rowi[0:4, :], mm[1][0:4, :], ACT.Identity, bias=small[0:4, 48:49]).then_inc(S["if_act"], 1)
                A.link(F(rowb[0:4, :], mm[1][32:36, :], ACT.Identity, bias=small[0:4, 49:50]))
                A.link(F(rowm[0:4, :], rowb[0:4, :], ACT.Abs))
                A.link(F(rowm[0:4, :], rowm[0:4, :], ACT.Exp, scale=-1.0))
                F(rowm[0:4, :], rowm[0:4, :], ACT.Ln, bias=misc(M_ONE, 1, 4)).then_inc(S["if_act"], 1)
                for u in (U_MX, U_MX + 1):
                    take_out(l, u, lambda u, g: F(mx[:, (T + 3) * (2 * (u - U_MX) + g) + 3:(T + 3) * (2 * (u - U_MX) + g) + 3 + T], gp[g], ACT.Copy))
                for h in range(HEADS):
                    act.wait_ge(S["conv_done"], 4 * l + h + 1)
                    F(xc[:, T * h:T * h + T], xc[:, T * h:T * h + T], ACT.Silu).then_inc(S["xc_ready"], 1)
                vview = va.rearrange("p (c h e) -> p c h e", c=NC, h=HEADS)
                for u in (U_LV, U_LV + 1):
                    h0 = 2 * (u - U_LV)
                    take_out(l, u, lambda u, g: F(vview[:, 4 * g:4 * g + 4, h0:h0 + 2, 0:128],
                                                  gp[g].rearrange("p (c h e) -> p c h e", c=4, h=2), ACT.Copy))
                act.wait_ge(S["colt_done"], 2 * l + 2)
                src = mm[0].rearrange("p (c x) -> p c x", c=NC)
                for k in range(4):
                    F(cols[:, 32 * k:32 * k + 32].rearrange("p (c h) -> p c h", c=NC), src[:, :, 32 * k:32 * k + 4],
                      ACT.Exp if k else ACT.Copy).then_inc(S["cols_done"], 1)
                F(dec, bank[2][:, 0:32], ACT.Exp).then_inc(S["cols_done"], 1)
                for c in range(NC):
                    act.wait_ge(S["w_arg"], 8 * l + 8)
                    F(wt[:, 512 * c:512 * c + 512], wt[:, 512 * c:512 * c + 512], ACT.Exp).then_inc(S["w_exp"], 1)
                for i in range(16):
                    w, h, half = i // 8, i // 2 % 4, i % 2
                    act.wait_ge(S["qk_mm"], 16 * l + i + 1)
                    dst = (kTt if w else qT).rearrange("p (c h t) -> p c h t", c=NC, h=HEADS)[:, 4 * half:4 * half + 4, h, :]
                    F(dst, bank[2 + i % 2].rearrange("p (c t) -> p c t", c=4), ACT.Copy, scale=128 ** -0.5 if w else 1.0).then_inc(S["qk_ev"], 1)
                gates(l, U_LO, 4, ACT.Tanh, 0.5)
                gates(l, U_LO + 1, 5, ACT.Tanh, 0.5)
                tables(l, 0)
                act.wait_ge(S["hn_var"], 2 * l + 2)
                F(sd[:, 0:32], mv.rearrange("p (n k) -> p n k", k=2)[:, :, 1], ACT.Sqrt, bias=misc(M_GNE)).then_inc(S["hn_sd"], 1)
                gates(l, U_LZ, 6, ACT.Silu)
                gates(l, U_LZ + 1, 7, ACT.Silu)
                tables(l, 1)
                for u in (U_SU, U_SU + 1):
                    take_out(l, u, lambda u, g: F(us[:, T * (2 * (u - U_SU) + g):T * (2 * (u - U_SU) + g) + T].rearrange("p (s j) -> p j s", s=BS),
                                                  gp[g].rearrange("p (j s) -> p j s", s=BS), ACT.Copy))
                    for q in TABLES_AT[u - 1]:
                        tables(l, q)
                for m in range(4):
                    act.wait_ge(g_free[m % 2], NUNIT * l + U_SU + m // 2 + 1)
                    act.dma_start(dram["ud"][128 * m:128 * m + 128, :], us[:, T * m:T * m + T]).then_inc(S["ud_out"], 16)
                store_tiles(l, 8, 8)
                for u in (U_SZ, U_SZ + 1):
                    take_out(l, u, lambda u, g: F(sz[:, T * (2 * (u - U_SZ) + g):T * (2 * (u - U_SZ) + g) + T].rearrange("p (s j) -> p j s", s=BS),
                                                  gp[g].rearrange("p (j s) -> p j s", s=BS), ACT.Silu))
                    for q in TABLES_AT.get(u - 1, ()):
                        tables(l, q)
                for b in range(NBATCH):
                    act.wait_ge(S["s_y"], NBATCH * l + b + 1)
                    F(yb[:, 256 * b:256 * b + 256], bank[2 + b % 2][:, 0:256], ACT.Copy).then_inc(S["s_ye"], 1)
                act.wait_ge(S["yc_in"], 16 * l + 16)
                for m in range(4):
                    A.link(F(yc[:, T * m:T * m + T], yc[:, T * m:T * m + T], ACT.Gelu_apprx_tanh))
                    F(yh[:, T * m:T * m + T], yc[:, T * m:T * m + T], ACT.Copy).then_inc(S["gy_hi"], 1)
                gates(l, U_GL, 8, ACT.Tanh, 0.5)
                gates(l, U_GL + 1, 9, ACT.Tanh, 0.5)
                for m in range(4):
                    act.wait_ge(gate_used[m % 2], NGATE * l + 9 + m // 2)
                    act.dma_start(dram["yt"][4 + m], s5o[m % 2]).then_inc(s5_out[m % 2], 16)

                def yhi(n):
                    kq = n % 8 // 2
                    act.wait_ge(y_in[n % 2], 16 * (8 * l + n // 2 + 1))
                    if n >= 8:
                        act.wait_ge(S["o_used"], NOUT * l + 2 * kq + 2)
                    F(oyh[:, 1024 * (n % 8):1024 * (n % 8) + 1024], yraw[n % 2], ACT.Copy).then_inc(S["oy_hi"], 1)

                def norm(c):
                    act.wait_ge(S["ln_var"], NC * l + c + 1)
                    F(sd[:, 32:33], mv[:, 33:34], ACT.Sqrt, bias=misc(M_LNE)).then_inc(S["ln_sd"], 1)
                    act.wait_ge(S["ln_y"], NC * l + c + 1)
                    act.dma_start(dram["xs"][l + 1, 128 * c:128 * c + 128, :], rr[c % 2]).then_inc(xs_out[c % 2], 16)
                    if c + 2 < NC:
                        xload(c + 2)

                def xload(c):
                    act.dma_start(xr[c % 2], dram["xs"][l, 128 * c:128 * c + 128, :]).then_inc(xr_in[c % 2], 16)

                act.wait_ge(S["cp_out"], 16)
                xload(0)
                xload(1)
                for j in range(NOUT):
                    if j % 2 == 0:
                        yhi(j)
                        yhi(j + 1)
                    if j + 1 < NOUT:
                        split(l, NUNIT + j + 1)
                    if j == 8:
                        for c in range(4):
                            norm(c)
                for c in range(4, NC):
                    norm(c)
            assert A.n == steps_a, A.n

        @block.vector
        def _(dve):
            V = Steps(dve, S["v_step"], steps_v)
            V.layer = 0
            TT, TS, STT = nc.vector.tensor_tensor, nc.vector.tensor_scalar, nc.vector.scalar_tensor_tensor

            def reduce_angle(link, x, k):
                link(TS(k, x, 1.0 / TWO_PI, MAGIC, ALU.mult, ALU.add))
                link(TS(k, k, MAGIC, None, ALU.subtract))
                for part in (C1, C2, C3):
                    link(STT(x, k, -part, x, ALU.mult, ALU.add))
                return TS(x, x, PI_LO, -PI_LO, ALU.min, ALU.max)

            def exp_(x, out, t):
                V.link(TS(x, x, -200.0, 200.0, ALU.max, ALU.min))
                V.link(TS(t, x, 1.0 / math.log(2.0), MAGIC, ALU.mult, ALU.add))
                V.link(TS(t, t, MAGIC, None, ALU.subtract))
                V.link(STT(x, t, -0.693359375, x, ALU.mult, ALU.add))
                V.link(STT(x, t, 2.12194440054690583e-4, x, ALU.mult, ALU.add))
                coef = [1 / math.factorial(n) for n in range(9)]
                V.link(TS(out, x, coef[8], coef[7], ALU.mult, ALU.add))
                for n in range(6, -1, -1):
                    V.link(TT(out, out, x, ALU.mult))
                    V.link(TS(out, out, coef[n], None, ALU.add))
                V.link(TS(t, t, -127.0, 128.0, ALU.max, ALU.min))
                V.link(TS(t, t, 127.0, 2.0 ** 23, ALU.add, ALU.mult))
                V.link(nc.vector.tensor_copy(x.bitcast(I32), t))
                V.link(TT(out, out, x, ALU.mult))

            dve.wait_ge(S["c_in"], 16)
            dve.wait_ge(S["pos_in"], 16)
            V.link(nc.vector.tensor_copy(rot[:, 0:1024], rot[:, 1024:2048].bitcast(I32)))
            V.link(TS(rot[:, 0:1024], rot[:, 0:1024], misc(M_INV), None, ALU.mult))
            reduce_angle(V.link, rot[:, 0:1024], rot[:, 1024:2048]).then_inc(S["rope_ang"], 1)
            V.base = V.n

            are, aim, ldt = (s_in[:, G5 * i:G5 * i + G5] for i in range(3))
            dt, la, th, kk, pp, dn, fr, fi, s8 = (s_s[:, G5 * i:G5 * i + G5] for i in range(9))
            sx, sy, su, sv = (s_co[:, a:b] for a, b in ((SX, SY), (SY, SU_), (SU_, SV), (SV, SA)))

            def powers(l):
                dve.wait_ge(S["s_par"], 16 * l + 16)
                exp_(ldt, dt, kk)
                V.link(TT(la, are, dt, ALU.mult))
                V.link(TT(th, aim, dt, ALU.mult))
                V.link(reduce_angle(V.link, th, kk))
                for t in range(BS + 1):
                    V.inc(TS(s_mag[:, G5 * t:G5 * t + G5], la, float(t), None, ALU.mult))
                    V.inc(TS(s_ang[:, G5 * t:G5 * t + G5], th, float(t), None, ALU.mult))
                V.join()
                exp_(s_mag, s_cos, s_sin)
                V.link(nc.vector.tensor_copy(s_mag, s_cos))
                V.link(reduce_angle(V.link, s_ang, s_sin))
                V.link(TS(s_co[:, SA:SA + G5], s_ang[:, G5 * BS:G5 * BS + G5], 1.0 / TWO_PI, None, ALU.mult))
                nc.vector.tensor_copy(s_co[:, SR:SR + G5], s_mag[:, G5 * BS:G5 * BS + G5]).then_inc(S["s_pow"], 1)

            def coefficients(l):
                dve.wait_ge(S["s_sc"], l + 1)
                V.link(TT(s_cos, s_mag, s_cos, ALU.mult))
                V.link(TT(s_sin, s_mag, s_sin, ALU.mult))
                V.link(TS(pp, s_cos[:, G5:2 * G5], -1.0, None, ALU.add))
                ai = s_sin[:, G5:2 * G5]
                V.link(TT(dn, are, are, ALU.mult))
                V.link(TT(s8, aim, aim, ALU.mult))
                V.link(TT(dn, dn, s8, ALU.add))
                V.link(nc.vector.reciprocal(dn, dn))
                V.link(TT(fr, pp, are, ALU.mult))
                V.link(TT(s8, ai, aim, ALU.mult))
                V.link(TT(fr, fr, s8, ALU.add))
                V.link(TT(fr, fr, dn, ALU.mult))
                V.link(TT(fi, ai, are, ALU.mult))
                V.link(TT(s8, pp, aim, ALU.mult))
                V.link(TT(fi, fi, s8, ALU.subtract))
                V.link(TT(fi, fi, dn, ALU.mult))

                def v3(x):
                    return x.rearrange("p (t g) -> p t g", g=G5)[:, 0:BS, :]

                frb, fib = bcast(fr, BS, 0), bcast(fi, BS, 0)
                V.inc(TT(v3(sx), v3(s_cos), frb, ALU.mult))
                V.inc(TT(v3(su), v3(s_sin), fib, ALU.mult))
                V.inc(TT(v3(sy), v3(s_cos), fib, ALU.mult))
                V.link(TT(v3(sv), v3(s_sin), frb, ALU.mult))
                V.inc(TT(v3(sx), v3(sx), v3(su), ALU.subtract))
                V.link(TT(v3(sy), v3(sy), v3(sv), ALU.add))
                V.inc(TS(sy, sy, misc(M_NSGN), None, ALU.mult))
                V.inc(TS(su, s_cos, misc(M_SGN), None, ALU.mult))
                V.link(TS(sv, s_sin, -1.0, None, ALU.mult))
                nc.vector.tensor_copy(s_s[:, 288:320], s_s[:, 0:32]).then_inc(S["s_made"], 1)

            def part(lo_, n, q):
                x = p_co[:, lo_:lo_ + G5 * n].rearrange("p (t g) -> p g t", g=G5)[:, :, :]
                return bcast(x[:, GP * q:GP * q + GP, :], C5, 3)

            def begin_tables(l, q):
                n = NPB * l + q
                tab = p_tab[q % 2].rearrange("p (g n) -> p g n", g=GP)
                m = 16 * ((NPB // 2) * l + q // 2)
                w, h0 = p_w[q % 2], p_h0[q % 2]

                def view(x, t):
                    return x[:, 0:GP * t * C5].rearrange("p (g t c) -> p g t c", g=GP, t=t)

                def chan(i, t):
                    return bcast(p_bc[q % 2][:, 64 * i:64 * i + 64].rearrange("p (g c) -> p g c", c=C5), t, 2)

                if q == 0:
                    dve.wait_ge(S["co_in"], 32 * l + 32)
                else:
                    dve.wait_ge(S["p_ang"], n)
                dve.wait_ge(bc_in[q % 2], m + 16)
                if q >= 2:
                    dve.wait_ge(tab_out[q % 2], m)
                ph = tab[:, :, TSIN:TSIN + NBT]
                k = p_k.rearrange("p (g j) -> p g j", g=GP)
                V.link(TT(ph, bcast(p_jr[:, 0:NBT], GP, 0), bcast(p_co[:, SA + GP * q:SA + GP * q + GP], NBT, 2), ALU.mult))
                V.link(TS(k, ph, MAGIC, None, ALU.add))
                STT(ph, k, MAGIC, ph, ALU.subtract, ALU.subtract).then_inc(S["p_ang"], 1)
                V.inc(TT(view(w, BS), part(SX, BS, q), chan(0, BS), ALU.mult))
                V.link(TT(view(p_t2, BS), part(SY, BS, q), chan(1, BS), ALU.mult))
                TT(view(w, BS), view(w, BS), view(p_t2, BS), ALU.add).then_inc(S["p_w"], 1)
                dve.wait_ge(S["p_w"], n + 1)
                V.inc(TT(view(h0, 9), part(SU_, 9, q), chan(2, 9), ALU.mult))
                V.link(TT(view(p_t2, 9), part(SV, 9, q), chan(3, 9), ALU.mult))
                TT(view(h0, 9), view(h0, 9), view(p_t2, 9), ALU.add).then_inc(S["p_h0"], 1)
                dve.wait_ge(S["p_h0"], n + 1)
                h2 = tab[:, :, TH2:TH2 + 128].rearrange("p g (t c) -> p g t c", c=C5)
                V.inc(TT(h2, part(SV + G5, BS, q), chan(2, BS), ALU.mult))
                V.link(TT(view(p_t2, BS), part(SU_ + G5, BS, q), chan(3, BS), ALU.mult))
                V.inc(TT(h2, h2, view(p_t2, BS), ALU.subtract))
                V.link(nc.vector.tensor_copy(tab[:, :, TR:TTOP], bcast(p_co[:, SR + GP * q:SR + GP * q + GP], TTOP - TR, 2)))

            def end_tables(l, q):
                n = NPB * l + q
                dve.wait_ge(S["p_k"], n + 1)
                if q:
                    dve.wait_ge(S["ks_out"], 16 * n)
                V.link(nc.vector.tensor_copy(p_ks, bank[3][0:16, :]))
                ks = p_ks.rearrange("c (g n) -> c g n", g=GP)[:, :, 0:C5]
                TT(ks, ks, p_bc[q % 2][0:16, 256:320].rearrange("c (g o) -> c g o", o=C5), ALU.add).then_inc(S["p_ke"], 1)

            def head_norm(l, h_, n):
                for i in range(32):
                    nc.vector.bn_stats(stats[:, 6 * i:6 * i + 6], h_[:, 128 * i:128 * i + 128]).then_inc(S["v_step"], 1)
                    V.n += 1
                V.join()
                nc.vector.memset(sd[0:1, 40:41], 0.0)
                for i in range(32):
                    last = nc.vector.bn_aggr(mv[:, 2 * i:2 * i + 2], stats[:, 6 * i:6 * i + 6])
                last.then_inc(S["hn_var"], 1)
                dve.wait_ge(S["hn_sd"], 2 * l + n + 1)
                V.link(nc.vector.reciprocal(sd[:, 0:32], sd[:, 0:32]))
                for i in range(32):
                    V.inc(TS(h_[:, 128 * i:128 * i + 128], h_[:, 128 * i:128 * i + 128], mv[:, 2 * i:2 * i + 1], sd[:, i:i + 1],
                             ALU.subtract, ALU.mult))
                V.join()

            with dve.Fori(0, DEPTH) as l:
                V.begin(l)
                dve.wait_ge(S["mem_hi"], l + 1)
                TT(meml, memraw, memh.bitcast(F32), ALU.subtract).then_inc(S["mem_lo"], 1)
                for i in range(16):
                    half, k = i // 8, i % 8
                    x0 = T * k + 512 * half
                    dve.wait_ge(S["xT_hi"], 16 * l + i + 1)
                    TT(xl[:, x0:x0 + 512], bank[i % 4], xh[:, x0:x0 + 512].bitcast(F32), ALU.subtract).then_inc(S["xT_lo"], 1)
                powers(l)
                dve.wait_ge(g_free[0], NUNIT * l + U_QK + 2)
                dve.wait_ge(g_free[1], NUNIT * l + U_QK + 2)
                dve.wait_ge(S["rope_in"], 16 * l + 16)
                a, b_ = (qk[:, 2048 * i:2048 * i + 2048].rearrange("p (k t) -> p k t", k=2) for i in range(2))
                ra, rb = (rot[:, 2048 * i:2048 * i + 2048].rearrange("p (k t) -> p k t", k=2) for i in range(2))
                co, si = bcast(rope[:, 0:T], 2, 0), bcast(rope[:, T:2 * T], 2, 0)
                V.inc(TT(ra, a, co, ALU.mult))
                V.link(TT(rb, b_, si, ALU.mult))
                TT(ra, ra, rb, ALU.subtract).then_inc(S["rope_done"], 1)
                V.inc(TT(a, a, si, ALU.mult))
                V.link(TT(b_, b_, co, ALU.mult))
                dve.wait_ge(S["rope_done"], 2 * l + 1)
                TT(rb, a, b_, ALU.add).then_inc(S["rope_done"], 1)

                coefficients(l)
                dve.wait_ge(S["co_out"], 16 * l + 16)
                dve.wait_ge(g_done[1], NUNIT * l + U_QK + 1)
                V.link(nc.vector.memset(sret, 0.0))
                dve.wait_ge(S["qk2_in"], 128 * l + 128)
                for c in range(NC):
                    dve.wait_ge(S["r_sc"], NC * l + c + 1)
                    if c >= 2:
                        dve.wait_ge(S["r_o"], NC * l + c - 1)
                        dve.wait_ge(S["r_u"], NC * l + c - 1)
                    TT(att[c % 2].rearrange("p (b n) -> p b n", b=2), mm[0].rearrange("p (b n) -> p b n", b=2)[:, :, 0:256],
                       cst[:, K_MASK:K_MASK + 512].rearrange("p (b n) -> p b n", b=2), ALU.mult).then_inc(S["r_att"], 1)
                    TT(kn[c % 2], bank[1][:, 256:512], cst[:, K_KDEC:K_KDEC + 256], ALU.mult).then_inc(S["r_kn"], 1)
                    dve.wait_ge(S["r_o"], NC * l + c + 1)
                    hv = hr[:, GW * c:GW * c + GW].rearrange("p (h e) -> p h e", h=HEADS)
                    TT(hv, bank[2].rearrange("p (h e) -> p h e", h=HEADS), bcast(misc(M_QD, 4), 128, 2), ALU.mult).then_inc(S["r_ho"], 1)
                    dve.wait_ge(S["r_u"], NC * l + c + 1)
                    if c:
                        dve.wait_ge(S["r_state"], NC * l + c)
                    for h in range(HEADS):
                        p, r0 = h // 2, 64 * (h % 2)
                        new, up = sret[r0:r0 + 64, 128 * h:128 * h + 128], bank[3][r0:r0 + 64, 128 * p:128 * p + 128]
                        if c:
                            last = STT(new, new, cst[r0:r0 + 64, K_MISC + M_CD + p:K_MISC + M_CD + p + 1], up, ALU.mult, ALU.add)
                        else:
                            last = nc.vector.tensor_copy(new, up)
                    last.then_inc(S["r_state"], 1)
                dve.wait_ge(S["r_ho"], NC * l + NC)
                head_norm(l, hr, 0)
                for i in range(4):
                    u, g = i // 2, i % 2
                    dve.wait_ge(g_free[g], NUNIT * l + U_RZ + u + 1)
                    hv = tview(hr, GW, g, u)
                    TT(hv, hv, gate[g].rearrange("p (c n) -> p c n", c=4), ALU.mult).then_inc(gate_used[g], 1)

                for i in range(8):
                    dve.wait_ge(S["x_s"], 8 * l + i + 1)
                    V.link(nc.vector.tensor_reduce(small[:, 0:4], mm[0].rearrange("p (c m) -> p c m", c=4), AX.X, ALU.max))
                    TS(small[:, 4:8], small[:, 0:4], -(128 ** -0.5), None, ALU.mult).then_inc(S["x_max"], 1)
                    dve.wait_ge(S["x_e"], 4 * (8 * l + i + 1))
                    V.link(nc.vector.reciprocal(small[:, 12:16], small[:, 8:12]))
                    pv = pm.rearrange("p (c m) -> p c m", c=4)
                    TT(pv, pv, bcast(small[:, 12:16], NMEM, 2), ALU.mult).then_inc(S["x_norm"], 1)
                for i in range(4):
                    u, g = i // 2, i % 2
                    dve.wait_ge(g_free[g], NUNIT * l + U_AZ + u + 1)
                    dve.wait_ge(S["x_pvev"], 8 * l + 8)
                    TT(xo[:, T * i:T * i + T], xo[:, T * i:T * i + T], gate[g], ALU.mult).then_inc(gate_used[g], 1)

                dve.wait_ge(S["wif_hi"], l + 1)
                TT(wifl, wifr, wifh.bitcast(F32), ALU.subtract).then_inc(S["wif_lo"], 1)
                dve.wait_ge(S["if_act"], 2 * l + 2)
                dve.wait_ge(S["res_in"], 16 * l + 16)
                V.link(STT(rowf[0:4, :], rowb[0:4, :], 0.0, rowm[0:4, :], ALU.min, ALU.subtract))
                V.inc(nc.vector.tensor_tensor_scan(rowb[0:4, :], rres[0:4, :], rowf[0:4, :], 0.0, ALU.mult, ALU.add))
                V.link(nc.vector.tensor_tensor_scan(rowm[0:4, :], rowf[0:4, :], rowi[0:4, :], 0.0, ALU.add, ALU.max))
                V.link(nc.vector.memset(rk, 0.0))
                V.inc(TT(rk[0:4, :], rowi[0:4, :], rowb[0:4, :], ALU.subtract))
                V.inc(TS(rk[96:100, :], rowm[0:4, :], -1.0, None, ALU.mult))
                V.inc(nc.vector.memset(small[0:4, 0:1], 0.0))
                V.inc(nc.vector.tensor_copy(small[0:4, 1:8], rowm[0:4, :].rearrange("p (c t) -> p c t", t=CH)[:, 0:7, CH - 1]))
                V.link(TT(rowf[0:4, :], rowb[0:4, :], rowm[0:4, :], ALU.subtract))
                V.link(nc.vector.tensor_copy(small[0:4, 8:16], rowf[0:4, :].rearrange("p (c t) -> p c t", t=CH)[:, :, CH - 1]))
                V.inc(TT(small[0:4, 16:24], small[0:4, 8:16], small[0:4, 0:8], ALU.add))

                def rows(x):
                    return x.rearrange("p (c t) -> p c t", t=CH)

                V.inc(TT(rows(rk[32:36, :]), rows(rowf[0:4, :]), bcast(small[0:4, 0:8], CH, 2), ALU.add))
                TT(rows(rk[64:68, :]), rows(rk[0:4, :]), bcast(small[0:4, 8:16], CH, 2), ALU.add).then_inc(S["rows_done"], 1)
                mxv = mx.rearrange("p (h t) -> p h t", h=HEADS)
                V.link(nc.vector.memset(mxv[:, :, 0:3], 0.0))
                dve.wait_ge(S["cw_in"], 16 * l + 16)
                for h in range(HEADS):
                    dve.wait_ge(g_free[h % 2], NUNIT * l + U_MX + h // 2 + 1)
                    y = xc[:, T * h:T * h + T]
                    for k in (3, 2, 1):
                        w = small[:, 32 + 4 * h + k:33 + 4 * h + k]
                        x_ = mxv[:, h, k:k + T]
                        V.link(TS(y, x_, w, None, ALU.mult) if k == 3 else STT(y, x_, w, y, ALU.mult, ALU.add))
                    STT(y, mxv[:, h, 0:T], small[:, 32 + 4 * h:33 + 4 * h], y, ALU.mult, ALU.add).then_inc(S["conv_done"], 1)
                dve.wait_ge(S["conv_done"], 4 * l + 4)
                nc.vector.memset(va.rearrange("p (g e) -> p g e", e=129)[:, :, 128:129], 1.0).then_inc(S["ones_done"], 1)
                dve.wait_ge(S["cols_done"], 5 * l + 5)
                for i in range(8):
                    h, half = i // 2, i % 2
                    dve.wait_ge(S["a_bc"], 8 * l + i + 1)
                    for c in range(4 * half, 4 * half + 4):
                        last = TS(wt[:, 512 * c + 128 * h:512 * c + 128 * h + 128], bank[i % 2][:, 128 * (c % 4):128 * (c % 4) + 128],
                                  cols[:, 4 * c + h:4 * c + h + 1], 0.0, ALU.add, ALU.min)
                    last.then_inc(S["w_arg"], 1)
                for c in range(NC):
                    dve.wait_ge(S["s_mm"], NC * l + c + 1)
                    dve.wait_ge(S["w_mask"], NC * l + c + 1)
                    w = wt[:, 512 * c:512 * c + 512]
                    TT(w, w, bank[c % 2], ALU.mult).then_inc(S["s_w"], 1)
                wi, wk, em = (cols[:, 32 * k:32 * k + 32] for k in (1, 2, 3))

                def k_weights(c):
                    dve.wait_ge(S["k_tr"], NC * l + c + 1)
                    if c >= 2:
                        dve.wait_ge(S["m_c"], NC * l + c - 1)
                    TT(kw[c % 2].rearrange("p (h d) -> p h d", h=HEADS), bank[3].rearrange("p (h d) -> p h d", h=HEADS),
                       bcast(wk[:, 4 * c:4 * c + 4], 128, 2), ALU.mult).then_inc(S["k_w"], 1)

                def heads2(x):
                    return x.rearrange("p (a x) -> p a x", a=2)[:, :, 0:258].rearrange("p a (b e) -> p a b e", b=2)

                num = inter.rearrange("p (a b e) -> p a b e", a=2, b=2)
                k_weights(0)
                for c in range(NC):
                    dve.wait_ge(S["m_num"], NC * l + c + 1)
                    if c == 0:
                        nc.vector.tensor_copy(num, heads2(gp[0])).then_inc(S["m_read"], 1)
                    else:
                        V.link(TT(num, heads2(gp[1]), bcast(wi[:, 4 * c:4 * c + 4].rearrange("p (a b) -> p a b", a=2), 129, 3), ALU.mult))
                        TT(num, num, heads2(gp[0]), ALU.add).then_inc(S["m_read"], 1)
                    dve.wait_ge(S["m_read"], NC * l + c + 1)
                    dn4 = small[:, 52:56]
                    den = inter.rearrange("p (h e) -> p h e", h=HEADS)[:, :, 128]
                    V.link(STT(dn4, den, -1.0, den, ALU.mult, ALU.max))
                    V.link(TT(dn4, dn4, em[:, 4 * c:4 * c + 4], ALU.max))
                    V.link(nc.vector.reciprocal(dn4, dn4))
                    V.link(TS(dn4, dn4, 0.5, None, ALU.mult))
                    V.inc(TT(hm[:, GW * c:GW * c + GW].rearrange("p (h e) -> p h e", h=HEADS),
                             inter.rearrange("p (h e) -> p h e", h=HEADS)[:, :, 0:128], bcast(dn4, 128, 2), ALU.mult))
                    if c + 1 < NC:
                        k_weights(c + 1)
                    dve.wait_ge(S["m_c"], NC * l + c + 1)
                    if c == 0:
                        nc.vector.tensor_copy(cst8.rearrange("p (a b e) -> p a b e", a=2, b=2), heads2(mm[0])).then_inc(S["m_st"], 1)
                    else:
                        dve.wait_ge(S["m_st"], NC * l + c)
                        for h in range(HEADS):
                            o0 = 512 * (h // 2) + 129 * (h % 2)
                            last = STT(cst8[:, 129 * h:129 * h + 129], cst8[:, 129 * h:129 * h + 129], dec[:, NC * h + c:NC * h + c + 1],
                                       mm[0][:, o0:o0 + 129], ALU.mult, ALU.add)
                        last.then_inc(S["m_st"], 1)
                V.join()
                for i in range(4):
                    u, g = i // 2, i % 2
                    dve.wait_ge(g_free[g], NUNIT * l + U_LO + u + 1)
                    hv = tview(hm, GW, g, u)
                    STT(hv, gate[g].rearrange("p (c n) -> p c n", c=4), 1.0, hv, ALU.add, ALU.mult).then_inc(gate_used[g], 1)
                    if i == 1:
                        begin_tables(l, 0)
                end_tables(l, 0)
                for g in range(2):
                    dve.wait_ge(gate_used[g], NGATE * l + 6)
                head_norm(l, hm, 1)
                dve.wait_ge(S["gn_in"], 16 * l + 16)
                for i in range(4):
                    u, g = i // 2, i % 2
                    dve.wait_ge(g_free[g], NUNIT * l + U_LZ + u + 1)
                    hv = tview(hm, GW, g, u)
                    V.link(TT(hv, hv, gate[g].rearrange("p (c n) -> p c n", c=4), ALU.mult))
                    TT(hv, hv, bcast(gn[:, 256 * u:256 * u + 256], 4, 0), ALU.mult).then_inc(gate_used[g], 1)
                    if i == 1:
                        begin_tables(l, 1)
                for u in range(U_LZ + 1, U_SZ + 1):
                    for q in TABLES_AT.get(u - 1, ()):
                        end_tables(l, q)
                    for q in TABLES_AT.get(u, ()):
                        begin_tables(l, q)

                dve.wait_ge(ys_out[0], 16 * 8 * (l + 1))
                dve.wait_ge(ys_out[1], 16 * 8 * (l + 1))
                zv = zin.rearrange("p (g j) -> p g j", g=GB)
                V.link(nc.vector.memset(zv[:, :, 0:1], 0.0))
                for b in range(NBATCH):
                    t = tb[b % SLOTS].rearrange("p (g n) -> p g n", g=GB)
                    ct, st = (t[:, :, o:o + NBT] for o in (TCOS, TSIN))
                    dve.wait_ge(tb_in[b % SLOTS], 48 * ((NBATCH // SLOTS) * l + b // SLOTS) + 48)
                    dve.wait_ge(S["s_g"], NBATCH * l + b + 1)
                    z1, z2 = (z.rearrange("p (g j) -> p g j", g=GB)[:, :, 1:NBT] for z in (zt1, zt2))
                    (TT(z1, ct[:, :, 1:NBT], bank[0][:, 0:256].rearrange("p (g j) -> p g j", g=GB), ALU.mult))
                    TT(z2, st[:, :, 1:NBT], bank[1][:, 0:256].rearrange("p (g j) -> p g j", g=GB), ALU.mult).then_inc(S["s_gr"], 1)
                    dve.wait_ge(S["s_gr"], NBATCH * l + b + 1)
                    V.link(TT(zv[:, :, 1:NBT], z1, z2, ALU.add))
                    for g in range(GB):
                        V.inc(nc.vector.tensor_tensor_scan(zz[:, NBT * g:NBT * g + NBT], bcast(t[:, g, TR:TR + 1], NBT, 1)[:, :, 0],
                                                           zin[:, NBT * g:NBT * g + NBT], 0.0, ALU.mult, ALU.add))
                    V.join()
                    if b >= 2:
                        dve.wait_ge(S["s_y"], NBATCH * l + b - 1)
                    zf = zz.rearrange("p (g j) -> p g j", g=GB)[:, :, 0:NB]
                    TT(zc[b % 2].rearrange("p (g j) -> p g j", g=GB), zf, ct[:, :, 0:NB], ALU.mult)
                    TT(zs[b % 2].rearrange("p (g j) -> p g j", g=GB), zf, st[:, :, 0:NB], ALU.mult).then_inc(S["s_z"], 1)
                dve.wait_ge(S["yd_out"], 128 * l + 128)
                for m in range(4):
                    dve.wait_ge(S["gy_hi"], 4 * l + m + 1)
                    TT(yl[:, T * m:T * m + T], yc[:, T * m:T * m + T], yh[:, T * m:T * m + T].bitcast(F32), ALU.subtract).then_inc(S["gy_lo"], 1)
                for m in range(4):
                    u, g = m // 2, m % 2
                    dve.wait_ge(g_free[g], NUNIT * l + U_GL + u + 1)
                    V.link(STT(gate[g], gate[g], 1.0, yc[:, T * m:T * m + T], ALU.add, ALU.mult))
                    if m >= 2:
                        dve.wait_ge(s5_out[g], 32 * l + 16)
                    (STT(s5o[g].rearrange("p (j s) -> p s j", s=BS), gate[g].rearrange("p (s j) -> p s j", s=BS), 0.5,
                               sz[:, T * m:T * m + T].rearrange("p (s j) -> p s j", s=BS), ALU.mult, ALU.mult)).then_inc(gate_used[g], 1)

                def ylo(n):
                    dve.wait_ge(S["oy_hi"], 16 * l + n + 1)
                    TT(oyl[:, 1024 * (n % 8):1024 * (n % 8) + 1024], yraw[n % 2],
                       oyh[:, 1024 * (n % 8):1024 * (n % 8) + 1024].bitcast(F32), ALU.subtract).then_inc(S["oy_lo"], 1)

                def norm(c):
                    dve.wait_ge(S["o_done"], 6 * l + 3 * (c // 4) + min(c % 4 + 1, 3))
                    if c % 4 == 3:
                        dve.wait_ge(S["o_used"], NOUT * l + 8 * (c // 4) + 8)
                    dve.wait_ge(xr_in[c % 2], 16 * (4 * l + c // 2 + 1))
                    if c >= 2:
                        dve.wait_ge(xs_out[c % 2], 16 * (4 * l + c // 2))
                    x_, r_ = xr[c % 2], rr[c % 2]
                    STT(r_, x_, ALPHA, (gp + mm)[c % 4], ALU.mult, ALU.add).then_inc(S["o_free"], 1)
                    dve.wait_ge(S["o_free"], NC * l + c + 1)
                    for i in range(2):
                        V.inc(nc.vector.bn_stats(stats[:, 6 * i:6 * i + 6], r_[:, 512 * i:512 * i + 512]))
                    V.join()
                    nc.vector.memset(sd[0:1, 40:41], 0.0)
                    nc.vector.bn_aggr(mv[:, 32:34], stats[:, 0:12]).then_inc(S["ln_var"], 1)
                    dve.wait_ge(S["ln_sd"], NC * l + c + 1)
                    V.link(nc.vector.reciprocal(sd[:, 33:34], sd[:, 32:33]))
                    V.link(STT(r_, r_, mv[:, 32:33], lng, ALU.subtract, ALU.mult))
                    STT(r_, r_, sd[:, 33:34], lnb, ALU.mult, ALU.add).then_inc(S["ln_y"], 1)

                dve.wait_ge(S["ln_in"], 32 * l + 32)
                for n in range(10):
                    ylo(n)
                for c in range(4):
                    norm(c)
                for n in range(10, 16):
                    ylo(n)
                for c in range(4, NC):
                    norm(c)
            assert V.n == steps_v, V.n


_OUT = (DEPTH + 1, T, D)


def kernel(x, mem, positions, w_in, s5_a_re, s5_a_im, s5_log_dt, s5_b_re, s5_b_im, s5_c_re, s5_c_im, s5_d, s5_w_glu,
           ml_conv_w, ml_wq, ml_wk, ml_b_ig, ml_b_fg, ml_gn, xa_w_kv, w_out, ln_g, ln_b):
    import concourse.bacc as bacc
    from concourse.bass_utils import run_bass_kernel_spmd

    A = np.ascontiguousarray
    x, mem, w_in = np.asarray(x), np.asarray(mem), np.asarray(w_in)
    widths = [256, 256] + [GW] * 8 + [HEADS, HEADS, GW, GW]
    edge = np.cumsum([0] + widths)
    rq, rk_, rv, rz, su, sz, mx, lv, lo, lz, mi, mf, aq, az = (w_in[:, :, a:b] for a, b in zip(edge[:-1], edge[1:]))

    def rope_halves(w):
        w = w.reshape(DEPTH, D, HEADS, 2, 32)
        return [w[:, :, :, i, :].reshape(DEPTH, D, 128) for i in range(2)]

    q0, q1 = rope_halves(rq)
    k0, k1 = rope_halves(rk_)
    kv = np.asarray(xa_w_kv)
    order = [kv[:, :, :GW], kv[:, :, GW:], np.concatenate([q0, k0, q1, k1], -1), rv, aq, rz, az, mx, lv, lo, lz, su, sz]

    def units(w, k, n):
        N = w.shape[-1]
        return w.reshape(DEPTH, k, 128, N // n, n).transpose(0, 3, 2, 1, 4).reshape(DEPTH, N // n, 128, k * n)

    parts = [units(w, KT, 256) for w in order]
    glu = units(np.asarray(s5_w_glu), 4, 256)
    parts.append(np.concatenate([glu, np.zeros_like(glu)], -1))
    wo = np.asarray(w_out).reshape(DEPTH, 4, GW, D)
    wo = [units(wo[:, q], 4, 512) for q in range(4)]
    parts += wo
    w = np.concatenate(parts, 1).reshape(DEPTH * NSTORED, 128, 2048)
    wif = np.zeros((DEPTH, D, 128), np.float32)
    wif[:, :, 0:HEADS], wif[:, :, 32:32 + HEADS] = mi, mf
    wif = wif.reshape(DEPTH, KT, 128, 128).transpose(0, 2, 1, 3).reshape(DEPTH, 128, KT * 128)
    wqk = np.stack([np.asarray(ml_wq), np.asarray(ml_wk)], 1).transpose(0, 3, 1, 2, 4).reshape(DEPTH, 128, 1024)

    def states(a):
        return np.swapaxes(np.asarray(a), 1, 2)

    def chunks(a, b):
        a = np.concatenate([a, b], 1).reshape(DEPTH, 128, NPB, GP * C5)
        return a.transpose(0, 2, 1, 3).reshape(DEPTH * NPB, 128, GP * C5)

    ldt = np.broadcast_to(np.asarray(s5_log_dt)[:, None, :], (DEPTH, 128, G5))
    s5a = np.concatenate([np.concatenate([states(s5_a_re)] * 2, 1), np.concatenate([states(s5_a_im)] * 2, 1), ldt], 2)
    s5a = np.concatenate([s5a, s5a[-1:]])
    br, bi = states(s5_b_re), states(s5_b_im)
    cr, ci = (states(np.swapaxes(np.asarray(c), 2, 3)) for c in (s5_c_re, s5_c_im))
    diag = np.zeros((DEPTH * NPB, 128, GP, C5), np.float32)
    diag[:, np.arange(C5), :, np.arange(C5)] = np.asarray(s5_d).reshape(DEPTH * NPB, GP, C5).transpose(2, 0, 1)
    s5bc = np.concatenate([chunks(br, bi), chunks(bi, br), chunks(cr, ci), chunks(ci, cr),
                           diag.reshape(DEPTH * NPB, 128, GP * C5)], 2)
    conv = np.asarray(ml_conv_w).reshape(DEPTH, 4, HEADS, 128).transpose(0, 3, 2, 1).reshape(DEPTH, 128, 16)
    bif = np.stack([np.asarray(ml_b_ig), np.asarray(ml_b_fg)], -1)
    cst, jc = constants()
    arrays = dict(x=x[0], memT=mem[0].T, pos=np.asarray(positions)[0].astype(np.int32), w=w, wif=wif, wqk=wqk,
                  s5a=s5a, s5bc=s5bc, convw=conv, bif=bif, gn=np.asarray(ml_gn).reshape(-1),
                  lng=np.asarray(ln_g).reshape(-1), lnb=np.asarray(ln_b).reshape(-1), cst=cst, jcst=jc)
    arrays = {k: A(v) for k, v in arrays.items()}
    nc = bacc.Bacc("TRN2", target_bir_lowering=False, num_devices=1)
    dram = {k: nc.dram_tensor("in_" + k, v.shape, mybir.dt.from_np(v.dtype), kind="ExternalInput").ap() for k, v in arrays.items()}
    for name, shape in (("yt", (16, 128, T)), ("ud", (GW, T)), ("yd", (GW, T)), ("ropetab", (128, 2 * T)),
                        ("tabs", (G5, 128, TTOP)), ("kd", (G5, C5, 240)), ("s5co", (128, SCOLS))):
        dram[name] = nc.dram_tensor(name, shape, F32, kind="Internal").ap()
    dram["xs"] = nc.dram_tensor("xs", _OUT, F32, kind="ExternalOutput").ap()
    build(nc, dram)
    r = run_bass_kernel_spmd(nc, [{"in_" + k: v for k, v in arrays.items()}], core_ids=[0])
    return np.asarray(r.results[0]["xs"])[DEPTH:DEPTH + 1]
```

```python
import math
import numpy as np
import concourse.bass as bass
from concourse import mybir
from contextlib import ExitStack

F32 = mybir.dt.float32
F32R = mybir.dt.float32r
I32 = mybir.dt.int32
ALU = mybir.AluOpType
ACT = mybir.ActivationFunctionType
AX = mybir.AxisListType

DEPTH, D, T, NMEM, GW = 2, 1024, 1024, 256, 512
HEADS, DK, DV = 4, 64, 128
KT = D // 128
CH = 128
NC = T // CH
REF_CHUNK = 64
ALPHA = (2 * DEPTH) ** 0.25
GN_EPS, LN_EPS = 1e-6, 1e-5
G5, C5, P5 = 32, 16, 64
BS = 8
NB = T // BS
GB = 2
NBATCH = G5 // GB
NBT = NB + 1
TG, TH, TH2, TCOS, TSIN, TR, TTOP = 0, 192, 320, 448, 448 + NBT, 448 + 2 * NBT, 708
GCOLS = TTOP + 128
SLOTS = 4
GP = 4
NPB = G5 // GP
SX, SY, SU_, SV, SA, SR = 0, 8 * G5, 16 * G5, 25 * G5, 34 * G5, 35 * G5
SCOLS = 36 * G5
(U_MK, U_MV, U_QK, U_RV, U_AQ, U_RZ, U_AZ, U_MX, U_LV, U_LO, U_LZ, U_SU, U_SZ, U_GL) = range(0, 28, 2)
TABLES_AT = {U_LO: (0,), U_LO + 1: (), U_LZ: (1,), U_LZ + 1: (2, 3), U_SU: (4, 5), U_SU + 1: (6, 7)}
CUNITS = {u + i for u in (U_QK, U_AQ, U_AZ, U_MX, U_SU, U_SZ) for i in range(2)}
NGATE = 10
NUNIT = 28
NOUT = 16
HALVES = 2 * 26 + 2 + 2 * NOUT
NSTORED = NUNIT + NOUT // 2
TWO_PI = 2 * math.pi
C1 = 6.28125
C2 = float(np.float32(round((TWO_PI - C1) * 2 ** 20) / 2 ** 20))
C3 = TWO_PI - C1 - C2
KQ = (0, 2, 3, 1)
MAGIC = 1.5 * 2 ** 23
TURN = 6.283185
PI_LO = 3.1415925
STEPS_V = 489
STEPS_A = 41
K_ID, K_MASK, K_KDEC, K_CAUS, K_ONE, K_MISC = 0, 128, 640, 896, 1024, 1536
(M_SGN, M_NSGN, M_HPI, M_GNE, M_LNE, M_INV, M_ONE, M_TURN, M_QD, M_CD) = (0, 1, 2, 3, 4, 5, 6, 7, 8, 12)
K_COLS = 1536 + 16
J_ROW, J_RES = 0, 136
J_COLS = J_RES + T


def constants():
    c = np.zeros((128, K_COLS), np.float64)
    c[:, K_ID:K_ID + 128] = np.eye(128)
    g = 1.0 - 2.0 ** (-5.0 - np.arange(HEADS))
    s, t = np.arange(CH)[:, None], np.arange(CH)[None, :]
    same = (s // REF_CHUNK) == (t // REF_CHUNK)
    for h in range(HEADS):
        m = np.where(s <= t, g[h] ** (t - s), np.where(same, g[h] ** (s - t), 0.0))
        m0 = K_MASK + 256 * (h % 2) + 128 * (h // 2)
        c[:, m0:m0 + 128] = m / g[h] ** (t + 1.0) * DK ** -0.5
        c[:, K_KDEC + h * DK:K_KDEC + (h + 1) * DK] = g[h] ** (CH - 1.0 - s) * DK ** -0.5
        c[:, K_MISC + M_QD + h] = (g[h] ** (np.arange(CH) + 1.0))
        c[h, K_ONE + h * 128:K_ONE + (h + 1) * 128] = 1.0
    for p in range(2):
        c[:64, K_MISC + M_CD + p] = g[2 * p] ** CH
        c[64:, K_MISC + M_CD + p] = g[2 * p + 1] ** CH
    c[:, K_CAUS:K_CAUS + 128] = (s <= t)
    c[:64, K_MISC + M_SGN], c[64:, K_MISC + M_SGN] = 1.0, -1.0
    c[:, K_MISC + M_NSGN] = -c[:, K_MISC + M_SGN]
    c[:, K_MISC + M_HPI] = math.pi / 2
    c[:, K_MISC + M_TURN] = TURN * c[:, K_MISC + M_NSGN]
    c[:, K_MISC + M_GNE], c[:, K_MISC + M_LNE] = GN_EPS, LN_EPS
    c[:, K_MISC + M_INV] = 10000.0 ** (-(np.arange(128) % 32) / 32.0)
    c[:, K_MISC + M_ONE] = 1.0
    j = np.zeros((128, J_COLS), np.float64)
    j[:, J_ROW:J_ROW + NBT] = np.arange(NBT)
    j[:, J_RES:] = (np.arange(T) % CH != 0)
    return c.astype(np.float32), j.astype(np.float32)


class Steps:

    def __init__(self, eng, sem, per_layer):
        self.eng, self.sem, self.per, self.n, self.base = eng, sem, per_layer, 0, 0

    def begin(self, layer):
        self.layer, self.n = layer, 0

    def inc(self, ins):
        ins.then_inc(self.sem, 1)
        self.n += 1

    def link(self, ins):
        self.inc(ins)
        self.eng.wait_ge(self.sem, self.layer * self.per + self.n + self.base)

    def join(self):
        self.eng.wait_ge(self.sem, self.layer * self.per + self.n + self.base)


def bcast(ap, n, dim):
    dim = max(dim, 1)
    dims = [list(x) for x in ap.ap]
    return bass.AP(ap.tensor, ap.offset, dims[:dim] + [[0, n]] + dims[dim:])


def tview(x, width, g, u):
    return x.rearrange("p (c n) -> p c n", n=width)[:, 4 * g:4 * g + 4, 256 * u:256 * u + 256]


def build(nc, dram, steps_v=STEPS_V, steps_a=STEPS_A):
    ctx = ExitStack()
    with ctx:
        arena = ctx.enter_context(nc.sbuf_tensor("arena", [128, 53200], F32))
        base = nc.sbuf_base - 53200 * 4 if nc.sbuf_base >= 53200 * 4 else 0

        def at(name, cols, off, dt=F32, rows=128):
            return nc.alloc_sbuf_tensor_at(name, [rows, cols], dt, offset=base + off * 4)[:, :]

        cursor = [0]

        def take(n):
            cursor[0] += (n + 7) // 8 * 8
            assert cursor[0] <= 53200, cursor[0]
            return cursor[0] - (n + 7) // 8 * 8

        o_x = take(2 * KT * T)
        xh, xl = at("xh", KT * T, o_x, F32R), at("xl", KT * T, o_x + KT * T, F32R)
        o_raw = take(2048)
        wraw = [at(f"wraw{i}", 1024, o_raw + 1024 * i) for i in range(2)]
        o_w = take(8192)
        whi = [at(f"whi{i}", 2048, o_w + 4096 * i, F32R) for i in range(2)]
        wlo = [at(f"wlo{i}", 2048, o_w + 4096 * i + 2048, F32R) for i in range(2)]
        R = [take(4096) for _ in range(4)]
        o_v = take(HEADS * NC * 129)
        o_g = take(2048)
        gate = [at(f"gate{i}", 1024, o_g + 1024 * i) for i in range(2)]
        o_ys = take(1024)
        ystage = [[at(f"ystage{k}{i}", 512, ((o_ys, o_ys + 512, R[3] + 3072, R[3] + 3584), (o_ys + 512, o_g, o_g + 512, o_g + 1024))[k][i]) for i in range(4)]
                  for k in range(2)]
        cst = at("cst", K_COLS, take(K_COLS))
        gn = at("gn", GW, take(GW))
        stats = at("stats", 32 * 6, take(32 * 6))
        mv = at("mv", 64, take(64))
        sd = at("sd", 64, take(64))
        cols = at("cols", NC * 16, take(NC * 16))
        dec = at("dec", 32, take(32))
        small = at("small", 128, take(128))
        qk = at("qk", 4096, R[0])
        rot = at("rot", 4096, R[2])
        hr = at("hr", 4096, R[2])
        rope = at("rope", 2048, o_g)
        rv = at("rv", 4096, o_v)
        qk2 = at("qk2", 4096, R[0])
        mkT, mvT = at("mkT", 1024, R[1]), at("mvT", 1024, R[1] + 1024)
        pm = [at(f"pm{i}", 1024, (R[1] + 2048, o_g)[i]) for i in range(2)]
        pt = [at(f"pt{i}", 1024, (R[1] + 3072, o_ys)[i]) for i in range(2)]
        memraw = at("memraw", 2048, o_v + 2048)
        memh, meml = at("memh", 2048, R[3], F32R), at("meml", 2048, R[3] + 2048, F32R)
        aq, xo = at("aq", 4096, R[3]), at("xo", 4096, R[0])
        att = [at(f"att{i}", 512, R[1] + 2048 + 512 * i) for i in range(2)]
        kn = [at(f"kn{i}", 256, R[1] + 3072 + 256 * i) for i in range(2)]
        sret = at("sret", 512, R[1] + 3584)
        mx, xc = at("mx", HEADS * (T + 3), o_v), at("xc", 4096, R[3])
        wifr = at("wifr", 1024, R[3])
        wifh, wifl = at("wifh", 1024, R[3] + 1024, F32R), at("wifl", 1024, R[3] + 2048, F32R)
        wqk = at("wqk", 1024, o_g + 1024)
        rowi, rowf, rowb, rowm = (at(f"row{n}", T, R[1] + T * i) for i, n in enumerate("ifbm"))
        rres = at("rres", T, o_g + 1024)
        rk = at("rk", T, o_g)
        va, qT, kTt, wt = at("va", NC * HEADS * 129, o_v), at("qT", 4096, R[0]), at("kTt", 4096, R[1]), at("wt", 4096, R[2])
        hm = at("hm", 4096, R[1])
        kw = [at(f"kw{i}", 512, R[3] + 512 * i) for i in range(2)]
        cst8 = at("cstate", HEADS * 129, R[3] + 1024)
        inter = at("inter", HEADS * 129, R[3] + 1024 + 520)
        us, uu, sz, yb = (at(n, 4096, R[i]) for n, i in (("us", 0), ("uu", 2), ("sz", 1), ("yb", 3)))
        yc = [at(f"yc{m}", T, o_x + 8192 * (m // 2) + 2048 + T * (m % 2)) for m in range(4)]
        tb = [at(f"tb{i}", GB * GCOLS, (o_v, R[0])[i // 2] + GB * GCOLS * (i % 2)) for i in range(SLOTS)]
        yh, yl = at("yh", 4096, R[2], F32R), at("yl", 4096, R[3], F32R)
        zin = at("zin", GB * NBT, o_ys)
        zz = at("zz", GB * NBT, o_ys + 264)
        zt1 = at("zt1", GB * NBT, o_g)
        zt2 = at("zt2", GB * NBT, o_g + 264)
        zc = [at(f"zc{i}", GB * NB, o_g + 528 + 256 * i) for i in range(2)]
        zs = [at(f"zs{i}", GB * NB, o_g + 1040 + 256 * i) for i in range(2)]
        s5o = [at(f"s5o{i}", 1024, o_v + 2048 + 1024 * i) for i in range(2)]
        oyh, oyl = at("oyh", 8192, o_x, F32R), at("oyl", 8192, o_x + 8192, F32R)
        yraw = [at(f"yraw{i}", 1024, o_v + 1024 * i) for i in range(2)]
        lng, lnb = at("lng", D, R[1] + 2048), at("lnb", D, R[1] + 3072)
        xr = [at(f"xr{i}", D, (R[0], R[2])[i // 4] + D * (i % 4)) for i in range(NC)]
        rp = at("rp", 4096, o_x + 8192)
        whi.append(at("whi2", 2048, R[3], F32R))
        wlo.append(at("wlo2", 2048, R[3] + 2048, F32R))

        gp = [ctx.enter_context(nc.psum_tensor(f"gp{i}", [128, 1024], F32))[:, :] for i in range(2)]
        mm = [ctx.enter_context(nc.psum_tensor(f"mm{i}", [128, 1024], F32))[:, :] for i in range(2)]
        bank = [mm[i // 2][:, 512 * (i % 2):512 * (i % 2) + 512] for i in range(4)]

        s_co = at("s_co", SCOLS, R[1] + 2048)
        s_mag, s_ang = at("s_mag", 288, R[1] + 3200), at("s_ang", 288, R[1] + 3488)
        s_in = at("s_in", 96, R[1] + 3776)
        s_sin, s_cos = at("s_sin", 288, o_ys), at("s_cos", 288, o_ys + 288)
        s_s = at("s_s", 288, o_ys + 576)
        p_co = at("p_co", SCOLS, R[2])
        p_w = [at(f"p_w{i}", GP * 128, R[2] + (1152, 2952)[i]) for i in range(2)]
        p_bc = [at(f"p_bc{i}", 320, R[2] + 1664 + 320 * i) for i in range(2)]
        p_ks, p_jr = at("p_ks", GP * 128, R[2] + 2304, rows=16), at("p_jr", 136, R[2] + 2816)
        p_tab = [at(f"p_tab{i}", GP * TTOP, (o_v, R[3])[i]) for i in range(2)]
        p_h0 = [at(f"p_h0{i}", GP * 144, (o_v + 2832, R[2] + 3464)[i]) for i in range(2)]
        p_t2, p_k = at("p_t2", GP * 144, R[3] + 2832), at("p_k", GP * NBT, R[3] + 3408)
        assert SCOLS <= 1152 and 3408 + GP * NBT <= 4096
        p_t3 = at("p_t3", GP * 128, o_ys)
        p_zero = at("p_zero", 112 * G5, R[0], rows=16)

        names = """c_in pos_in s_par s_pow s_sc s_made co_out co_in bc_in0 bc_in1 cp_out zeroed kd_zeroed p_ang p_h0 p_w p_prod p_tr p_ev p_k p_ke p_hc tab_out0 tab_out1 ks_out
            rope_ang rope_sc rope_st xT_hi xT_lo raw_in0 raw_in1 hi_done lo_done o_used g_done0 g_done1 g_free0
            g_free1 mem_in mem_hi mem_lo rope_in rope_done qk2_in r_sc r_att r_kn r_o r_ho r_u r_state hn_var hn_sd
            gate_used0 gate_used1 tr_done tr_free ys_out0 ys_out1 ys_out2 ys_out3 x_s x_max x_e x_norm x_t x_pt x_pv x_pvev xa_out wif_in
            wif_hi wif_lo bias_in if_done if_act rows_done res_in colt_done cols_done wqk_in conv_done xc_ready
            ones_done a_bc w_arg w_exp w_mask qk_mm qk_ev s_mm s_w k_tr k_w m_num m_read m_c m_st gn_in cw_in ud_out uu_in yc_in0 yc_in1 yc_in2 yc_in3
            tb_in0 tb_in1 tb_in2 tb_in3 s_g s_gr s_z s_y s_ye yd_out0 yd_out1 yd_out2 yd_out3 gy_hi gy_lo s5_out0 s5_out1 y_in0 y_in1 oy_hi oy_lo o_done o_free
            xr_in ln_in ln_var ln_sd x_rows xs_out0 xs_out1 xn_in xt_done v_step a_step""".split()
        S = {n: ctx.enter_context(nc.semaphore(n)) for n in names}
        raw_in, g_done, g_free = [[S[f"{n}{i}"] for i in range(2)] for n in ("raw_in", "g_done", "g_free")]
        gate_used = [S[f"gate_used{i}"] for i in range(2)]
        ys_out = [S[f"ys_out{i}"] for i in range(4)]
        s5_out, bc_in, tab_out, xs_out = [[S[f"{n}{i}"] for i in range(2)] for n in ("s5_out", "bc_in", "tab_out", "xs_out")]
        y_in = [S[f"y_in{i}"] for i in range(2)]
        tb_in = [S[f"tb_in{i}"] for i in range(SLOTS)]

        def half0(u):
            return 2 * u if u < U_GL else 2 * U_GL + (u - U_GL) if u < NUNIT else 2 * U_GL + 2 + 2 * (u - NUNIT)

        def slot(u):
            return u % 2 if u < NUNIT else (u - NUNIT) % 3

        def nhalf(u):
            return 1 if U_GL <= u < NUNIT else 2

        def misc(i, n=1, rows=128):
            return cst[0:rows, K_MISC + i:K_MISC + i + n]

        ident = cst[:, K_ID:K_ID + 128]
        def part(lo_, n, q):
            x = p_co[:, lo_:lo_ + G5 * n].rearrange("p (t g) -> p g t", g=G5)
            return bcast(x[:, GP * q:GP * q + GP, :], C5, 3)

        def view(x, t):
            return x[:, 0:GP * t * C5].rearrange("p (g t c) -> p g t c", g=GP, t=t)

        def chan(q, i, t):
            return bcast(p_bc[q % 2][:, 64 * i:64 * i + 64].rearrange("p (g c) -> p g c", c=C5), t, 2)

        block = ctx.enter_context(nc.Block())

        @block.sync
        def _(sp):
            sp.dma_start(cst, dram["cst"]).then_inc(S["c_in"], 16)
            sp.dma_start(rp[:, 1024:2048].bitcast(I32), bass.AP(dram["pos"].tensor, 0, [[0, 128], [1, T]])).then_inc(S["pos_in"], 16)
            sp.dma_start(s_in, dram["s5a"][0]).then_inc(S["s_par"], 16)

            def mem_load():
                sp.dma_start(memraw.rearrange("p (k m) -> p k m", k=KT), dram["memT"].rearrange("(k p) m -> p k m", p=128)).then_inc(S["mem_in"], 16)

            def raw(l, u):
                for i in range(nhalf(u)):
                    n = half0(u) + i
                    if n >= 2:
                        sp.wait_ge(S["hi_done"], l * HALVES + n - 1)
                        sp.wait_ge(S["lo_done"], l * HALVES + n - 1)
                    row = l * NSTORED + (u if u < NUNIT else NUNIT + 2 * KQ[(u - NUNIT) % 8 // 2] + u % 2)
                    sp.dma_start(wraw[n % 2], dram["w"][row, :, 1024 * i:1024 * i + 1024]).then_inc(raw_in[n % 2], 16)

            mem_load()
            raw(0, 0)
            with sp.Fori(0, DEPTH) as l:
                raw(l, 1)
                sp.wait_ge(S["rope_st"], 32)
                sp.dma_start(rope, dram["ropetab"]).then_inc(S["rope_in"], 16)
                sp.dma_start(gn, bass.AP(dram["gn"].tensor, l * GW, [[0, 128], [1, GW]])).then_inc(S["gn_in"], 16)
                sp.dma_start(small[:, 32:48], dram["convw"][l]).then_inc(S["cw_in"], 16)
                sp.dma_start(small[0:4, 48:50], dram["bif"][l]).then_inc(S["bias_in"], 16)
                for u in range(2, U_QK + 4):
                    raw(l, u)
                sp.wait_ge(S["rope_done"], 2 * l + 2)
                for half in range(2):
                    for h in range(HEADS):
                        src = rot[32 * h:32 * h + 32, 2048 * half:2048 * half + 2048]
                        r0 = 64 * (h % 2) + 32 * half
                        sp.dma_start(qk2[r0:r0 + 32, 2048 * (h // 2):2048 * (h // 2) + 2048], src).then_inc(S["qk2_in"], 16)
                for u in range(U_QK + 4, U_MX):
                    raw(l, u)
                sp.wait_ge(S["x_pvev"], 8 * l + 8)
                sp.dma_start(wifr, dram["wif"][l]).then_inc(S["wif_in"], 16)
                raw(l, U_MX)
                sp.wait_ge(gate_used[1], NGATE * l + 4)
                sp.dma_start(rres[0:4, :], dram["jcst"][0:4, J_RES:J_RES + T]).then_inc(S["res_in"], 16)
                for u in range(U_MX + 1, U_LO + 1):
                    raw(l, u)
                sp.wait_ge(S["rows_done"], l + 1)
                sp.dma_start(wqk, dram["wqk"][l]).then_inc(S["wqk_in"], 16)
                raw(l, U_LO + 1)
                sp.wait_ge(S["m_st"], NC * l + NC)
                sp.wait_ge(S["co_out"], 16 * l + 16)
                sp.dma_start(p_co, dram["s5co"]).then_inc(S["co_in"], 16)
                sp.dma_start(p_jr, dram["jcst"][:, 0:136]).then_inc(S["co_in"], 16)
                for u in range(U_LO + 1, NUNIT):
                    if u > U_LO + 1:
                        raw(l, u)
                    for q in {U_LO + 1: (0, 1), U_LZ + 1: (2,), U_SU: (3,), U_SU + 1: (4, 5), U_SZ + 1: (6, 7)}.get(u, ()):
                        if q >= 2:
                            sp.wait_ge(S["p_ke"], NPB * l + q - 1)
                        sp.dma_start(p_bc[q % 2], dram["s5bc"][l * NPB + q]).then_inc(bc_in[q % 2], 16)
                sp.wait_ge(S["ud_out"], 64 * l + 64)
                for i in range(2):
                    sp.wait_ge(tab_out[i], 64 * l + 64)
                sp.wait_ge(S["ks_out"], 128 * l + 128)
                for s in range(BS):
                    src = dram["ud"].rearrange("(g c) (s j) -> s c g j", c=C5, s=BS)[BS - 1 - s]
                    sp.dma_start(uu[C5 * s:C5 * s + C5, :].rearrange("c (g j) -> c g j", g=G5), src).then_inc(S["uu_in"], 16)
                def y_back(m):
                    sp.wait_ge(S[f"yd_out{m}"], 128 * l + 128)
                    if m == 0:
                        sp.wait_ge(g_done[1], NUNIT * l + U_SZ + 2)
                    sp.dma_start(yc[m], dram["yd"][128 * m:128 * m + 128, :]).then_inc(S[f"yc_in{m}"], 16)

                for b in range(NBATCH):
                    if b >= SLOTS:
                        sp.wait_ge(S["s_y"], NBATCH * l + b - SLOTS + 1)
                    t = tb[b % SLOTS].rearrange("p (g n) -> p g n", g=GB)
                    sp.dma_start(t[:, :, 0:TTOP], dram["tabs"][GB * b:GB * b + GB].rearrange("g p n -> p g n")).then_inc(tb_in[b % SLOTS], 16)
                    for g in range(GB):
                        src = bass.AP(dram["kd"].tensor, (b * GB + g) * C5 * 240, [[16, BS], [240, C5], [1, 128]])
                        sp.dma_start(t[:, g, TTOP:GCOLS], src).then_inc(tb_in[b % SLOTS], 16)
                    if b in (8, 12, 15):
                        y_back((8, 12, 15).index(b))
                y_back(3)

                def y_load(n):
                    if n >= 2:
                        sp.wait_ge(S["oy_hi"], 16 * l + n - 1)
                        sp.wait_ge(S["oy_lo"], 16 * l + n - 1)
                    k0, t0 = 4 * KQ[n % 8 // 2] + 2 * (n % 2), 512 * (n // 8)
                    sp.dma_start(yraw[n % 2].rearrange("p (k t) -> p k t", k=2),
                                 dram["yt"][k0:k0 + 2, :, t0:t0 + 512].rearrange("k p t -> p k t")).then_inc(y_in[n % 2], 16)

                sp.wait_ge(S["xa_out"], 64 * l + 64)
                for i in range(4):
                    sp.wait_ge(ys_out[i], 64 * l + 64)
                for n in range(4):
                    y_load(n)
                raw(l, NUNIT)
                y_load(4)
                y_load(5)
                raw(l, NUNIT + 1)
                raw(l, NUNIT + 2)
                sp.wait_ge(s5_out[0], 32 * l + 32)
                sp.wait_ge(s5_out[1], 32 * l + 32)
                y_load(6)
                y_load(7)

                def rows_out(c):
                    sp.wait_ge(S["x_rows"], NC * l + c + 2)
                    sp.dma_start(dram["xs"][l + 1, 128 * c:128 * c + 128, :], xr[c]).then_inc(xs_out[c % 2], 16)

                for j in range(3, NOUT):
                    raw(l, NUNIT + j)
                    if j % 2 and j + 5 < NOUT:
                        y_load(j + 5)
                        y_load(j + 6)
                    if j == 12:
                        for c in range(4):
                            rows_out(c)
                mem_load()
                sp.wait_ge(S["hi_done"], HALVES * l + HALVES)
                sp.wait_ge(S["lo_done"], HALVES * l + HALVES)
                raw(l + 1, 0)
                for c in range(4, NC):
                    rows_out(c)
                for i in range(2):
                    sp.wait_ge(xs_out[i], 64 * l + 64)
                sp.dma_start(s_in, dram["s5a"][l + 1]).then_inc(S["s_par"], 16)
            sp.wait_ge(S["s_par"], 16 * DEPTH + 16)

        @block.tensor
        def _(pe):
            def mm3(out, ah, al, bh, bl, start, stop):
                nc.tensor.matmul(out, ah, bh, start=start, stop=False)
                nc.tensor.matmul(out, ah, bl, start=False, stop=False)
                return nc.tensor.matmul(out, al, bh, start=False, stop=stop)

            pe.wait_ge(S["c_in"], 16)

            def tables(l, q):
                n = NPB * l + q
                bt, bk = bank[2 - 2 * (q % 2)], bank[3 - 2 * (q % 2)]
                pe.wait_ge(S["p_w"], n + 1)
                if q >= 2:
                    pe.wait_ge(S["p_ev"], n - 1)
                if q in (5, 7):
                    pe.wait_ge(S["tr_free"], 16 * l + 16)
                for g in range(GP):
                    last = nc.tensor.transpose(bt[:, 128 * g:128 * g + 128], p_w[q % 2][:, 128 * g:128 * g + 128], ident)
                last.then_inc(S["p_tr"], 1)
                pe.wait_ge(S["p_h0"], n + 1)
                if q >= 2:
                    pe.wait_ge(S["p_ke"], n - 1)
                for g in range(GP):
                    last = nc.tensor.matmul(bk[0:16, 128 * g:128 * g + 128], p_w[q % 2][:, 128 * g:128 * g + C5],
                                            p_h0[q % 2][:, 144 * g:144 * g + 128], start=True, stop=True)
                last.then_inc(S["p_k"], 1)

            def unit(l, u):
                kind = "MC" if u < U_MV else "MT" if u < U_QK else "C" if u in CUNITS else "G" if u >= U_GL else "T"
                wh, wl = whi[slot(u)], wlo[slot(u)]
                pe.wait_ge(S["lo_done"], l * HALVES + half0(u) + nhalf(u))
                for g in range(2):
                    if u:
                        pe.wait_ge(g_free[g], NUNIT * l + u)
                    if kind in ("C", "G"):
                        kt, rh, rl = (KT, xh, xl) if kind == "C" else (4, yh, yl)
                        for k in range(kt):
                            if u == U_GL and g == 0:
                                pe.wait_ge(S["gy_hi"], 4 * l + k + 1)
                                pe.wait_ge(S["gy_lo"], 4 * l + k + 1)
                            for n in range(2):
                                w0, x0 = 256 * k + 128 * g, T * k + 512 * n
                                last = mm3(gp[g][:, 512 * n:512 * n + 512], wh[:, w0:w0 + 128], wl[:, w0:w0 + 128],
                                           rh[:, x0:x0 + 512], rl[:, x0:x0 + 512], k == 0, k == kt - 1)
                    elif kind == "MC":
                        for k in range(KT):
                            w0 = 256 * k + 128 * g
                            last = mm3(gp[g][:, 0:256], wh[:, w0:w0 + 128], wl[:, w0:w0 + 128],
                                       memh[:, NMEM * k:NMEM * k + NMEM], meml[:, NMEM * k:NMEM * k + NMEM], k == 0, k == KT - 1)
                    else:
                        for c in range(1 if kind == "MT" else 4):
                            for k in range(KT):
                                if kind == "MT":
                                    ah, al, a0 = memh, meml, NMEM * k + 128 * g
                                else:
                                    ah, al, a0 = xh, xl, T * k + 128 * (4 * g + c)
                                last = mm3(gp[g][:, 256 * c:256 * c + 256], ah[:, a0:a0 + 128], al[:, a0:a0 + 128],
                                           wh[:, 256 * k:256 * k + 256], wl[:, 256 * k:256 * k + 256], k == 0, k == KT - 1)
                    last.then_inc(g_done[g], 1)

            def transposes(l, first, src, used):
                for g in range(2):
                    pe.wait_ge(gate_used[g], NGATE * l + used)
                for i in range(8):
                    j, half, n = i // 2, i % 2, first + i
                    if i >= 2:
                        pe.wait_ge(S["tr_free"], 16 * l + n - 1)
                    for c in range(4):
                        a0 = GW * (4 * half + c) + 128 * j
                        last = nc.tensor.transpose(bank[i % 2][:, 128 * c:128 * c + 128], src[:, a0:a0 + 128], ident)
                    last.then_inc(S["tr_done"], 1)

            with pe.Fori(0, DEPTH) as l:
                pe.wait_ge(S["mem_lo"], l + 1)
                for u in range(U_MK, U_QK):
                    unit(l, u)
                pe.wait_ge(S["xn_in"], 16 * NC)
                pe.wait_ge(S["x_rows"], NC * l + 1)
                for i in range(16):
                    half, k = i // 8, i % 8
                    if i >= 4:
                        pe.wait_ge(S["xT_hi"], 16 * l + i - 3)
                        pe.wait_ge(S["xT_lo"], 16 * l + i - 3)
                    for c in range(4):
                        last = nc.tensor.transpose(bank[i % 4][:, 128 * c:128 * c + 128], xr[4 * half + c][:, 128 * k:128 * k + 128],
                                                   ident)
                    last.then_inc(S["xt_done"], 1)
                pe.wait_ge(S["xT_hi"], 16 * l + 16)
                pe.wait_ge(S["xT_lo"], 16 * l + 16)
                for u in range(U_QK, U_RZ):
                    unit(l, u)

                pe.wait_ge(S["qk2_in"], 128 * l + 128)
                v = rv

                def r_scores(c):
                    if c:
                        pe.wait_ge(S["r_att"], NC * l + c)
                        pe.wait_ge(S["r_kn"], NC * l + c)
                    for h in range(HEADS):
                        p, r0 = h // 2, 64 * (h % 2)
                        nc.tensor.matmul(bank[h % 2][:, 128 * p:128 * p + 128],
                                         qk2[r0:r0 + 64, 2048 * p + T + 128 * c:2048 * p + T + 128 * c + 128],
                                         qk2[r0:r0 + 64, 2048 * p + 128 * c:2048 * p + 128 * c + 128], start=True, stop=True)
                    for p in range(2):
                        last = nc.tensor.transpose(bank[1][:, 256 + 128 * p:256 + 128 * p + 128],
                                                   qk2[:, 2048 * p + T + 128 * c:2048 * p + T + 128 * c + 128], ident)
                    last.then_inc(S["r_sc"], 1)

                r_scores(0)
                for c in range(NC):
                    if c + 1 < NC:
                        r_scores(c + 1)
                    pe.wait_ge(S["r_att"], NC * l + c + 1)
                    if c:
                        pe.wait_ge(S["r_ho"], NC * l + c)
                        pe.wait_ge(S["r_state"], NC * l + c)
                    for h in range(HEADS):
                        p, r0 = h // 2, 64 * (h % 2)
                        o = bank[2][:, 128 * h:128 * h + 128]
                        last = nc.tensor.matmul(o, att[c % 2][:, 256 * (h % 2) + 128 * p:256 * (h % 2) + 128 * p + 128], v[:, GW * c + 128 * h:GW * c + 128 * h + 128],
                                                start=True, stop=c == 0)
                        if c:
                            last = nc.tensor.matmul(o, qk2[:, 2048 * p + 128 * c:2048 * p + 128 * c + 128],
                                                    sret[:, 128 * h:128 * h + 128], start=False, stop=True)
                    last.then_inc(S["r_o"], 1)
                    pe.wait_ge(S["r_kn"], NC * l + c + 1)
                    if c:
                        pe.wait_ge(S["r_state"], NC * l + c)
                    for h in range(HEADS):
                        p, r0 = h // 2, 64 * (h % 2)
                        last = nc.tensor.matmul(bank[3][r0:r0 + 64, 128 * p:128 * p + 128], kn[c % 2][:, DK * h:DK * h + DK],
                                                v[:, GW * c + 128 * h:GW * c + 128 * h + 128], start=True, stop=True)
                    last.then_inc(S["r_u"], 1)
                unit(l, U_RZ)
                unit(l, U_RZ + 1)

                def x_scores(i):
                    h, half = i // 2, i % 2
                    if i >= 2:
                        pe.wait_ge(S["x_e"], 4 * (8 * l + i - 1))
                    for c in range(4):
                        a0 = T * h + 512 * half + 128 * c
                        last = nc.tensor.matmul(gp[i % 2][:, 256 * c:256 * c + 256], aq[:, a0:a0 + 128], mkT[:, NMEM * h:NMEM * h + NMEM],
                                                start=True, stop=True)
                    last.then_inc(S["x_s"], 1)

                def x_values(i):
                    h = i // 2
                    pe.wait_ge(S["x_pt"], 8 * l + i + 1)
                    for m in range(2):
                        last = nc.tensor.matmul(mm[i % 2][:, 0:512], mvT[:, GW * m + 128 * h:GW * m + 128 * h + 128],
                                                pt[i % 2][:, 512 * m:512 * m + 512], start=m == 0, stop=m == 1)
                    last.then_inc(S["x_pv"], 1)

                for g in range(2):
                    pe.wait_ge(g_free[g], NUNIT * l + U_RZ + 2)
                pe.wait_ge(S["r_ho"], NC * l + NC)
                pe.wait_ge(S["r_state"], NC * l + NC)
                x_scores(0)
                x_scores(1)
                for i in range(8):
                    pe.wait_ge(S["x_norm"], 8 * l + i + 1)
                    if i >= 2:
                        pe.wait_ge(S["x_pvev"], 8 * l + i - 1)
                    for m in range(2):
                        for c in range(4):
                            last = nc.tensor.transpose(mm[i % 2][:, 512 * m + 128 * c:512 * m + 128 * c + 128],
                                                       pm[i % 2][:, 256 * c + 128 * m:256 * c + 128 * m + 128], ident)
                    last.then_inc(S["x_t"], 1)
                    if i < 6:
                        x_scores(i + 2)
                    if i:
                        x_values(i - 1)
                x_values(7)
                pe.wait_ge(S["x_e"], 32 * (l + 1))
                pe.wait_ge(S["x_pvev"], 8 * l + 8)
                transposes(l, 0, hr, 2)
                unit(l, U_AZ)
                pe.wait_ge(S["wif_hi"], l + 1)
                pe.wait_ge(S["wif_lo"], l + 1)
                pe.wait_ge(S["tr_free"], 16 * l + 8)
                for n in range(2):
                    for k in range(KT):
                        last = mm3(mm[1][:, 512 * n:512 * n + 512], wifh[:, 128 * k:128 * k + 128], wifl[:, 128 * k:128 * k + 128],
                                   xh[:, T * k + 512 * n:T * k + 512 * n + 512], xl[:, T * k + 512 * n:T * k + 512 * n + 512],
                                   k == 0, k == KT - 1)
                last.then_inc(S["if_done"], 1)
                unit(l, U_AZ + 1)

                for u in range(U_MX, U_LO):
                    unit(l, u)
                pe.wait_ge(S["rows_done"], l + 1)
                for c in range(NC):
                    last = nc.tensor.transpose(mm[0][:, 128 * c:128 * c + 128], rk[:, 128 * c:128 * c + 128], ident)
                last.then_inc(S["colt_done"], 1)
                for h in range(HEADS):
                    last = nc.tensor.matmul(bank[2][:, NC * h:NC * h + NC], cst[0:4, K_ONE + 128 * h:K_ONE + 128 * h + 128],
                                            small[0:4, 16:24], start=True, stop=True)
                last.then_inc(S["colt_done"], 1)
                pe.wait_ge(S["cols_done"], 5 * l + 5)
                for i in range(8):
                    h, half = i // 2, i % 2
                    if i >= 2:
                        pe.wait_ge(S["w_arg"], 8 * l + i - 1)
                    nc.tensor.matmul(bank[i % 2], cst[0:4, K_ONE + 128 * h:K_ONE + 128 * h + 128],
                                     rowf[0:4, 512 * half:512 * half + 512], start=True, stop=True).then_inc(S["a_bc"], 1)
                pe.wait_ge(S["wqk_in"], 16 * l + 16)
                for i in range(16):
                    w, h, half = i // 8, i // 2 % 4, i % 2
                    pe.wait_ge(S["xc_ready"], 4 * l + h + 1)
                    if i >= 2:
                        pe.wait_ge(S["qk_ev"], 16 * l + i - 1)
                    nc.tensor.matmul(bank[2 + i % 2], wqk[:, 512 * w + 128 * h:512 * w + 128 * h + 128],
                                     xc[:, T * h + 512 * half:T * h + 512 * half + 512], start=True, stop=True).then_inc(S["qk_mm"], 1)
                pe.wait_ge(S["qk_ev"], 16 * l + 16)
                pe.wait_ge(S["w_arg"], 8 * l + 8)
                for c in range(NC):
                    if c >= 2:
                        pe.wait_ge(S["s_w"], NC * l + c - 1)
                    for h in range(HEADS):
                        a0 = 512 * c + 128 * h
                        last = nc.tensor.matmul(bank[c % 2][:, 128 * h:128 * h + 128], kTt[:, a0:a0 + 128], qT[:, a0:a0 + 128],
                                                start=True, stop=True)
                    last.then_inc(S["s_mm"], 1)
                pe.wait_ge(S["ones_done"], l + 1)
                pe.wait_ge(g_free[0], NUNIT * l + U_LO)
                pe.wait_ge(g_free[1], NUNIT * l + U_LO)
                pe.wait_ge(S["s_w"], NC * l + NC)

                def k_natural(c):
                    if c:
                        pe.wait_ge(S["k_w"], NC * l + c)
                    for h in range(HEADS):
                        last = nc.tensor.transpose(bank[3][:, 128 * h:128 * h + 128], kTt[:, 512 * c + 128 * h:512 * c + 128 * h + 128], ident)
                    last.then_inc(S["k_tr"], 1)

                k_natural(0)
                for c in range(NC):
                    if c + 1 < NC:
                        k_natural(c + 1)
                    if c:
                        pe.wait_ge(S["m_read"], NC * l + c)
                    for h in range(HEADS):
                        a0, o0, v0 = 512 * c + 128 * h, 512 * (h // 2) + 129 * (h % 2), 129 * (HEADS * c + h)
                        last = nc.tensor.matmul(gp[0][:, o0:o0 + 129], wt[:, a0:a0 + 128], va[:, v0:v0 + 129], start=True, stop=True)
                    if c:
                        pe.wait_ge(S["m_st"], NC * l + c)
                        for h in range(HEADS):
                            a0, o0 = 512 * c + 128 * h, 512 * (h // 2) + 129 * (h % 2)
                            last = nc.tensor.matmul(gp[1][:, o0:o0 + 129], qT[:, a0:a0 + 128], cst8[:, 129 * h:129 * h + 129],
                                                    start=True, stop=True)
                    last.then_inc(S["m_num"], 1)
                    pe.wait_ge(S["k_w"], NC * l + c + 1)
                    if c:
                        pe.wait_ge(S["m_st"], NC * l + c)
                    for h in range(HEADS):
                        o0, v0 = 512 * (h // 2) + 129 * (h % 2), 129 * (HEADS * c + h)
                        last = nc.tensor.matmul(mm[0][:, o0:o0 + 129], kw[c % 2][:, 128 * h:128 * h + 128], va[:, v0:v0 + 129],
                                                start=True, stop=True)
                    last.then_inc(S["m_c"], 1)
                pe.wait_ge(S["m_read"], NC * l + NC)
                pe.wait_ge(S["m_st"], NC * l + NC)
                for u in range(U_LO, U_SZ + 2):
                    unit(l, u)
                    if u == U_SU + 1:
                        pe.wait_ge(S["p_ev"], NPB * l + 4)
                        pe.wait_ge(S["p_ke"], NPB * l + 4)
                        transposes(l, 8, hm, 8)
                    for q in TABLES_AT.get(u - 1, ()):
                        tables(l, q)

                pe.wait_ge(S["uu_in"], 128 * l + 128)
                pe.wait_ge(S["tr_free"], 16 * l + 16)

                def s_inputs(b):
                    pe.wait_ge(tb_in[b % SLOTS], 48 * ((NBATCH // SLOTS) * l + b // SLOTS) + 48)
                    if b:
                        pe.wait_ge(S["s_gr"], NBATCH * l + b)
                    for g in range(GB):
                        for w in range(2):
                            a0 = GCOLS * g + TG + 64 * w
                            last = nc.tensor.matmul(bank[w][:, 128 * g:128 * g + 128], tb[b % SLOTS][:, a0:a0 + 128],
                                                    uu[:, 128 * (GB * b + g):128 * (GB * b + g) + 128], start=True, stop=True)
                    last.then_inc(S["s_g"], 1)

                s_inputs(0)
                for b in range(NBATCH):
                    if b + 1 < NBATCH:
                        s_inputs(b + 1)
                    pe.wait_ge(S["s_z"], NBATCH * l + b + 1)
                    if b >= 2:
                        pe.wait_ge(S["s_ye"], NBATCH * l + b - 1)
                    for g in range(GB):
                        t = tb[b % SLOTS][:, GCOLS * g:GCOLS * g + GCOLS]
                        o = bank[2 + b % 2][:, 128 * g:128 * g + 128]
                        nc.tensor.matmul(o, t[:, TTOP:TTOP + 128],
                                         uu[:, 128 * (GB * b + g):128 * (GB * b + g) + 128], start=True, stop=False)
                        nc.tensor.matmul(o, t[:, TH:TH + 128], zc[b % 2][:, 128 * g:128 * g + 128], start=False, stop=False)
                        last = nc.tensor.matmul(o, t[:, TH2:TH2 + 128], zs[b % 2][:, 128 * g:128 * g + 128],
                                                start=False, stop=True)
                    last.then_inc(S["s_y"], 1)
                unit(l, U_GL)
                unit(l, U_GL + 1)

                op = gp + mm
                pe.wait_ge(g_free[0], NUNIT * l + NUNIT)
                pe.wait_ge(g_free[1], NUNIT * l + NUNIT)
                pe.wait_ge(S["s_ye"], NBATCH * l + NBATCH)
                for j in range(NOUT):
                    hf, ki, n = j // 8, j % 8 // 2, j % 2
                    u = NUNIT + j
                    if ki < 3:
                        order = [(cc, j) for cc in range(4)]
                    elif n == 0:
                        order = [(cc, j + i) for cc in range(4) for i in range(2)]
                        pe.wait_ge(S["lo_done"], l * HALVES + half0(u + 1) + 2)
                    else:
                        continue
                    pe.wait_ge(S["lo_done"], l * HALVES + half0(u) + 2)
                    pe.wait_ge(S["oy_hi"], 16 * l + 8 * hf + 2 * ki + 2)
                    pe.wait_ge(S["oy_lo"], 16 * l + 8 * hf + 2 * ki + 2)
                    for cc, jj in order:
                        n, kq, u = jj % 2, KQ[ki], NUNIT + jj
                        if hf and ki == 0 and n == 0:
                            pe.wait_ge(S["o_free"], NC * l + cc + 1)
                        for k in range(4):
                            y0, w0 = 512 * (4 * kq + k) + 128 * cc, 512 * k
                            last = mm3(op[cc][:, 512 * n:512 * n + 512], oyh[:, y0:y0 + 128], oyl[:, y0:y0 + 128],
                                       whi[slot(u)][:, w0:w0 + 512], wlo[slot(u)][:, w0:w0 + 512], ki == 0 and k == 0, ki == 3 and k == 3)
                        if cc == 3:
                            last.then_inc(S["o_used"], 1)
                        elif ki == 3 and n == 1:
                            last.then_inc(S["o_done"], 1)
                pe.wait_ge(S["o_free"], NC * (l + 1))

        @block.gpsimd
        def _(pool):
            def lo(l, u):
                for i in range(nhalf(u)):
                    n = half0(u) + i
                    pool.wait_ge(S["hi_done"], l * HALVES + n + 1)
                    nc.gpsimd.tensor_tensor(wlo[slot(u)][:, 1024 * i:1024 * i + 1024], wraw[n % 2],
                                            whi[slot(u)][:, 1024 * i:1024 * i + 1024].bitcast(F32), ALU.subtract).then_inc(S["lo_done"], 1)

            nc.gpsimd.memset(p_zero[:, 0:112 * G5], 0.0).then_inc(S["zeroed"], 1)
            pool.wait_ge(S["zeroed"], 1)
            pool.dma_start(bass.AP(dram["kd"].tensor, 0, [[240, C5], [C5 * 240, G5], [1, 112]]),
                           p_zero[:, 0:112 * G5].rearrange("c (g z) -> c g z", z=112)).then_inc(S["kd_zeroed"], 16)
            pool.wait_ge(S["kd_zeroed"], 16)
            with pool.Fori(0, DEPTH) as l:
                for u in range(U_LO + 1):
                    lo(l, u)
                for c in range(NC):
                    pool.wait_ge(S["w_exp"], NC * l + c + 1)
                    w = wt[:, 512 * c:512 * c + 512].rearrange("p (h t) -> p h t", h=HEADS)
                    nc.gpsimd.tensor_tensor(w, w, bcast(cst[:, K_CAUS:K_CAUS + 128], HEADS, 0), ALU.mult).then_inc(S["w_mask"], 1)
                for u in range(U_LO + 1, NUNIT + NOUT):
                    lo(l, u)
                    for q in TABLES_AT.get(u - 1, ()):
                        n = NPB * l + q
                        if q == 0:
                            pool.wait_ge(S["co_in"], 32 * l + 32)
                        pool.wait_ge(bc_in[q % 2], 64 * l + 16 * (q // 2) + 16)
                        if q >= 2:
                            pool.wait_ge(S["p_k"], n - 1)
                        if q:
                            pool.wait_ge(S["p_w"], n)
                        w = view(p_w[q % 2], BS)
                        nc.gpsimd.tensor_tensor(w, part(SX, BS, q), chan(q, 0, BS), ALU.mult)
                        nc.gpsimd.tensor_tensor(view(p_t3, BS), part(SY, BS, q), chan(q, 1, BS), ALU.mult).then_inc(S["p_prod"], 1)
                        pool.wait_ge(S["p_prod"], n + 1)
                        nc.gpsimd.tensor_tensor(w, w, view(p_t3, BS), ALU.add).then_inc(S["p_w"], 1)

        @block.scalar
        def _(act):
            A = Steps(act, S["a_step"], steps_a)
            A.layer, A.base = 0, 0
            F = nc.scalar.activation

            act.wait_ge(S["c_in"], 16)
            act.wait_ge(S["mem_in"], 16)
            act.wait_ge(S["kd_zeroed"], 16)
            for c in range(NC):
                act.dma_start(xr[c], dram["x"][128 * c:128 * c + 128, :]).then_inc(S["xn_in"], 16)
            act.wait_ge(S["rope_ang"], 1)
            A.link(F(rp[:, 2048:3072], rp[:, 0:1024], ACT.Abs))
            A.link(F(rp[:, 3072:4096], rp[:, 2048:3072], ACT.Sin, scale=-1.0, bias=misc(M_HPI)))
            F(rp[:, 1024:2048], rp[:, 0:1024], ACT.Sin).then_inc(S["rope_sc"], 1)
            act.wait_ge(S["rope_sc"], 1)
            act.dma_start(dram["ropetab"][:, 0:1024], rp[:, 3072:4096]).then_inc(S["rope_st"], 16)
            act.dma_start(dram["ropetab"][:, 1024:2048], rp[:, 1024:2048]).then_inc(S["rope_st"], 16)
            act.dma_start(dram["xs"][0], dram["x"]).then_inc(S["cp_out"], 16)
            A.base = A.n

            def tables(l, q):
                n = NPB * l + q
                tab = p_tab[q % 2].rearrange("p (g n) -> p g n", g=GP)
                co, si = tab[:, :, TCOS:TCOS + NBT], tab[:, :, TSIN:TSIN + NBT]
                act.wait_ge(S["p_tr"], n + 1)
                bk = bank[2 - 2 * (q % 2)].rearrange("p (g n) -> p g n", g=GP)
                A.inc(F(tab[:, :, TG:TG + 128], bk, ACT.Copy))
                F(tab[:, :, TG + 128:TG + 192], bk[:, :, 0:64], ACT.Copy).then_inc(S["p_ev"], 1)
                act.wait_ge(S["p_ang"], n + 1)
                A.link(F(co, si, ACT.Abs))
                A.inc(F(co, co, ACT.Sin, scale=-TURN, bias=misc(M_HPI)))
                A.inc(F(si, si, ACT.Sin, scale=misc(M_TURN)))
                act.wait_ge(S["p_h0"], n + 1)
                F(tab[:, :, TH:TH + 128], p_h0[q % 2].rearrange("p (g n) -> p g n", g=GP)[:, :, C5:144], ACT.Copy).then_inc(S["p_hc"], 1)
                A.join()
                act.wait_ge(S["p_ev"], n + 1)
                act.wait_ge(S["p_hc"], n + 1)
                act.wait_ge(S["p_ke"], n + 1)
                act.dma_start(dram["tabs"][GP * q:GP * q + GP].rearrange("g p n -> p g n"), tab).then_inc(tab_out[q % 2], 16)
                act.dma_start(dram["kd"].rearrange("g c n -> c g n")[:, GP * q:GP * q + GP, 112:240],
                              p_ks.rearrange("c (g n) -> c g n", g=GP)).then_inc(S["ks_out"], 16)

            def split(l, u):
                if 2 <= u < NUNIT + 2:
                    act.wait_ge(g_done[1], NUNIT * l + u - 1)
                elif u == NUNIT + 2:
                    act.wait_ge(g_done[1], NUNIT * l + NUNIT)
                elif u > NUNIT + 2:
                    act.wait_ge(S["o_used"], NOUT * l + u - 3 - NUNIT + 1)
                for i in range(nhalf(u)):
                    n = half0(u) + i
                    act.wait_ge(raw_in[n % 2], 16 * ((HALVES // 2) * l + n // 2 + 1))
                    F(whi[slot(u)][:, 1024 * i:1024 * i + 1024], wraw[n % 2], ACT.Copy).then_inc(S["hi_done"], 1)

            def take_out(l, u, fn):
                split(l, u + 1)
                for g in range(2):
                    act.wait_ge(g_done[g], NUNIT * l + u + 1)
                    fn(u, g).then_inc(g_free[g], 1)

            def gates(l, u, n, func, scale=1.0):
                split(l, u + 1)
                for g in range(2):
                    act.wait_ge(g_done[g], NUNIT * l + u + 1)
                    if n:
                        act.wait_ge(gate_used[g], NGATE * l + n)
                    F(gate[g], gp[g], func, scale=scale).then_inc(g_free[g], 1)

            def store_tiles(l, first, tile0):
                for i in range(8):
                    j, half, n = i // 2, i % 2, first + i
                    act.wait_ge(S["tr_done"], 16 * l + n + 1)
                    if n >= 4:
                        act.wait_ge(ys_out[i % 4], 16 * (4 * l + n // 4))
                    F(ystage[first // 8][i % 4], bank[i % 2], ACT.Copy).then_inc(S["tr_free"], 1)
                    act.wait_ge(S["tr_free"], 16 * l + n + 1)
                    act.dma_start(dram["yt"][tile0 + j, :, 512 * half:512 * half + 512], ystage[first // 8][i % 4]).then_inc(ys_out[i % 4], 16)

            with act.Fori(0, DEPTH) as l:
                A.begin(l)
                act.wait_ge(S["mem_in"], 16 * l + 16)
                F(memh, memraw, ACT.Copy).then_inc(S["mem_hi"], 1)
                split(l, 0)
                for u in (U_MK, U_MK + 1):
                    take_out(l, u, lambda u, g: F(mkT[:, NMEM * (2 * (u - U_MK) + g):NMEM * (2 * (u - U_MK) + g) + NMEM],
                                                  gp[g][:, 0:NMEM], ACT.Copy))
                for u in (U_MV, U_MV + 1):
                    take_out(l, u, lambda u, g: F(mvT[:, GW * g + 256 * (u - U_MV):GW * g + 256 * (u - U_MV) + 256],
                                                  gp[g][:, 0:256], ACT.Copy))
                for i in range(16):
                    half, k = i // 8, i % 8
                    act.wait_ge(S["xt_done"], 16 * l + i + 1)
                    F(xh[:, T * k + 512 * half:T * k + 512 * half + 512], bank[i % 4], ACT.Copy).then_inc(S["xT_hi"], 1)
                for u in (U_QK, U_QK + 1):
                    take_out(l, u, lambda u, g: F(qk[:, T * (2 * (u - U_QK) + g):T * (2 * (u - U_QK) + g) + T], gp[g], ACT.Copy))
                act.wait_ge(S["s_pow"], l + 1)
                A.link(F(s_cos, s_ang, ACT.Abs))
                A.link(F(s_cos, s_cos, ACT.Sin, scale=-1.0, bias=misc(M_HPI)))
                F(s_sin, s_ang, ACT.Sin).then_inc(S["s_sc"], 1)
                for u in (U_RV, U_RV + 1):
                    take_out(l, u, lambda u, g: F(tview(rv, GW, g, u - U_RV), gp[g].rearrange("p (c n) -> p c n", c=4), ACT.Copy))
                for u in (U_AQ, U_AQ + 1):
                    take_out(l, u, lambda u, g: F(aq[:, T * (2 * (u - U_AQ) + g):T * (2 * (u - U_AQ) + g) + T], gp[g], ACT.Copy))
                act.wait_ge(S["s_made"], l + 1)
                act.dma_start(dram["s5co"], s_co).then_inc(S["co_out"], 16)
                act.wait_ge(S["hn_var"], 2 * l + 1)
                F(sd[:, 0:32], mv.rearrange("p (n k) -> p n k", k=2)[:, :, 1], ACT.Sqrt, bias=misc(M_GNE)).then_inc(S["hn_sd"], 1)
                gates(l, U_RZ, 0, ACT.Silu)
                gates(l, U_RZ + 1, 1, ACT.Silu)

                def x_exp(i):
                    act.wait_ge(S["x_max"], 8 * l + i + 1)
                    if i >= 2:
                        act.wait_ge(S["x_t"], 8 * l + i - 1)
                    for c in range(4):
                        s0 = 16 * (i % 2)
                        F(pm[i % 2][:, 256 * c:256 * c + 256], gp[i % 2][:, 256 * c:256 * c + 256], ACT.Exp, scale=128 ** -0.5,
                          bias=small[:, s0 + 4 + c:s0 + 5 + c], accum_out=small[:, s0 + 8 + c:s0 + 9 + c]).then_inc(S["x_e"], 1)

                def x_out(i):
                    h, half = i // 2, i % 2
                    act.wait_ge(S["x_pv"], 8 * l + i + 1)
                    F(xo[:, T * h + 512 * half:T * h + 512 * half + 512], mm[i % 2][:, 0:512], ACT.Copy).then_inc(S["x_pvev"], 1)

                x_exp(0)
                for i in range(8):
                    if i < 7:
                        x_exp(i + 1)
                    act.wait_ge(S["x_t"], 8 * l + i + 1)
                    if i >= 2:
                        act.wait_ge(S["x_pv"], 8 * l + i - 1)
                    F(pt[i % 2], mm[i % 2], ACT.Copy).then_inc(S["x_pt"], 1)
                    if i:
                        x_out(i - 1)
                x_out(7)
                store_tiles(l, 0, 0)
                act.wait_ge(S["wif_in"], 16 * l + 16)
                F(wifh, wifr, ACT.Copy).then_inc(S["wif_hi"], 1)
                gates(l, U_AZ, 2, ACT.Silu)
                act.wait_ge(S["if_done"], l + 1)
                act.wait_ge(S["bias_in"], 16 * l + 16)
                F(rowi[0:4, :], mm[1][0:4, :], ACT.Identity, bias=small[0:4, 48:49]).then_inc(S["if_act"], 1)
                A.link(F(rowb[0:4, :], mm[1][32:36, :], ACT.Identity, bias=small[0:4, 49:50]))
                A.link(F(rowm[0:4, :], rowb[0:4, :], ACT.Abs))
                A.link(F(rowm[0:4, :], rowm[0:4, :], ACT.Exp, scale=-1.0))
                F(rowm[0:4, :], rowm[0:4, :], ACT.Ln, bias=misc(M_ONE, 1, 4)).then_inc(S["if_act"], 1)
                gates(l, U_AZ + 1, 3, ACT.Silu)
                for j in range(4):
                    act.wait_ge(gate_used[j % 2], NGATE * l + 3 + j // 2)
                    act.dma_start(dram["yt"][12 + j], xo[:, T * j:T * j + T]).then_inc(S["xa_out"], 16)
                for u in (U_MX, U_MX + 1):
                    take_out(l, u, lambda u, g: F(mx[:, (T + 3) * (2 * (u - U_MX) + g) + 3:(T + 3) * (2 * (u - U_MX) + g) + 3 + T], gp[g], ACT.Copy))
                for h in range(HEADS):
                    act.wait_ge(S["conv_done"], 4 * l + h + 1)
                    F(xc[:, T * h:T * h + T], xc[:, T * h:T * h + T], ACT.Silu).then_inc(S["xc_ready"], 1)
                vview = va.rearrange("p (c h e) -> p c h e", c=NC, h=HEADS)
                for u in (U_LV, U_LV + 1):
                    h0 = 2 * (u - U_LV)
                    take_out(l, u, lambda u, g: F(vview[:, 4 * g:4 * g + 4, h0:h0 + 2, 0:128],
                                                  gp[g].rearrange("p (c h e) -> p c h e", c=4, h=2), ACT.Copy))
                act.wait_ge(S["colt_done"], 2 * l + 2)
                src = mm[0].rearrange("p (c x) -> p c x", c=NC)
                for k in range(4):
                    F(cols[:, 32 * k:32 * k + 32].rearrange("p (c h) -> p c h", c=NC), src[:, :, 32 * k:32 * k + 4],
                      ACT.Exp if k else ACT.Copy).then_inc(S["cols_done"], 1)
                F(dec, bank[2][:, 0:32], ACT.Exp).then_inc(S["cols_done"], 1)
                for c in range(NC):
                    act.wait_ge(S["w_arg"], 8 * l + 8)
                    F(wt[:, 512 * c:512 * c + 512], wt[:, 512 * c:512 * c + 512], ACT.Exp).then_inc(S["w_exp"], 1)
                act.wait_ge(S["xa_out"], 64 * l + 64)
                for i in range(16):
                    w, h, half = i // 8, i // 2 % 4, i % 2
                    act.wait_ge(S["qk_mm"], 16 * l + i + 1)
                    dst = (kTt if w else qT).rearrange("p (c h t) -> p c h t", c=NC, h=HEADS)[:, 4 * half:4 * half + 4, h, :]
                    F(dst, bank[2 + i % 2].rearrange("p (c t) -> p c t", c=4), ACT.Copy, scale=128 ** -0.5 if w else 1.0).then_inc(S["qk_ev"], 1)
                gates(l, U_LO, 4, ACT.Tanh, 0.5)
                gates(l, U_LO + 1, 5, ACT.Tanh, 0.5)
                tables(l, 0)
                act.wait_ge(S["hn_var"], 2 * l + 2)
                F(sd[:, 0:32], mv.rearrange("p (n k) -> p n k", k=2)[:, :, 1], ACT.Sqrt, bias=misc(M_GNE)).then_inc(S["hn_sd"], 1)
                gates(l, U_LZ, 6, ACT.Silu)
                gates(l, U_LZ + 1, 7, ACT.Silu)
                tables(l, 1)
                for u in (U_SU, U_SU + 1):
                    take_out(l, u, lambda u, g: F(us[:, T * (2 * (u - U_SU) + g):T * (2 * (u - U_SU) + g) + T].rearrange("p (s j) -> p j s", s=BS),
                                                  gp[g].rearrange("p (j s) -> p j s", s=BS), ACT.Copy))
                    for m in range(2 * (u - U_SU), 2 * (u - U_SU) + 2):
                        act.wait_ge(g_free[m % 2], NUNIT * l + u + 1)
                        act.dma_start(dram["ud"][128 * m:128 * m + 128, :], us[:, T * m:T * m + T]).then_inc(S["ud_out"], 16)
                    if u == U_SU + 1:
                        store_tiles(l, 8, 8)
                    for q in TABLES_AT[u - 1]:
                        tables(l, q)

                def s_gate(u):
                    take_out(l, u, lambda u, g: F(sz[:, T * (2 * (u - U_SZ) + g):T * (2 * (u - U_SZ) + g) + T].rearrange("p (s j) -> p j s", s=BS),
                                                  gp[g].rearrange("p (j s) -> p j s", s=BS), ACT.Silu))

                s_gate(U_SZ)
                for q in TABLES_AT[U_SZ - 1]:
                    tables(l, q)
                s_gate(U_SZ + 1)

                def gelu(m):
                    act.wait_ge(S[f"yc_in{m}"], 16 * l + 16)
                    A.inc(F(yc[m], yc[m], ACT.Gelu_apprx_tanh))

                for b in range(NBATCH):
                    act.wait_ge(S["s_y"], NBATCH * l + b + 1)
                    F(yb[:, 256 * b:256 * b + 256], bank[2 + b % 2][:, 0:256], ACT.Copy).then_inc(S["s_ye"], 1)
                    if b % 4 == 3:
                        m = b // 4
                        act.wait_ge(S["s_ye"], NBATCH * l + b + 1)
                        for t in range(BS):
                            dst = dram["yd"][128 * m:128 * m + 128, :].rearrange("(g c) (t j) -> t c g j", c=C5, t=BS)[t]
                            src = yb[C5 * t:C5 * t + C5, T * m:T * m + T].rearrange("c (g j) -> c g j", g=8)
                            act.dma_start(dst, src).then_inc(S[f"yd_out{m}"], 16)
                    if b == 12:
                        gelu(0)

                def yhi(n):
                    act.wait_ge(y_in[n % 2], 16 * (8 * l + n // 2 + 1))
                    if n >= 8:
                        act.wait_ge(S["o_used"], NOUT * l + 2 * (n % 8 // 2) + 2)
                    y0 = 1024 * (2 * KQ[n % 8 // 2] + n % 2)
                    F(oyh[:, y0:y0 + 1024], yraw[n % 2], ACT.Copy).then_inc(S["oy_hi"], 1)

                for m in range(4):
                    if m:
                        gelu(m)
                    A.join()
                    F(yh[:, T * m:T * m + T], yc[m], ACT.Copy).then_inc(S["gy_hi"], 1)
                yhi(0)
                yhi(1)
                gates(l, U_GL, 8, ACT.Tanh, 0.5)
                yhi(2)
                yhi(3)
                gates(l, U_GL + 1, 9, ACT.Tanh, 0.5)
                yhi(4)
                yhi(5)
                for m in range(4):
                    act.wait_ge(gate_used[m % 2], NGATE * l + 9 + m // 2)
                    act.dma_start(dram["yt"][4 + m], s5o[m % 2]).then_inc(s5_out[m % 2], 16)

                def norm(c):
                    act.wait_ge(S["ln_var"], NC * l + c + 1)
                    F(sd[:, 32:33], mv[:, 33:34], ACT.Sqrt, bias=misc(M_LNE)).then_inc(S["ln_sd"], 1)

                for j in range(NOUT):
                    if j == 0:
                        split(l, NUNIT + 1)
                        split(l, NUNIT + 2)
                        yhi(6)
                        yhi(7)
                        act.wait_ge(S["cp_out"], 16)
                        act.dma_start(lng, bass.AP(dram["lng"].tensor, l * D, [[0, 128], [1, D]])).then_inc(S["ln_in"], 16)
                        act.dma_start(lnb, bass.AP(dram["lnb"].tensor, l * D, [[0, 128], [1, D]])).then_inc(S["ln_in"], 16)
                        for c in range(NC):
                            act.dma_start(xr[c], dram["xs"][l, 128 * c:128 * c + 128, :]).then_inc(S["xr_in"], 16)
                    elif j in (2, 4, 6):
                        yhi(j + 6)
                        yhi(j + 7)
                    if j == 7:
                        for c in range(3):
                            norm(c)
                    if 0 < j < NOUT - 2:
                        split(l, NUNIT + j + 2)
                    if j == 7:
                        norm(3)
                    if j == 8:
                        yhi(14)
                        yhi(15)
                for c in range(4, NC):
                    norm(c)

        @block.vector
        def _(dve):
            V = Steps(dve, S["v_step"], steps_v)
            V.layer = 0
            TT, TS, STT = nc.vector.tensor_tensor, nc.vector.tensor_scalar, nc.vector.scalar_tensor_tensor

            def reduce_angle(link, x, k):
                link(TS(k, x, 1.0 / TWO_PI, MAGIC, ALU.mult, ALU.add))
                link(TS(k, k, MAGIC, None, ALU.subtract))
                for part in (C1, C2, C3):
                    link(STT(x, k, -part, x, ALU.mult, ALU.add))
                return TS(x, x, PI_LO, -PI_LO, ALU.min, ALU.max)

            def exp_(x, out, t):
                V.link(TS(x, x, -200.0, 200.0, ALU.max, ALU.min))
                V.link(TS(t, x, 1.0 / math.log(2.0), MAGIC, ALU.mult, ALU.add))
                V.link(TS(t, t, MAGIC, None, ALU.subtract))
                V.link(STT(x, t, -0.693359375, x, ALU.mult, ALU.add))
                V.link(STT(x, t, 2.12194440054690583e-4, x, ALU.mult, ALU.add))
                coef = [1 / math.factorial(n) for n in range(9)]
                V.link(TS(out, x, coef[8], coef[7], ALU.mult, ALU.add))
                for n in range(6, -1, -1):
                    V.link(TT(out, out, x, ALU.mult))
                    V.link(TS(out, out, coef[n], None, ALU.add))
                V.link(TS(t, t, -127.0, 128.0, ALU.max, ALU.min))
                V.link(TS(t, t, 127.0, 2.0 ** 23, ALU.add, ALU.mult))
                V.link(nc.vector.tensor_copy(x.bitcast(I32), t))
                V.link(TT(out, out, x, ALU.mult))

            dve.wait_ge(S["c_in"], 16)
            dve.wait_ge(S["pos_in"], 16)
            V.link(nc.vector.tensor_copy(rp[:, 0:1024], rp[:, 1024:2048].bitcast(I32)))
            V.link(TS(rp[:, 0:1024], rp[:, 0:1024], misc(M_INV), None, ALU.mult))
            reduce_angle(V.link, rp[:, 0:1024], rp[:, 1024:2048]).then_inc(S["rope_ang"], 1)
            nc.vector.memset(sd[:, 63:64], 0.0).then_inc(S["x_rows"], 1)
            V.base = V.n

            are, aim, ldt = (s_in[:, G5 * i:G5 * i + G5] for i in range(3))
            dt, la, th, kk, pp, dn, fr, fi, s8 = (s_s[:, G5 * i:G5 * i + G5] for i in range(9))
            sx, sy, su, sv = (s_co[:, a:b] for a, b in ((SX, SY), (SY, SU_), (SU_, SV), (SV, SA)))

            def powers(l):
                dve.wait_ge(S["s_par"], 16 * l + 16)
                exp_(ldt, dt, kk)
                V.link(TT(la, are, dt, ALU.mult))
                V.link(TT(th, aim, dt, ALU.mult))
                V.link(reduce_angle(V.link, th, kk))
                for t in range(BS + 1):
                    V.inc(TS(s_mag[:, G5 * t:G5 * t + G5], la, float(t), None, ALU.mult))
                    V.inc(TS(s_ang[:, G5 * t:G5 * t + G5], th, float(t), None, ALU.mult))
                V.join()
                exp_(s_mag, s_cos, s_sin)
                V.link(nc.vector.tensor_copy(s_mag, s_cos))
                V.link(reduce_angle(V.link, s_ang, s_sin))
                V.link(TS(s_co[:, SA:SA + G5], s_ang[:, G5 * BS:G5 * BS + G5], 1.0 / TWO_PI, None, ALU.mult))
                nc.vector.tensor_copy(s_co[:, SR:SR + G5], s_mag[:, G5 * BS:G5 * BS + G5]).then_inc(S["s_pow"], 1)

            def coefficients(l):
                dve.wait_ge(S["s_sc"], l + 1)
                V.link(TT(s_cos, s_mag, s_cos, ALU.mult))
                V.link(TT(s_sin, s_mag, s_sin, ALU.mult))
                V.link(TS(pp, s_cos[:, G5:2 * G5], -1.0, None, ALU.add))
                ai = s_sin[:, G5:2 * G5]
                V.link(TT(dn, are, are, ALU.mult))
                V.link(TT(s8, aim, aim, ALU.mult))
                V.link(TT(dn, dn, s8, ALU.add))
                V.link(nc.vector.reciprocal(dn, dn))
                V.link(TT(fr, pp, are, ALU.mult))
                V.link(TT(s8, ai, aim, ALU.mult))
                V.link(TT(fr, fr, s8, ALU.add))
                V.link(TT(fr, fr, dn, ALU.mult))
                V.link(TT(fi, ai, are, ALU.mult))
                V.link(TT(s8, pp, aim, ALU.mult))
                V.link(TT(fi, fi, s8, ALU.subtract))
                V.link(TT(fi, fi, dn, ALU.mult))

                def v3(x):
                    return x.rearrange("p (t g) -> p t g", g=G5)[:, 0:BS, :]

                frb, fib = bcast(fr, BS, 0), bcast(fi, BS, 0)
                V.inc(TT(v3(sx), v3(s_cos), frb, ALU.mult))
                V.inc(TT(v3(su), v3(s_sin), fib, ALU.mult))
                V.inc(TT(v3(sy), v3(s_cos), fib, ALU.mult))
                V.link(TT(v3(sv), v3(s_sin), frb, ALU.mult))
                V.inc(TT(v3(sx), v3(sx), v3(su), ALU.subtract))
                V.link(TT(v3(sy), v3(sy), v3(sv), ALU.add))
                V.inc(TS(sy, sy, misc(M_NSGN), None, ALU.mult))
                V.link(TS(su, s_cos, misc(M_SGN), None, ALU.mult))
                TS(sv, s_sin, -1.0, None, ALU.mult).then_inc(S["s_made"], 1)

            def begin_tables(l, q):
                n = NPB * l + q
                tab = p_tab[q % 2].rearrange("p (g n) -> p g n", g=GP)
                m = 16 * ((NPB // 2) * l + q // 2)
                h0 = p_h0[q % 2]

                if q == 0:
                    dve.wait_ge(S["co_in"], 32 * l + 32)
                else:
                    dve.wait_ge(S["p_ang"], n)
                dve.wait_ge(bc_in[q % 2], m + 16)
                if q >= 2:
                    dve.wait_ge(tab_out[q % 2], m)
                ph = tab[:, :, TSIN:TSIN + NBT]
                k = p_k.rearrange("p (g j) -> p g j", g=GP)
                V.link(TT(ph, bcast(p_jr[:, 0:NBT], GP, 0), bcast(p_co[:, SA + GP * q:SA + GP * q + GP], NBT, 2), ALU.mult))
                V.link(TS(k, ph, MAGIC, None, ALU.add))
                STT(ph, k, MAGIC, ph, ALU.subtract, ALU.subtract).then_inc(S["p_ang"], 1)
                if q >= 2:
                    dve.wait_ge(S["p_k"], n - 1)
                    dve.wait_ge(S["p_hc"], n - 1)
                V.inc(TT(view(h0, 9), part(SU_, 9, q), chan(q, 2, 9), ALU.mult))
                V.link(TT(view(p_t2, 9), part(SV, 9, q), chan(q, 3, 9), ALU.mult))
                TT(view(h0, 9), view(h0, 9), view(p_t2, 9), ALU.add).then_inc(S["p_h0"], 1)
                dve.wait_ge(S["p_h0"], n + 1)
                h2 = tab[:, :, TH2:TH2 + 128].rearrange("p g (t c) -> p g t c", c=C5)
                V.inc(TT(h2, part(SV + G5, BS, q), chan(q, 2, BS), ALU.mult))
                V.link(TT(view(p_t2, BS), part(SU_ + G5, BS, q), chan(q, 3, BS), ALU.mult))
                V.inc(TT(h2, h2, view(p_t2, BS), ALU.subtract))
                V.link(nc.vector.tensor_copy(tab[:, :, TR:TTOP], bcast(p_co[:, SR + GP * q:SR + GP * q + GP], TTOP - TR, 2)))

            def end_tables(l, q):
                n = NPB * l + q
                dve.wait_ge(S["p_k"], n + 1)
                if q:
                    dve.wait_ge(S["ks_out"], 16 * n)
                V.link(nc.vector.tensor_copy(p_ks, bank[3 - 2 * (q % 2)][0:16, :]))
                ks = p_ks.rearrange("c (g n) -> c g n", g=GP)[:, :, 0:C5]
                TT(ks, ks, p_bc[q % 2][0:16, 256:320].rearrange("c (g o) -> c g o", o=C5), ALU.add).then_inc(S["p_ke"], 1)

            def head_norm(l, h_, n):
                for i in range(32):
                    nc.vector.bn_stats(stats[:, 6 * i:6 * i + 6], h_[:, 128 * i:128 * i + 128]).then_inc(S["v_step"], 1)
                    V.n += 1
                V.join()
                nc.vector.memset(sd[0:1, 40:41], 0.0)
                for i in range(32):
                    last = nc.vector.bn_aggr(mv[:, 2 * i:2 * i + 2], stats[:, 6 * i:6 * i + 6])
                last.then_inc(S["hn_var"], 1)
                dve.wait_ge(S["hn_sd"], 2 * l + n + 1)
                V.link(nc.vector.reciprocal(sd[:, 0:32], sd[:, 0:32]))
                for i in range(32):
                    V.inc(TS(h_[:, 128 * i:128 * i + 128], h_[:, 128 * i:128 * i + 128], mv[:, 2 * i:2 * i + 1], sd[:, i:i + 1],
                             ALU.subtract, ALU.mult))
                V.join()

            with dve.Fori(0, DEPTH) as l:
                V.begin(l)
                dve.wait_ge(S["mem_hi"], l + 1)
                TT(meml, memraw, memh.bitcast(F32), ALU.subtract).then_inc(S["mem_lo"], 1)
                for i in range(16):
                    half, k = i // 8, i % 8
                    x0 = T * k + 512 * half
                    dve.wait_ge(S["xT_hi"], 16 * l + i + 1)
                    TT(xl[:, x0:x0 + 512], bank[i % 4], xh[:, x0:x0 + 512].bitcast(F32), ALU.subtract).then_inc(S["xT_lo"], 1)
                powers(l)
                dve.wait_ge(g_free[0], NUNIT * l + U_QK + 2)
                dve.wait_ge(g_free[1], NUNIT * l + U_QK + 2)
                dve.wait_ge(S["rope_in"], 16 * l + 16)
                a, b_ = (qk[:, 2048 * i:2048 * i + 2048].rearrange("p (k t) -> p k t", k=2) for i in range(2))
                ra, rb = (rot[:, 2048 * i:2048 * i + 2048].rearrange("p (k t) -> p k t", k=2) for i in range(2))
                co, si = bcast(rope[:, 0:T], 2, 0), bcast(rope[:, T:2 * T], 2, 0)
                V.inc(TT(ra, a, co, ALU.mult))
                V.link(TT(rb, b_, si, ALU.mult))
                TT(ra, ra, rb, ALU.subtract).then_inc(S["rope_done"], 1)
                V.inc(TT(a, a, si, ALU.mult))
                V.link(TT(b_, b_, co, ALU.mult))
                dve.wait_ge(S["rope_done"], 2 * l + 1)
                TT(rb, a, b_, ALU.add).then_inc(S["rope_done"], 1)

                coefficients(l)
                dve.wait_ge(S["co_out"], 16 * l + 16)
                dve.wait_ge(g_done[1], NUNIT * l + U_QK + 1)
                V.link(nc.vector.memset(sret, 0.0))
                dve.wait_ge(S["qk2_in"], 128 * l + 128)
                def r_begin(c):
                    dve.wait_ge(S["r_sc"], NC * l + c + 1)
                    if c >= 2:
                        dve.wait_ge(S["r_o"], NC * l + c - 1)
                        dve.wait_ge(S["r_u"], NC * l + c - 1)
                    TT(att[c % 2].rearrange("p (b n) -> p b n", b=2), mm[0].rearrange("p (b n) -> p b n", b=2)[:, :, 0:256],
                       cst[:, K_MASK:K_MASK + 512].rearrange("p (b n) -> p b n", b=2), ALU.mult).then_inc(S["r_att"], 1)
                    TT(kn[c % 2], bank[1][:, 256:512], cst[:, K_KDEC:K_KDEC + 256], ALU.mult).then_inc(S["r_kn"], 1)

                r_begin(0)
                for c in range(NC):
                    if c + 1 < NC:
                        r_begin(c + 1)
                    dve.wait_ge(S["r_o"], NC * l + c + 1)
                    hv = hr[:, GW * c:GW * c + GW].rearrange("p (h e) -> p h e", h=HEADS)
                    TT(hv, bank[2].rearrange("p (h e) -> p h e", h=HEADS), bcast(misc(M_QD, 4), 128, 2), ALU.mult).then_inc(S["r_ho"], 1)
                    dve.wait_ge(S["r_u"], NC * l + c + 1)
                    if c:
                        dve.wait_ge(S["r_state"], NC * l + c)
                    for h in range(HEADS):
                        p, r0 = h // 2, 64 * (h % 2)
                        new, up = sret[r0:r0 + 64, 128 * h:128 * h + 128], bank[3][r0:r0 + 64, 128 * p:128 * p + 128]
                        if c:
                            last = STT(new, new, cst[r0:r0 + 64, K_MISC + M_CD + p:K_MISC + M_CD + p + 1], up, ALU.mult, ALU.add)
                        else:
                            last = nc.vector.tensor_copy(new, up)
                    last.then_inc(S["r_state"], 1)
                dve.wait_ge(S["r_ho"], NC * l + NC)
                head_norm(l, hr, 0)
                for i in range(4):
                    u, g = i // 2, i % 2
                    dve.wait_ge(g_free[g], NUNIT * l + U_RZ + u + 1)
                    hv = tview(hr, GW, g, u)
                    TT(hv, hv, gate[g].rearrange("p (c n) -> p c n", c=4), ALU.mult).then_inc(gate_used[g], 1)


                def x_max(i):
                    s0 = 16 * (i % 2)
                    dve.wait_ge(S["x_s"], 8 * l + i + 1)
                    V.link(nc.vector.tensor_reduce(small[:, s0:s0 + 4], gp[i % 2].rearrange("p (c m) -> p c m", c=4), AX.X, ALU.max))
                    TS(small[:, s0 + 4:s0 + 8], small[:, s0:s0 + 4], -(128 ** -0.5), None, ALU.mult).then_inc(S["x_max"], 1)

                for g in range(2):
                    dve.wait_ge(gate_used[g], NGATE * l + 2)
                x_max(0)
                x_max(1)
                for i in range(8):
                    s0 = 16 * (i % 2)
                    dve.wait_ge(S["x_e"], 4 * (8 * l + i + 1))
                    V.link(nc.vector.reciprocal(small[:, s0 + 12:s0 + 16], small[:, s0 + 8:s0 + 12]))
                    pv = pm[i % 2].rearrange("p (c m) -> p c m", c=4)
                    TT(pv, pv, bcast(small[:, s0 + 12:s0 + 16], NMEM, 2), ALU.mult).then_inc(S["x_norm"], 1)
                    if 1 <= i < 7:
                        x_max(i + 1)
                for i in range(4):
                    u, g = i // 2, i % 2
                    if i == 0:
                        dve.wait_ge(S["wif_hi"], l + 1)
                        TT(wifl, wifr, wifh.bitcast(F32), ALU.subtract).then_inc(S["wif_lo"], 1)
                    dve.wait_ge(g_free[g], NUNIT * l + U_AZ + u + 1)
                    dve.wait_ge(S["x_pvev"], 8 * l + 8)
                    TT(xo[:, T * i:T * i + T], xo[:, T * i:T * i + T], gate[g], ALU.mult).then_inc(gate_used[g], 1)

                dve.wait_ge(S["if_act"], 2 * l + 2)
                dve.wait_ge(S["res_in"], 16 * l + 16)
                V.link(STT(rowf[0:4, :], rowb[0:4, :], 0.0, rowm[0:4, :], ALU.min, ALU.subtract))
                V.inc(nc.vector.tensor_tensor_scan(rowb[0:4, :], rres[0:4, :], rowf[0:4, :], 0.0, ALU.mult, ALU.add))
                V.link(nc.vector.tensor_tensor_scan(rowm[0:4, :], rowf[0:4, :], rowi[0:4, :], 0.0, ALU.add, ALU.max))
                V.link(nc.vector.memset(rk, 0.0))
                V.inc(TT(rk[0:4, :], rowi[0:4, :], rowb[0:4, :], ALU.subtract))
                V.inc(TS(rk[96:100, :], rowm[0:4, :], -1.0, None, ALU.mult))
                V.inc(nc.vector.memset(small[0:4, 0:1], 0.0))
                V.inc(nc.vector.tensor_copy(small[0:4, 1:8], rowm[0:4, :].rearrange("p (c t) -> p c t", t=CH)[:, 0:7, CH - 1]))
                V.link(TT(rowf[0:4, :], rowb[0:4, :], rowm[0:4, :], ALU.subtract))
                V.link(nc.vector.tensor_copy(small[0:4, 8:16], rowf[0:4, :].rearrange("p (c t) -> p c t", t=CH)[:, :, CH - 1]))
                V.inc(TT(small[0:4, 16:24], small[0:4, 8:16], small[0:4, 0:8], ALU.add))

                def rows(x):
                    return x.rearrange("p (c t) -> p c t", t=CH)

                V.inc(TT(rows(rk[32:36, :]), rows(rowf[0:4, :]), bcast(small[0:4, 0:8], CH, 2), ALU.add))
                TT(rows(rk[64:68, :]), rows(rk[0:4, :]), bcast(small[0:4, 8:16], CH, 2), ALU.add).then_inc(S["rows_done"], 1)
                mxv = mx.rearrange("p (h t) -> p h t", h=HEADS)
                V.link(nc.vector.memset(mxv[:, :, 0:3], 0.0))
                dve.wait_ge(S["cw_in"], 16 * l + 16)
                for h in range(HEADS):
                    dve.wait_ge(g_free[h % 2], NUNIT * l + U_MX + h // 2 + 1)
                    if h == 3:
                        for i in (2, 3):
                            dve.wait_ge(ys_out[i], 64 * l + 32)
                    y = xc[:, T * h:T * h + T]
                    for k in (3, 2, 1):
                        w = small[:, 32 + 4 * h + k:33 + 4 * h + k]
                        x_ = mxv[:, h, k:k + T]
                        V.link(TS(y, x_, w, None, ALU.mult) if k == 3 else STT(y, x_, w, y, ALU.mult, ALU.add))
                    STT(y, mxv[:, h, 0:T], small[:, 32 + 4 * h:33 + 4 * h], y, ALU.mult, ALU.add).then_inc(S["conv_done"], 1)
                dve.wait_ge(S["conv_done"], 4 * l + 4)
                nc.vector.memset(va.rearrange("p (g e) -> p g e", e=129)[:, :, 128:129], 1.0).then_inc(S["ones_done"], 1)
                dve.wait_ge(S["cols_done"], 5 * l + 5)
                for i in range(8):
                    h, half = i // 2, i % 2
                    dve.wait_ge(S["a_bc"], 8 * l + i + 1)
                    for c in range(4 * half, 4 * half + 4):
                        last = TS(wt[:, 512 * c + 128 * h:512 * c + 128 * h + 128], bank[i % 2][:, 128 * (c % 4):128 * (c % 4) + 128],
                                  cols[:, 4 * c + h:4 * c + h + 1], 0.0, ALU.add, ALU.min)
                    last.then_inc(S["w_arg"], 1)
                for c in range(NC):
                    dve.wait_ge(S["s_mm"], NC * l + c + 1)
                    dve.wait_ge(S["w_mask"], NC * l + c + 1)
                    w = wt[:, 512 * c:512 * c + 512]
                    TT(w, w, bank[c % 2], ALU.mult).then_inc(S["s_w"], 1)
                wi, wk, em = (cols[:, 32 * k:32 * k + 32] for k in (1, 2, 3))

                def k_weights(c):
                    dve.wait_ge(S["k_tr"], NC * l + c + 1)
                    if c >= 2:
                        dve.wait_ge(S["m_c"], NC * l + c - 1)
                    TT(kw[c % 2].rearrange("p (h d) -> p h d", h=HEADS), bank[3].rearrange("p (h d) -> p h d", h=HEADS),
                       bcast(wk[:, 4 * c:4 * c + 4], 128, 2), ALU.mult).then_inc(S["k_w"], 1)

                def heads2(x):
                    return x.rearrange("p (a x) -> p a x", a=2)[:, :, 0:258].rearrange("p a (b e) -> p a b e", b=2)

                num = inter.rearrange("p (a b e) -> p a b e", a=2, b=2)
                k_weights(0)
                for c in range(NC):
                    if c + 1 < NC:
                        k_weights(c + 1)
                    dve.wait_ge(S["m_num"], NC * l + c + 1)
                    if c:
                        V.join()
                    if c == 0:
                        nc.vector.tensor_copy(num, heads2(gp[0])).then_inc(S["m_read"], 1)
                    else:
                        V.link(TT(num, heads2(gp[1]), bcast(wi[:, 4 * c:4 * c + 4].rearrange("p (a b) -> p a b", a=2), 129, 3), ALU.mult))
                        TT(num, num, heads2(gp[0]), ALU.add).then_inc(S["m_read"], 1)
                    dve.wait_ge(S["m_read"], NC * l + c + 1)
                    dve.wait_ge(S["m_c"], NC * l + c + 1)
                    if c == 0:
                        nc.vector.tensor_copy(cst8.rearrange("p (a b e) -> p a b e", a=2, b=2), heads2(mm[0])).then_inc(S["m_st"], 1)
                    else:
                        dve.wait_ge(S["m_st"], NC * l + c)
                        for h in range(HEADS):
                            o0 = 512 * (h // 2) + 129 * (h % 2)
                            last = STT(cst8[:, 129 * h:129 * h + 129], cst8[:, 129 * h:129 * h + 129], dec[:, NC * h + c:NC * h + c + 1],
                                       mm[0][:, o0:o0 + 129], ALU.mult, ALU.add)
                        last.then_inc(S["m_st"], 1)
                    dn4 = small[:, 52:56]
                    den = inter.rearrange("p (h e) -> p h e", h=HEADS)[:, :, 128]
                    V.link(STT(dn4, den, -1.0, den, ALU.mult, ALU.max))
                    V.link(TT(dn4, dn4, em[:, 4 * c:4 * c + 4], ALU.max))
                    V.link(nc.vector.reciprocal(dn4, dn4))
                    V.link(TS(dn4, dn4, 0.5, None, ALU.mult))
                    V.inc(TT(hm[:, GW * c:GW * c + GW].rearrange("p (h e) -> p h e", h=HEADS),
                             inter.rearrange("p (h e) -> p h e", h=HEADS)[:, :, 0:128], bcast(dn4, 128, 2), ALU.mult))
                V.join()
                for i in range(4):
                    u, g = i // 2, i % 2
                    dve.wait_ge(g_free[g], NUNIT * l + U_LO + u + 1)
                    hv = tview(hm, GW, g, u)
                    STT(hv, gate[g].rearrange("p (c n) -> p c n", c=4), 1.0, hv, ALU.add, ALU.mult).then_inc(gate_used[g], 1)
                    if i == 1:
                        begin_tables(l, 0)
                end_tables(l, 0)
                for g in range(2):
                    dve.wait_ge(gate_used[g], NGATE * l + 6)
                head_norm(l, hm, 1)
                dve.wait_ge(S["gn_in"], 16 * l + 16)
                for i in range(4):
                    u, g = i // 2, i % 2
                    dve.wait_ge(g_free[g], NUNIT * l + U_LZ + u + 1)
                    hv = tview(hm, GW, g, u)
                    V.link(TT(hv, hv, gate[g].rearrange("p (c n) -> p c n", c=4), ALU.mult))
                    TT(hv, hv, bcast(gn[:, 256 * u:256 * u + 256], 4, 0), ALU.mult).then_inc(gate_used[g], 1)
                    if i == 1:
                        begin_tables(l, 1)
                for u in range(U_LZ + 1, U_SZ + 1):
                    for q in TABLES_AT.get(u - 1, ()):
                        end_tables(l, q)
                    for q in TABLES_AT.get(u, ()):
                        begin_tables(l, q)

                for i in range(4):
                    dve.wait_ge(ys_out[i], 64 * l + 64)
                zv = zin.rearrange("p (g j) -> p g j", g=GB)
                V.link(nc.vector.memset(zv[:, :, 0:1], 0.0))
                for b in range(NBATCH):
                    t = tb[b % SLOTS].rearrange("p (g n) -> p g n", g=GB)
                    ct, st = (t[:, :, o:o + NBT] for o in (TCOS, TSIN))
                    dve.wait_ge(tb_in[b % SLOTS], 48 * ((NBATCH // SLOTS) * l + b // SLOTS) + 48)
                    dve.wait_ge(S["s_g"], NBATCH * l + b + 1)
                    z1, z2 = (z.rearrange("p (g j) -> p g j", g=GB)[:, :, 1:NBT] for z in (zt1, zt2))
                    (TT(z1, ct[:, :, 1:NBT], bank[0][:, 0:256].rearrange("p (g j) -> p g j", g=GB), ALU.mult))
                    TT(z2, st[:, :, 1:NBT], bank[1][:, 0:256].rearrange("p (g j) -> p g j", g=GB), ALU.mult).then_inc(S["s_gr"], 1)
                    dve.wait_ge(S["s_gr"], NBATCH * l + b + 1)
                    V.link(TT(zv[:, :, 1:NBT], z1, z2, ALU.add))
                    for g in range(GB):
                        V.inc(nc.vector.tensor_tensor_scan(zz[:, NBT * g:NBT * g + NBT], bcast(t[:, g, TR:TR + 1], NBT, 1)[:, :, 0],
                                                           zin[:, NBT * g:NBT * g + NBT], 0.0, ALU.mult, ALU.add))
                    V.join()
                    if b >= 2:
                        dve.wait_ge(S["s_y"], NBATCH * l + b - 1)
                    zf = zz.rearrange("p (g j) -> p g j", g=GB)[:, :, 0:NB]
                    TT(zc[b % 2].rearrange("p (g j) -> p g j", g=GB), zf, ct[:, :, 0:NB], ALU.mult)
                    TT(zs[b % 2].rearrange("p (g j) -> p g j", g=GB), zf, st[:, :, 0:NB], ALU.mult).then_inc(S["s_z"], 1)
                def ylo(n):
                    y0 = 1024 * (2 * KQ[n % 8 // 2] + n % 2)
                    dve.wait_ge(S["oy_hi"], 16 * l + n + 1)
                    TT(oyl[:, y0:y0 + 1024], yraw[n % 2], oyh[:, y0:y0 + 1024].bitcast(F32), ALU.subtract).then_inc(S["oy_lo"], 1)

                for m in range(4):
                    dve.wait_ge(S[f"yd_out{m}"], 128 * l + 128)
                for m in range(4):
                    dve.wait_ge(S["gy_hi"], 4 * l + m + 1)
                    TT(yl[:, T * m:T * m + T], yc[m], yh[:, T * m:T * m + T].bitcast(F32), ALU.subtract).then_inc(S["gy_lo"], 1)
                for m in range(4):
                    if m % 2 == 0:
                        ylo(m)
                        ylo(m + 1)
                    u, g = m // 2, m % 2
                    dve.wait_ge(g_free[g], NUNIT * l + U_GL + u + 1)
                    V.link(STT(gate[g], gate[g], 1.0, yc[m], ALU.add, ALU.mult))
                    if m >= 2:
                        dve.wait_ge(s5_out[g], 32 * l + 16)
                    (STT(s5o[g].rearrange("p (j s) -> p s j", s=BS), gate[g].rearrange("p (s j) -> p s j", s=BS), 0.5,
                               sz[:, T * m:T * m + T].rearrange("p (s j) -> p s j", s=BS), ALU.mult, ALU.mult)).then_inc(gate_used[g], 1)

                for n in range(4, 8):
                    ylo(n)

                def norm(c):
                    if c:
                        dve.wait_ge(S["x_rows"], NC * l + c + 1)
                    dve.wait_ge(S["o_done"], 6 * l + 3 * (c // 4) + min(c % 4 + 1, 3))
                    if c % 4 == 3:
                        dve.wait_ge(S["o_used"], NOUT * l + 8 * (c // 4) + 8)
                    STT(xr[c], xr[c], ALPHA, (gp + mm)[c % 4], ALU.mult, ALU.add).then_inc(S["o_free"], 1)
                    dve.wait_ge(S["o_free"], NC * l + c + 1)
                    for i in range(2):
                        V.inc(nc.vector.bn_stats(stats[:, 6 * i:6 * i + 6], xr[c][:, 512 * i:512 * i + 512]))
                    V.join()
                    nc.vector.memset(sd[0:1, 62:63], 0.0)
                    nc.vector.bn_aggr(mv[:, 32:34], stats[:, 0:12]).then_inc(S["ln_var"], 1)
                    dve.wait_ge(S["ln_var"], NC * l + c + 1)
                    dve.wait_ge(S["ln_sd"], NC * l + c + 1)
                    V.link(nc.vector.reciprocal(sd[:, 32:33], sd[:, 32:33]))
                    V.link(STT(xr[c], xr[c], mv[:, 32:33], lng, ALU.subtract, ALU.mult))
                    STT(xr[c], xr[c], sd[:, 32:33], lnb, ALU.mult, ALU.add).then_inc(S["x_rows"], 1)

                dve.wait_ge(S["ln_in"], 32 * l + 32)
                dve.wait_ge(S["xr_in"], 128 * l + 128)
                for hf in range(2):
                    for n in range(8, 14) if hf == 0 else range(14, 16):
                        ylo(n)
                    for c in range(4 * hf, 4 * hf + 4):
                        norm(c)
            assert V.n == steps_v, V.n


_OUT = (DEPTH + 1, T, D)


def kernel(x, mem, positions, w_in, s5_a_re, s5_a_im, s5_log_dt, s5_b_re, s5_b_im, s5_c_re, s5_c_im, s5_d, s5_w_glu,
           ml_conv_w, ml_wq, ml_wk, ml_b_ig, ml_b_fg, ml_gn, xa_w_kv, w_out, ln_g, ln_b):
    import concourse.bacc as bacc
    from concourse.bass_utils import run_bass_kernel_spmd

    A = np.ascontiguousarray
    x, mem, w_in = np.asarray(x), np.asarray(mem), np.asarray(w_in)
    widths = [256, 256] + [GW] * 8 + [HEADS, HEADS, GW, GW]
    edge = np.cumsum([0] + widths)
    rq, rk_, rv, rz, su, sz, mx, lv, lo, lz, mi, mf, aq, az = (w_in[:, :, a:b] for a, b in zip(edge[:-1], edge[1:]))

    def rope_halves(w):
        w = w.reshape(DEPTH, D, HEADS, 2, 32)
        return [w[:, :, :, i, :].reshape(DEPTH, D, 128) for i in range(2)]

    q0, q1 = rope_halves(rq)
    k0, k1 = rope_halves(rk_)
    kv = np.asarray(xa_w_kv)
    order = [kv[:, :, :GW], kv[:, :, GW:], np.concatenate([q0, k0, q1, k1], -1), rv, aq, rz, az, mx, lv, lo, lz, su, sz]

    def units(w, k, n):
        N = w.shape[-1]
        return w.reshape(DEPTH, k, 128, N // n, n).transpose(0, 3, 2, 1, 4).reshape(DEPTH, N // n, 128, k * n)

    parts = [units(w, KT, 256) for w in order]
    glu = units(np.asarray(s5_w_glu), 4, 256)
    parts.append(np.concatenate([glu, np.zeros_like(glu)], -1))
    wo = np.asarray(w_out).reshape(DEPTH, 4, GW, D)
    wo = [units(wo[:, q], 4, 512) for q in range(4)]
    parts += wo
    w = np.concatenate(parts, 1).reshape(DEPTH * NSTORED, 128, 2048)
    w = np.concatenate([w, w[-1:]])
    wif = np.zeros((DEPTH, D, 128), np.float32)
    wif[:, :, 0:HEADS], wif[:, :, 32:32 + HEADS] = mi, mf
    wif = wif.reshape(DEPTH, KT, 128, 128).transpose(0, 2, 1, 3).reshape(DEPTH, 128, KT * 128)
    wqk = np.stack([np.asarray(ml_wq), np.asarray(ml_wk)], 1).transpose(0, 3, 1, 2, 4).reshape(DEPTH, 128, 1024)

    def states(a):
        return np.swapaxes(np.asarray(a), 1, 2)

    def chunks(a, b):
        a = np.concatenate([a, b], 1).reshape(DEPTH, 128, NPB, GP * C5)
        return a.transpose(0, 2, 1, 3).reshape(DEPTH * NPB, 128, GP * C5)

    ldt = np.broadcast_to(np.asarray(s5_log_dt)[:, None, :], (DEPTH, 128, G5))
    s5a = np.concatenate([np.concatenate([states(s5_a_re)] * 2, 1), np.concatenate([states(s5_a_im)] * 2, 1), ldt], 2)
    s5a = np.concatenate([s5a, s5a[-1:]])
    br, bi = states(s5_b_re), states(s5_b_im)
    cr, ci = (states(np.swapaxes(np.asarray(c), 2, 3)) for c in (s5_c_re, s5_c_im))
    diag = np.zeros((DEPTH * NPB, 128, GP, C5), np.float32)
    diag[:, np.arange(C5), :, np.arange(C5)] = np.asarray(s5_d).reshape(DEPTH * NPB, GP, C5).transpose(2, 0, 1)
    s5bc = np.concatenate([chunks(br, bi), chunks(bi, br), chunks(cr, ci), chunks(ci, cr),
                           diag.reshape(DEPTH * NPB, 128, GP * C5)], 2)
    conv = np.asarray(ml_conv_w).reshape(DEPTH, 4, HEADS, 128).transpose(0, 3, 2, 1).reshape(DEPTH, 128, 16)
    bif = np.stack([np.asarray(ml_b_ig), np.asarray(ml_b_fg)], -1)
    cst, jc = constants()
    arrays = dict(x=x[0], memT=mem[0].T, pos=np.asarray(positions)[0].astype(np.int32), w=w, wif=wif, wqk=wqk,
                  s5a=s5a, s5bc=s5bc, convw=conv, bif=bif, gn=np.asarray(ml_gn).reshape(-1),
                  lng=np.asarray(ln_g).reshape(-1), lnb=np.asarray(ln_b).reshape(-1), cst=cst, jcst=jc)
    arrays = {k: A(v) for k, v in arrays.items()}
    nc = bacc.Bacc("TRN2", target_bir_lowering=False, num_devices=1)
    dram = {k: nc.dram_tensor("in_" + k, v.shape, mybir.dt.from_np(v.dtype), kind="ExternalInput").ap() for k, v in arrays.items()}
    for name, shape in (("yt", (16, 128, T)), ("ud", (GW, T)), ("yd", (GW, T)), ("ropetab", (128, 2 * T)),
                        ("tabs", (G5, 128, TTOP)), ("kd", (G5, C5, 240)), ("s5co", (128, SCOLS))):
        dram[name] = nc.dram_tensor(name, shape, F32, kind="Internal").ap()
    dram["xs"] = nc.dram_tensor("xs", _OUT, F32, kind="ExternalOutput").ap()
    build(nc, dram)
    r = run_bass_kernel_spmd(nc, [{"in_" + k: v for k, v in arrays.items()}], core_ids=[0])
    return np.asarray(r.results[0]["xs"])[DEPTH:DEPTH + 1]
```
